# Optimizing a Trainium2 kernel written in Bass

```python
import math
import jax, jax.numpy as jnp
from jax import lax
import numpy as np

D_MODEL = 1024
BATCH = 1
SEQ = 512
DEPTH = 1
DEC_BATCH = 8
DEC_SEQ = 4
PAST_LEN = 4096
PAGE_SIZE = 128

N_META = 16
D_CONF = D_MODEL
CONF_K = 31
D_INNER = 2 * D_MODEL
SSM_HEAD_DIM = 64
SSM_HEADS = D_INNER // SSM_HEAD_DIM
SSM_GROUPS = 8
SSM_STATE = 128
SSM_K = 4
CONV_DIM = D_INNER + 2 * SSM_GROUPS * SSM_STATE
SSD_CHUNK = 128
SSM_NORM_GROUPS = SSM_GROUPS
N_GATES = 2
N_IN = 2 * D_CONF + D_INNER + CONV_DIM + SSM_HEADS + N_GATES * D_MODEL
N_EXPERT_GROUPS = 4
EXPERTS_PER_GROUP = 8
N_EXPERTS = N_EXPERT_GROUPS * EXPERTS_PER_GROUP
TOP_K_INNER = 2
D_EXPERT = D_MODEL // 4
EPS = 1e-6

kernel_name = "hybrid_conformer_ssd_hmoe_step"

def rms_norm(x, w):
    xf = x.astype(jnp.float32)
    y = xf * lax.rsqrt(jnp.mean(xf * xf, axis=-1, keepdims=True) + EPS)
    return (y * w.astype(jnp.float32)).astype(x.dtype)

def layer_norm(x, g, b):
    xf = x.astype(jnp.float32)
    mu = jnp.mean(xf, axis=-1, keepdims=True)
    var = jnp.mean(jnp.square(xf - mu), axis=-1, keepdims=True)
    y = (xf - mu) * lax.rsqrt(var + EPS)
    return (y * g.astype(jnp.float32) + b.astype(jnp.float32)).astype(x.dtype)

def causal_dwconv(x_full, w, b):
    c = x_full.shape[-1]
    y = lax.conv_general_dilated(x_full, w[:, None, :].astype(x_full.dtype), window_strides=(1,),
                                 padding='VALID', dimension_numbers=('NWC', 'WIO', 'NWC'),
                                 feature_group_count=c)
    return y + b.astype(y.dtype)

def ssd_chunk(h, x, dt, A, bm, cm):
    t = x.shape[1]
    cum = jnp.cumsum(dt * A, axis=1)
    seg = cum[:, :, None] - cum[:, None, :]
    causal = jnp.tril(jnp.ones((t, t), dtype=bool))[None, :, :, None, None]
    decay = jnp.exp(jnp.where(causal, seg, -jnp.inf))
    cb = jnp.einsum('btgn,bsgn->btsg', cm, bm)
    w = cb[..., None] * decay * dt[:, None]
    y = jnp.einsum('btsgh,bsghp->btghp', w, x)
    y = y + jnp.einsum('btgn,bghpn->btghp', cm, h) * jnp.exp(cum)[..., None]
    tail = jnp.exp(cum[:, -1:] - cum) * dt
    h_new = jnp.exp(cum[:, -1])[..., None, None] * h + jnp.einsum('bsgh,bsgn,bsghp->bghpn', tail, bm, x)
    return h_new, y

def ssd(x, dt, A, bm, cm, h0, lead):
    bsz, length = x.shape[0], x.shape[1]
    h, y_lead = ssd_chunk(h0, x[:, :lead], dt[:, :lead], A, bm[:, :lead], cm[:, :lead])
    rest = length - lead
    if rest == 0:
        return y_lead, h
    n = rest // SSD_CHUNK

    def to_chunks(a):
        a = a[:, lead:]
        return jnp.moveaxis(a.reshape((bsz, n, SSD_CHUNK) + a.shape[2:]), 1, 0)

    def step(hc, inp):
        xc, dtc, bc, cc = inp
        return ssd_chunk(hc, xc, dtc, A, bc, cc)

    h, ys = lax.scan(step, h, (to_chunks(x), to_chunks(dt), to_chunks(bm), to_chunks(cm)))
    ys = jnp.moveaxis(ys, 0, 1).reshape((bsz, rest) + ys.shape[3:])
    return jnp.concatenate([y_lead, ys], axis=1), h

def token_mixer(xn, conf_buf, ssm_buf, h0, lead, w_in, conf_dw_w, conf_dw_b, conf_ln_g, conf_ln_b,
                conf_out_w, conf_out_b, ssm_conv_w, ssm_conv_b, dt_bias, a_log, d_skip, ssm_norm_w,
                ssm_out_w, gate_b, w_o):
    bsz, length, _ = xn.shape
    f32 = jnp.float32
    hg = SSM_HEADS // SSM_GROUPS
    u = xn @ w_in
    s1 = D_CONF
    s2 = s1 + D_CONF
    s3 = s2 + D_INNER
    s4 = s3 + CONV_DIM
    s5 = s4 + SSM_HEADS
    glu_v, glu_g, z, xbc, dt_raw, gate_logit = jnp.split(u, [s1, s2, s3, s4, s5], axis=-1)
    a = glu_v * jax.nn.sigmoid(glu_g)
    a_full = jnp.concatenate([conf_buf.astype(a.dtype), a], axis=1)
    new_conf_buf = a_full[:, -(CONF_K - 1):]
    a = causal_dwconv(a_full, conf_dw_w, conf_dw_b)
    a = jax.nn.silu(layer_norm(a, conf_ln_g, conf_ln_b))
    y_a = a @ conf_out_w + conf_out_b
    xbc_full = jnp.concatenate([ssm_buf.astype(xbc.dtype), xbc], axis=1)
    new_ssm_buf = xbc_full[:, -(SSM_K - 1):]
    xbc = jax.nn.silu(causal_dwconv(xbc_full, ssm_conv_w, ssm_conv_b))
    xs, bm, cm = jnp.split(xbc, [D_INNER, D_INNER + SSM_GROUPS * SSM_STATE], axis=-1)
    xs_h = xs.astype(f32).reshape(bsz, length, SSM_GROUPS, hg, SSM_HEAD_DIM)
    dt = jax.nn.softplus(dt_raw.astype(f32) + dt_bias.astype(f32)).reshape(bsz, length, SSM_GROUPS, hg)
    A = -jnp.exp(a_log.astype(f32)).reshape(SSM_GROUPS, hg)
    bm = bm.astype(f32).reshape(bsz, length, SSM_GROUPS, SSM_STATE)
    cm = cm.astype(f32).reshape(bsz, length, SSM_GROUPS, SSM_STATE)
    h0g = h0.astype(f32).reshape(bsz, SSM_GROUPS, hg, SSM_HEAD_DIM, SSM_STATE)
    y, h = ssd(xs_h, dt, A, bm, cm, h0g, lead)
    y = y + d_skip.astype(f32).reshape(SSM_GROUPS, hg)[:, :, None] * xs_h
    y = y.reshape(bsz, length, D_INNER) * jax.nn.silu(z.astype(f32))
    yg = y.reshape(bsz, length, SSM_NORM_GROUPS, D_INNER // SSM_NORM_GROUPS)
    yg = yg * lax.rsqrt(jnp.mean(yg * yg, axis=-1, keepdims=True) + EPS)
    y = (yg.reshape(bsz, length, D_INNER) * ssm_norm_w.astype(f32)).astype(xn.dtype)
    y_b = y @ ssm_out_w
    gates = jax.nn.sigmoid(gate_logit + gate_b).reshape(bsz, length, N_GATES, D_MODEL)
    merged = gates[:, :, 0] * y_a + gates[:, :, 1] * y_b
    out = merged @ w_o
    new_h = h.reshape(bsz, SSM_HEADS, SSM_HEAD_DIM, SSM_STATE).astype(h0.dtype)
    return out, new_conf_buf, new_ssm_buf, new_h

def hier_moe(xn, rg_w, rg_b, re_w, re_b, w1, w3, w2):
    shp = xn.shape
    x = xn.reshape(-1, D_MODEL)
    t = x.shape[0]
    f32 = jnp.float32
    g_logit = (x @ rg_w + rg_b).astype(f32)
    g_prob = jax.nn.softmax(g_logit, axis=-1)
    g_sel = jnp.argmax(g_logit, axis=-1)
    e_logit = (x @ re_w + re_b).astype(f32).reshape(t, N_EXPERT_GROUPS, EXPERTS_PER_GROUP)
    e_in = jnp.take_along_axis(e_logit, g_sel[:, None, None], axis=1)[:, 0]
    vals, idx = lax.top_k(e_in, TOP_K_INNER)
    w = jax.nn.softmax(vals, axis=-1) * jnp.take_along_axis(g_prob, g_sel[:, None], axis=1)
    ids = g_sel[:, None] * EXPERTS_PER_GROUP + idx
    combine = jnp.sum(jax.nn.one_hot(ids, N_EXPERTS, dtype=f32) * w[..., None], axis=1)
    combine = combine.astype(x.dtype).reshape(t, N_EXPERT_GROUPS, EXPERTS_PER_GROUP)
    out = jnp.zeros_like(x)
    for gi in range(N_EXPERT_GROUPS):
        sl = slice(gi * EXPERTS_PER_GROUP, (gi + 1) * EXPERTS_PER_GROUP)
        h1 = jnp.einsum('td,edf->tef', x, w1[sl])
        h3 = jnp.einsum('td,edf->tef', x, w3[sl])
        act = jax.nn.silu(h1) * h3 * combine[:, gi, :, None]
        out = out + jnp.einsum('tef,efd->td', act, w2[sl])
    return out.reshape(shp)

def setup_inputs(seed: int = 0) -> dict:
    key = jax.random.key(seed)
    ks = jax.random.split(key, 32)
    nrm = jax.random.normal
    f32 = jnp.float32
    L = DEPTH
    dt0 = jnp.exp(jax.random.uniform(ks[14], (L, SSM_HEADS), minval=math.log(1e-3), maxval=math.log(1e-1)))
    return {
        "x_prompt": nrm(ks[0], (BATCH, SEQ, D_MODEL), f32),
        "x_sample": nrm(ks[1], (DEC_BATCH, DEC_SEQ, D_MODEL), f32),
        "state_conf_conv": 0.5 * nrm(ks[2], (L, DEC_BATCH, CONF_K - 1, D_CONF), f32),
        "state_ssm_conv": 0.5 * nrm(ks[3], (L, DEC_BATCH, SSM_K - 1, CONV_DIM), f32),
        "state_ssm": 0.1 * nrm(ks[4], (L, DEC_BATCH, SSM_HEADS, SSM_HEAD_DIM, SSM_STATE), f32),
        "meta_tokens": nrm(ks[5], (N_META, D_MODEL), f32),
        "norm_mix_w": 1.0 + 0.05 * nrm(ks[6], (L, D_MODEL), f32),
        "w_in": nrm(ks[7], (L, D_MODEL, N_IN), f32) * D_MODEL ** -0.5,
        "conf_dw_w": nrm(ks[8], (L, CONF_K, D_CONF), f32) * CONF_K ** -0.5,
        "conf_dw_b": 0.02 * nrm(ks[9], (L, D_CONF), f32),
        "conf_ln_g": 1.0 + 0.05 * nrm(ks[10], (L, D_CONF), f32),
        "conf_ln_b": 0.02 * nrm(ks[11], (L, D_CONF), f32),
        "conf_out_w": nrm(ks[12], (L, D_CONF, D_MODEL), f32) * D_CONF ** -0.5,
        "conf_out_b": 0.02 * nrm(ks[13], (L, D_MODEL), f32),
        "ssm_conv_w": nrm(ks[15], (L, SSM_K, CONV_DIM), f32) * SSM_K ** -0.5,
        "ssm_conv_b": 0.02 * nrm(ks[16], (L, CONV_DIM), f32),
        "dt_bias": dt0 + jnp.log(-jnp.expm1(-dt0)),
        "a_log": jnp.log(jax.random.uniform(ks[17], (L, SSM_HEADS), minval=1.0, maxval=16.0)),
        "d_skip": 1.0 + 0.05 * nrm(ks[18], (L, SSM_HEADS), f32),
        "ssm_norm_w": 1.0 + 0.05 * nrm(ks[19], (L, D_INNER), f32),
        "ssm_out_w": nrm(ks[20], (L, D_INNER, D_MODEL), f32) * D_INNER ** -0.5,
        "gate_b": 0.02 * nrm(ks[21], (L, N_GATES * D_MODEL), f32),
        "w_o": nrm(ks[22], (L, D_MODEL, D_MODEL), f32) * D_MODEL ** -0.5,
        "norm_ffn_w": 1.0 + 0.05 * nrm(ks[23], (L, D_MODEL), f32),
        "router_group_w": nrm(ks[24], (L, D_MODEL, N_EXPERT_GROUPS), f32) * D_MODEL ** -0.5,
        "router_group_b": 0.01 * nrm(ks[25], (L, N_EXPERT_GROUPS), f32),
        "router_expert_w": nrm(ks[26], (L, D_MODEL, N_EXPERTS), f32) * D_MODEL ** -0.5,
        "router_expert_b": 0.01 * nrm(ks[27], (L, N_EXPERTS), f32),
        "exp_w1": nrm(ks[28], (L, N_EXPERTS, D_MODEL, D_EXPERT), f32) * D_MODEL ** -0.5,
        "exp_w3": nrm(ks[29], (L, N_EXPERTS, D_MODEL, D_EXPERT), f32) * D_MODEL ** -0.5,
        "exp_w2": nrm(ks[30], (L, N_EXPERTS, D_EXPERT, D_MODEL), f32) * D_EXPERT ** -0.5,
        "norm_final_w": 1.0 + 0.05 * nrm(ks[31], (D_MODEL,), f32),
    }

def reference(x_prompt, x_sample, state_conf_conv, state_ssm_conv, state_ssm, meta_tokens, norm_mix_w,
              w_in, conf_dw_w, conf_dw_b, conf_ln_g, conf_ln_b, conf_out_w, conf_out_b, ssm_conv_w,
              ssm_conv_b, dt_bias, a_log, d_skip, ssm_norm_w, ssm_out_w, gate_b, w_o, norm_ffn_w,
              router_group_w, router_group_b, router_expert_w, router_expert_b, exp_w1, exp_w3, exp_w2,
              norm_final_w):
    bp = x_prompt.shape[0]
    dt_ = x_prompt.dtype
    meta = jnp.broadcast_to(meta_tokens[None].astype(dt_), (bp, N_META, D_MODEL))
    xp = jnp.concatenate([meta, x_prompt], axis=1)
    xs = x_sample
    pc, pm, ps, sc, sm, ss = [], [], [], [], [], []
    for l in range(DEPTH):
        wts = (w_in[l], conf_dw_w[l], conf_dw_b[l], conf_ln_g[l], conf_ln_b[l], conf_out_w[l], conf_out_b[l],
               ssm_conv_w[l], ssm_conv_b[l], dt_bias[l], a_log[l], d_skip[l], ssm_norm_w[l], ssm_out_w[l],
               gate_b[l], w_o[l])
        moe_w = (router_group_w[l], router_group_b[l], router_expert_w[l], router_expert_b[l],
                 exp_w1[l], exp_w3[l], exp_w2[l])
        zc = jnp.zeros((bp, CONF_K - 1, D_CONF), dt_)
        zm = jnp.zeros((bp, SSM_K - 1, CONV_DIM), dt_)
        zh = jnp.zeros((bp, SSM_HEADS, SSM_HEAD_DIM, SSM_STATE), dt_)
        o, c1, c2, c3 = token_mixer(rms_norm(xp, norm_mix_w[l]), zc, zm, zh, N_META, *wts)
        xp = xp + o
        xp = xp + hier_moe(rms_norm(xp, norm_ffn_w[l]), *moe_w)
        pc.append(c1)
        pm.append(c2)
        ps.append(c3)
        o, c1, c2, c3 = token_mixer(rms_norm(xs, norm_mix_w[l]), state_conf_conv[l], state_ssm_conv[l],
                                    state_ssm[l], xs.shape[1], *wts)
        xs = xs + o
        xs = xs + hier_moe(rms_norm(xs, norm_ffn_w[l]), *moe_w)
        sc.append(c1)
        sm.append(c2)
        ss.append(c3)
    y_prompt = rms_norm(xp, norm_final_w)[:, N_META:]
    y_sample = rms_norm(xs, norm_final_w)
    new_conf_prompt = jnp.stack(pc)
    new_sconv_prompt = jnp.stack(pm)
    new_ssm_prompt = jnp.stack(ps)
    new_conf_sample = jnp.stack(sc)
    new_sconv_sample = jnp.stack(sm)
    new_ssm_sample = jnp.stack(ss)
    return (y_prompt, y_sample, new_conf_prompt, new_sconv_prompt, new_ssm_prompt,
            new_conf_sample, new_sconv_sample, new_ssm_sample)


_drawn_inputs = setup_inputs


def setup_inputs(seed=0):
    import zlib

    import numpy as np

    out = dict(_drawn_inputs(seed))
    spreads = {}
    factors = {'conf_dw_b': 2.769,
     'conf_ln_b': 3.545,
     'conf_out_b': 2.97,
     'gate_b': 4.011,
     'router_group_b': 3.64,
     'router_expert_b': 4.017}
    for name, (base, spread) in spreads.items():
        noise = np.random.default_rng([zlib.crc32(name.encode()), seed]).standard_normal(out[name].shape)
        drawn = base * np.exp(spread * noise) if base else spread * noise
        out[name] = __import__('jax').numpy.asarray(drawn.astype(out[name].dtype))
    for name, factor in factors.items():
        out[name] = (out[name] * factor).astype(out[name].dtype)
    return out
```

```python
from contextlib import ExitStack, contextmanager

import concourse.bass as bass
from concourse import mybir

F32 = mybir.dt.float32
U32 = mybir.dt.uint32
ALU = mybir.AluOpType
ACT = mybir.ActivationFunctionType
AX_X = mybir.AxisListType.X

P = 128
D = 1024
KD = D // P
NSAMP, TSAMP = 8, 4
META, SEQ = 16, 512
SAMP = NSAMP * TSAMP
PROMPT = META + SEQ
T = SAMP + PROMPT
CK, SK = 31, 4
G = 8
HG = 4
NH = G * HG
HD = 64
N = 128
DI = 2 * D
EPS = 1e-6
CHUNK = 128
CHUNKS = [(0, SAMP), (SAMP, META)] + [(SAMP + META + CHUNK * i, CHUNK) for i in range(SEQ // CHUNK)]
ORDER = [1, 2, 3, 4, 5, 0]
TILES = [(0, SAMP + META)] + CHUNKS[2:]
W_GV, W_GG, W_Z, W_X, W_B, W_C = 0, D, 2 * D, 4 * D, 6 * D, 7 * D
W_DT, W_GATE = 8 * D, 8 * D + NH
R_CW, R_CB, R_LG, R_LB, R_OB, R_NMIX = 0, CK, CK + 1, CK + 2, CK + 3, CK + 4
R_X, R_BC = CK + 5, CK + 15
R_NW = CK + 25
R_GB = CK + 27
R_NFFN = CK + 29
R_DS = CK + 30
NR = CK + 32
UO = 208
USPLIT = 512 - UO
RING = 5
DVE_STEPS = 59
N_CROW = 19
U_TILES = 14
U_OF = [0, 1, 2, 3, 4, 5, 8, 9, 10, 11]


class Steps:

    def __init__(self, eng, sem):
        self.eng, self.sem, self.base, self.n = eng, sem, 0, 0

    def link(self, ins):
        ins.then_inc(self.sem, 1)
        self.n += 1
        self.eng.wait_ge(self.sem, self.base + self.n)

    def enter(self, g, per):
        self.start, self.per = self.n, per
        self.base, self.n = g * per + self.n, 0

    def leave(self, trips):
        assert self.n == self.per, self.n
        self.n, self.base = self.start + trips * self.per, 0


@contextmanager
def semaphores(nc):
    held = []

    def sem(name):
        held.append(nc.alloc_semaphore(name=name))
        return held[-1]

    yield sem
    nc.clear_and_free_semaphores(held)
    nc.all_engine_barrier()


def trunk(nc, A, O, keep):
    aconv, yn, cs = keep["aconv"], keep["yn"], keep["cs"]
    ident, ones = keep["ident"], keep["ones"]
    w_in = A["w_in"][0]
    with ExitStack() as ctx:
        def sb(name, shape, dt=F32):
            return ctx.enter_context(nc.sbuf_tensor(name, shape, dt))

        sem = ctx.enter_context(semaphores(nc))

        xnT = sb("xnT", [P, KD, T])
        ring = sb("ring", [P, RING, KD, P])
        scr = sb("scr", [P, 5 * D])
        xin = scr[:, :].rearrange("p (t d) -> p t d", t=5)
        h0 = scr[:, 0:2048].rearrange("p (i b n) -> p i b n", i=2, b=NSAMP)
        h0T = scr[:, 2048:4096].rearrange("p (i b m) -> p i b m", i=2, b=NSAMP)
        Bblk = scr[0:SAMP, 4096:5120].rearrange("p (b n) -> p b n", b=NSAMP)
        stage = yn[:, :, :].rearrange("p a b -> p (a b)")
        crow = stage[0:R_DS, 0:D]
        confrow = stage[0:120, D:3 * D].rearrange("p (t d) -> p t d", t=2)
        ssmrow = stage[0:NSAMP * (SK - 1), 3 * D:7 * D]
        wdt = stage[:, 7 * D:7 * D + 256].rearrange("p (k m) -> p k m", k=KD)
        stC = sb("stC", [P, KD, NSAMP * (CK - 1)])
        stS = sb("stS", [P, 32, NSAMP * (SK - 1)])
        gc = sb("gc", [P, NR])
        U = sb("U", [P, P])
        SL = sb("SL", [P, P])
        Ub = sb("Ub", [SAMP, SAMP])
        SLb = sb("SLb", [SAMP, SAMP])
        Bm = sb("Bm", [SAMP, NSAMP])
        dtb = sb("dtb", [P, NH])
        expA = sb("expA", [P, NH])
        dtt = sb("dtt", [P, 6, NH])
        tmp1 = sb("tmp1", [P, 6, NH])
        tmp2 = sb("tmp2", [P, 6, NH])
        aa = sb("aa", [P, 6, NH])
        tail = sb("tail", [P, 6, NH])
        Dl = sb("Dl", [P, 6, NH])
        ss = sb("ss", [P, 8])
        raw_p = sb("raw_p", [P, 4, SK - 1 + PROMPT])
        raw_s = sb("raw_s", [P, 4, NSAMP, SK - 1 + TSAMP])
        cv = sb("cv", [P, 4, T])
        th = sb("th", [P, 2, T])
        a_p = sb("a_p", [P, CK - 1 + PROMPT])
        a_s = sb("a_s", [P, NSAMP, CK - 1 + TSAMP])
        cacc = sb("cacc", [P, T])
        ybuf = sb("ybuf", [P, 2, T])
        zc = sb("zc", [P, 2, T])
        Ed = sb("Ed", [P, 2, T])
        ab = sb("ab", [P, 6, HG * HD])
        ds0 = sb("ds0", [1, NH])
        dsrow = cv[0:1, :, :].rearrange("p q t -> p (q t)")[:, 0:DI]
        gbuf = sb("gbuf", [P, T])
        aU = sb("aU", [P, HG, P])
        Lx = sb("Lx", [P, HG, P])
        Tt = sb("Tt", [P, 4, P])
        cbm = sb("cbm", [P, P])
        xdt = sb("xdt", [P, HG, HD])
        xtl = sb("xtl", [P, HG, HD])
        hT = sb("hT", [P, HG, HD])
        hTd = sb("hTd", [P, HG, HD])
        yi = sb("yi", [P, 2, P])
        pk = sb("pk", [P, 4, 27])
        pk_rows = sb("pk_rows", [27, 4, P])
        pa = sb("pa", [P, 62])
        pa_rows = sb("pa_rows", [62, P])
        hout = sb("hout", [P, 2, P])
        pu = [ctx.enter_context(nc.psum_tensor(f"pu{i}", [P, 1024], F32)) for i in range(2)]
        pS, pT, pC, pY = (ctx.enter_context(nc.psum_tensor(n, [P, 512], F32)) for n in ("pS", "pT", "pC", "pY"))

        s_x, s_meta, s_crow, s_conf, s_ssm, s_wdt, s_dtb = map(
            sem, ("s_x", "s_meta", "s_crow", "s_conf", "s_ssm", "s_wdt", "s_dtb"))
        s_w = [sem(f"s_w{i}") for i in range(RING)]
        s_h0 = sem("s_h0")
        s_st_conf, s_st_ssm, s_st_h, s_st_pk, s_st_pa, s_st_hp = map(
            sem, ("s_st_conf", "s_st_ssm", "s_st_h", "s_st_pk", "s_st_pa", "s_st_hp"))
        s_zero, s_const, s_sq, s_var, s_sqrt, s_xs, s_fill, s_fillfree = map(
            sem, ("s_zero", "s_const", "s_sq", "s_var", "s_sqrt", "s_xs", "s_fill", "s_fillfree"))
        s_cs, s_dtp, s_dtraw, s_dte, s_dtl, s_a, s_tp, s_te, s_pro = map(
            sem, ("s_cs", "s_dtp", "s_dtraw", "s_dte", "s_dtl", "s_a", "s_tp", "s_te", "s_pro"))
        s_gc, s_u, s_ufree, s_raw, s_st, s_conv, s_thx, s_cv = map(
            sem, ("s_gc", "s_u", "s_ufree", "s_raw", "s_st", "s_conv", "s_thx", "s_cv"))
        s_pre, s_ab, s_pe1, s_L, s_T, s_W, s_xtl, s_hTd, s_pe2, s_y = map(
            sem, ("s_pre", "s_ab", "s_pe1", "s_L", "s_T", "s_W", "s_xtl", "s_hTd", "s_pe2", "s_y"))
        s_gv, s_ga, s_confst, s_cconv, s_z, s_yz, s_sq2, s_ms, s_rec, s_r, s_yn = map(
            sem, ("s_gv", "s_ga", "s_confst", "s_cconv", "s_z", "s_yz", "s_sq2", "s_ms", "s_rec", "s_r", "s_yn"))
        s_h0t, s_h0tev, s_Bblk, s_hs, s_hnew = map(sem, ("s_h0t", "s_h0tev", "s_Bblk", "s_hs", "s_hnew"))
        s_pk, s_out, s_outev = map(sem, ("s_pk", "s_out", "s_outev"))
        s_ident, s_ss, s_expA, s_stc, s_sts, s_g, s_gst = map(
            sem, ("s_ident", "s_ss", "s_expA", "s_stc", "s_sts", "s_g", "s_gst"))
        s_ds0, s_dsr, s_settled = sem("s_ds0"), sem("s_dsr"), sem("s_settled")
        c_dve, c_act, c_pool = map(sem, ("c_dve", "c_act", "c_pool"))
        block = ctx.enter_context(nc.Block())

        def settled(eng):
            eng.sem_inc(s_settled, 1)

        @block.sync
        def _(sp):
            sp.dma_start(crow[0:CK, :], A["conf_dw_w"][0]).then_inc(s_crow, 16)
            loads = [(R_CB, A["conf_dw_b"]), (R_LG, A["conf_ln_g"]), (R_LB, A["conf_ln_b"]),
                     (R_OB, A["conf_out_b"]), (R_NMIX, A["norm_mix_w"]), (R_NFFN, A["norm_ffn_w"])]
            for r, ap in loads:
                sp.dma_start(crow[r:r + 1, :], ap).then_inc(s_crow, 16)
            cw, cb = A["ssm_conv_w"][0], A["ssm_conv_b"]
            for i in range(2):
                dst = crow[R_X + 5 * i:R_X + 5 * i + 5, :].rearrange("r (g c) -> r g c", g=G)
                src = cw[:, 0:DI].rearrange("k (g i c) -> i k g c", i=2, g=G)[i]
                sp.dma_start(dst[0:SK], src).then_inc(s_crow, 16)
                src = cb[:, 0:DI].rearrange("k (g i c) -> i k g c", i=2, g=G)[i]
                sp.dma_start(dst[SK:SK + 1], src).then_inc(s_crow, 16)
                r = R_BC + 5 * i
                sp.dma_start(crow[r:r + SK, :], cw[:, DI + D * i:DI + D * i + D]).then_inc(s_crow, 16)
                sp.dma_start(crow[r + SK:r + SK + 1, :], cb[:, DI + D * i:DI + D * i + D]).then_inc(s_crow, 16)
                dst = crow[R_NW + i:R_NW + i + 1, :].rearrange("r (g c) -> r g c", g=G)
                src = A["ssm_norm_w"].rearrange("k (g i c) -> i k g c", i=2, g=G)[i]
                sp.dma_start(dst, src).then_inc(s_crow, 16)
                sp.dma_start(crow[R_GB + i:R_GB + i + 1, :], A["gate_b"][:, D * i:D * i + D]).then_inc(s_crow, 16)
            sp.dma_start(ds0[:, :], A["d_skip"]).then_inc(s_ds0, 16)
            def w_block(g, k):
                first = [W_GV + P * g, W_GG + P * g, W_X + 2 * P * g, W_X + 2 * P * g + P, W_B + P * g,
                         W_C + P * g, W_Z + 2 * P * g, W_Z + 2 * P * g + P, W_GATE + P * g,
                         W_GATE + D + P * g][k]
                src = w_in.rearrange("(k p) n -> p k n", p=P)[:, :, bass.ds(first, P)]
                sp.dma_start(ring[:, k % RING], src).then_inc(s_w[k % RING], 16)

            sp.dma_start(dtb[:, :], A["dt_bias"][0].partition_broadcast(P)).then_inc(s_dtb, 16)
            sp.dma_start(expA[:, :], A["a_log"][0].partition_broadcast(P)).then_inc(s_dtb, 16)
            sp.dma_start(wdt, w_in.rearrange("(k p) n -> p k n", p=P)[:, :, W_DT:W_DT + NH]).then_inc(s_wdt, 16)
            for k in range(RING):
                w_block(0, k)
            for t in range(2):
                src = A["state_conf_conv"][0].rearrange("(t b) r c -> t (b r) c", t=2)[t]
                sp.dma_start(confrow[:, t], src).then_inc(s_conf, 16)
            sp.dma_start(ssmrow, A["state_ssm_conv"][0].rearrange("b r c -> (b r) c")).then_inc(s_ssm, 16)
            sp.dma_start(O["new_conf_sample"][0][:, 0:CK - 1 - TSAMP, :],
                         A["state_conf_conv"][0][:, TSAMP:CK - 1, :]).then_inc(s_st_conf, 16)

            def states_in(g):
                sp.wait_ge(s_pro, 1)
                sp.wait_ge(s_st_h, 32 * g + 1)
                src = A["state_ssm"][0].rearrange("b (g i h) p n -> g i (h p) b n", i=2, h=2)
                for i in range(2):
                    sp.dma_start(h0[:, i], src[g, i]).then_inc(s_h0, 16)

            def states_out(g):
                sp.wait_ge(s_hnew, 4 * g + 4 + 1)
                dst = O["new_ssm_sample"][0].rearrange("b (g i h) p n -> g i (h p) b n", i=2, h=2)
                for i in range(2):
                    sp.dma_start(dst[g, i], h0[:, i]).then_inc(s_st_h, 16)

            def blocks(g, gnext, ks):
                for k in ks:
                    sp.wait_ge(s_u, U_TILES * g + U_OF[(k - RING) % (2 * RING)] + 2)
                    w_block(gnext, k)

            with sp.Fori(0, G - 1) as g:
                states_in(g)
                blocks(g, g, range(RING, 2 * RING))
                blocks(g, g + 1, range(RING))
                states_out(g)
            states_in(G - 1)
            blocks(G - 1, G - 1, range(RING, 2 * RING))
            states_out(G - 1)
            sp.wait_ge(s_st_h, 32 * G + 1)
            sp.wait_ge(s_st_conf, 16)

        @block.gpsimd
        def _(pool):
            for started in (s_st_h, s_pe1, s_pe2, s_yn, s_u, s_g, s_cconv, s_conv, s_y, s_hs, s_out, s_hnew, s_ufree, s_pk, s_xtl, s_W, s_gst, s_st_pk, s_st_pa, s_st_hp, s_outev):
                pool.sem_inc(started, 1)
            k = Steps(pool, c_pool)
            for m in (U, SL, ones, Ub, SLb, Bm):
                pool.memset(m[:, :], 1.0).then_inc(s_zero, 1)
            pool.memset(ident[:, :], 0.0).then_inc(s_zero, 1)
            pool.wait_ge(s_zero, 7)

            def mask(m, cond, base, pattern, mult, fill=0.0):
                k.link(pool.affine_select(out=m, in_=m, compare_op=cond, fill=fill, base=base,
                                          pattern=pattern, channel_multiplier=mult))

            mask(ident[:, :], ALU.not_equal, 0, [[-1, P]], 1, 1.0)
            pool.sem_inc(s_ident, 1)
            mask(U[:, :], ALU.is_ge, 0, [[1, P]], -1)
            mask(SL[:, :], ALU.is_gt, 0, [[-1, P]], 1)
            Ub3 = Ub[:, :].rearrange("k (b r) -> k b r", b=NSAMP)
            mask(Ub3, ALU.is_ge, 0, [[TSAMP, NSAMP], [1, TSAMP]], -1)
            mask(Ub3, ALU.is_ge, 0, [[-TSAMP, NSAMP], [0, TSAMP]], 1)
            SLb3 = SLb[:, :].rearrange("k (b r) -> k b r", b=NSAMP)
            mask(SLb3, ALU.is_gt, 0, [[-TSAMP, NSAMP], [-1, TSAMP]], 1)
            mask(SLb3, ALU.is_ge, TSAMP - 1, [[TSAMP, NSAMP], [0, TSAMP]], -1)
            mask(Bm[:, :], ALU.is_ge, 0, [[-TSAMP, NSAMP]], 1)
            mask(Bm[:, :], ALU.is_ge, TSAMP - 1, [[TSAMP, NSAMP]], -1)
            pool.memset(tail[:, :, :], 0.0).then_inc(s_const, 1)
            pool.memset(dtt[:, :, :], 0.0).then_inc(s_const, 1)
            pool.memset(raw_p[:, :, 0:SK - 1], 0.0).then_inc(s_const, 1)
            pool.memset(a_p[:, 0:CK - 1], 0.0).then_inc(s_const, 1)
            pool.wait_ge(s_pro, 1)

            with pool.Fori(0, G) as g:
                pool.wait_ge(s_yn, 2 * g + 1)
                pool.wait_ge(s_u, U_TILES * g + 1)
                pool.wait_ge(s_g, 2 * g + 1)
                settled(pool)
                pool.tensor_copy(gc[:, :], cs[:, g, :]).then_inc(s_gc, 1)
                for j in range(6):
                    ci, S = j, CHUNKS[j][1]
                    a4 = aa[0:S, ci, bass.ds(HG * g, HG)].unsqueeze(2)
                    pool.tensor_copy(ab[0:S, j, :].rearrange("s (h p) -> s h p", h=HG),
                                     a4.broadcast_to([S, HG, HD])).then_inc(s_ab, 1)
                pool.wait_ge(s_cconv, g + 1)
                settled(pool)
                pool.tensor_copy(a_s[:, :, 0:CK - 1],
                                 stC[:, g, :].rearrange("p (b r) -> p b r", b=NSAMP)).then_inc(s_stc, 1)
                pool.wait_ge(s_conv, 4 * g + 1)
                for q, m in enumerate((2 * g, 2 * g + 1, G * 2 + g, G * 3 + g)):
                    pool.tensor_copy(raw_s[:, q, :, 0:SK - 1],
                                     stS[:, m, :].rearrange("p (b r) -> p b r", b=NSAMP)).then_inc(s_sts, 1)

                def decay_rows(j):
                    ci = ORDER[j]
                    S = CHUNKS[ci][1]
                    a4 = aa[0:S, ci, bass.ds(HG * g, HG)].unsqueeze(2)
                    um = (Ub if ci == 0 else U)[0:S, 0:S].unsqueeze(1).broadcast_to([S, HG, S])
                    pool.wait_ge(s_pe1, 6 * g + j + 1)
                    settled(pool)
                    pool.tensor_tensor(aU[0:S, :, 0:S], a4.broadcast_to([S, HG, S]), um,
                                       ALU.mult).then_inc(s_pre, 1)

                decay_rows(0)
                for j in range(6):
                    ci = ORDER[j]
                    S = CHUNKS[ci][1]
                    t4 = tail[0:S, ci, bass.ds(HG * g, HG)].unsqueeze(2).broadcast_to([S, HG, HD])
                    pool.wait_ge(s_T, 6 * g + j + 1)
                    settled(pool)
                    pool.tensor_tensor(xtl[0:S, :, :],
                                       Tt[0:S, 0:2, :].rearrange("s i (h p) -> s (i h) p", h=2), t4,
                                       ALU.mult).then_inc(s_xtl, 1)
                    if 0 < j < 5:
                        d4 = Dl[:, ci, bass.ds(HG * g, HG)].unsqueeze(2).broadcast_to([P, HG, HD])
                        pool.wait_ge(s_y, 6 * g + j + 1)
                        settled(pool)
                        pool.tensor_tensor(hTd[:, :, :], hT[:, :, :], d4, ALU.mult).then_inc(s_hTd, 1)
                    if j == 5:
                        pool.wait_ge(s_hs, 4 * g + 1)
                        settled(pool)
                        pool.tensor_tensor(Bblk, Tt[0:SAMP, 2, :].unsqueeze(1).broadcast_to([SAMP, NSAMP, N]),
                                           Bm[:, :].unsqueeze(2).broadcast_to([SAMP, NSAMP, N]),
                                           ALU.mult).then_inc(s_Bblk, 1)
                    if j < 5:
                        decay_rows(j + 1)
                    if j == 0:
                        pool.wait_ge(s_out, 2 * g + 1)
                        settled(pool)
                        pool.tensor_copy(pk[:, :, 0:3], raw_p[:, :, PROMPT:PROMPT + 3]).then_inc(s_pk, 1)
                        for q in range(4):
                            pool.tensor_copy(pk[:, q, 3:27].rearrange("p (b r) -> p b r", b=NSAMP),
                                             raw_s[:, q, :, TSAMP:TSAMP + 3]).then_inc(s_pk, 1)
                        pool.tensor_copy(pa[:, 0:CK - 1], a_p[:, PROMPT:PROMPT + CK - 1]).then_inc(s_pk, 1)
                        pool.tensor_copy(pa[:, CK - 1:62].rearrange("p (r b) -> p b r", b=NSAMP),
                                         a_s[:, :, CK - 1:CK - 1 + TSAMP]).then_inc(s_pk, 1)

        def u_cols(i, a, b):
            return pu[i % 2][:, UO + a:UO + b]

        @block.scalar
        def _(act):
            k = Steps(act, c_act)
            act.dma_start(xin[0:SAMP, 0, :], A["x_sample"].rearrange("b t d -> (b t) d")).then_inc(s_x, 16)
            act.dma_start(xin[SAMP:SAMP + META, 0, :], A["meta_tokens"]).then_inc(s_x, 16)
            act.dma_start(xin[:, 1:5, :], A["x_prompt"][0].rearrange("(t p) d -> p t d", p=P)).then_inc(s_x, 16)
            act.wait_ge(s_x, 48)
            act.wait_ge(s_ss, 1)
            for t, (c, S) in enumerate(TILES):
                k.link(act.activation(ybuf[0:S, :, :].rearrange("p a b -> p (a b)")[:, 0:D], xin[0:S, t, :],
                                      ACT.Square, accum_out=ss[0:S, t:t + 1]))
            act.sem_inc(s_sq, 1)
            act.wait_ge(s_var, 1)
            act.activation(ss[:, 0:5], ss[:, 0:5], ACT.Sqrt).then_inc(s_sqrt, 1)
            act.wait_ge(s_dtb, 32)
            act.activation(expA[:, :], expA[:, :], ACT.Exp).then_inc(s_expA, 1)
            act.wait_ge(s_dte, 1)
            k.link(act.activation(tmp2[:, :, :], tmp2[:, :, :], ACT.Exp))
            act.activation(tmp2[:, :, :], tmp2[:, :, :], ACT.Ln, bias=1.0).then_inc(s_dtl, 1)
            act.wait_ge(s_tp, 1)
            for ci, (c, S) in enumerate(CHUNKS):
                act.activation(tail[0:S, ci, :], pY[0:S, NH * ci:NH * ci + NH], ACT.Exp).then_inc(s_te, 1)
            act.activation(Dl[:, 1:6, :], pY[:, 7 * NH:12 * NH].rearrange("p (c h) -> p c h", c=5),
                           ACT.Exp).then_inc(s_te, 1)

            with act.Fori(0, G) as g:
                U0 = U_TILES * g

                def evac(r):
                    act.wait_ge(s_u, U0 + r + 2)

                evac(0)
                act.wait_ge(s_yn, 2 * g + 1)
                act.activation(zc[:, 0, :], u_cols(0, 0, T), ACT.Copy, scale=0.5).then_inc(s_ufree, 1)
                evac(1)
                act.activation(zc[:, 1, :], u_cols(1, 0, T), ACT.Tanh, scale=0.5).then_inc(s_ufree, 1)

                def raw(q):
                    evac(2 + q)
                    act.wait_ge(s_conv, 4 * g + 1)
                    act.wait_ge(s_pk, 7 * g + 1)
                    act.activation(raw_p[:, q, SK - 1:], u_cols(q, SAMP, T), ACT.Copy).then_inc(s_raw, 1)
                    act.activation(raw_s[:, q, :, SK - 1:], u_cols(q, 0, SAMP).rearrange("p (b r) -> p b r", b=NSAMP),
                                   ACT.Copy).then_inc(s_ufree, 1)

                def silu(q):
                    act.wait_ge(s_conv, 4 * g + q + 2)
                    if q < 2:
                        act.wait_ge(s_u, U0 + 1)
                    else:
                        act.wait_ge(s_cv, 4 * g + q - 1)
                    act.activation(th[:, q % 2, :], cv[:, q, :], ACT.Tanh).then_inc(s_thx, 1)

                raw(0)
                raw(1)
                silu(0)
                raw(2)
                silu(1)
                raw(3)
                silu(2)
                for i in range(2):
                    evac(6 + i)
                    act.wait_ge(s_hnew, 4 * g + 1)
                    act.activation(Ed[:, i, :], u_cols(i, 0, T), ACT.Exp).then_inc(s_ufree, 1)
                silu(3)

                def chunk(j):
                    ci = ORDER[j]
                    S = CHUNKS[ci][1]
                    act.wait_ge(s_pe1, 6 * g + j + 2)
                    act.wait_ge(s_pe2, 6 * g + j + 1)
                    act.activation(Lx[0:S, :, 0:S], pS[0:S, :].rearrange("s (h t) -> s h t", h=HG)[:, :, 0:S],
                                   ACT.Exp).then_inc(s_L, 1)
                    act.wait_ge(s_W, 6 * g + j + 1)
                    act.wait_ge(s_xtl, 6 * g + j + 1)
                    act.wait_ge(s_hs, 4 * g + 1)
                    if S == P:
                        act.activation(Tt[:, :, :].rearrange("s a t -> s (a t)"), pT[:, :], ACT.Copy).then_inc(s_T, 1)
                    else:
                        act.activation(Tt[0:S, 0:3, :].rearrange("s a t -> s (a t)"), pT[0:S, 0:3 * P], ACT.Copy)
                        act.activation(Tt[0:S, 3, 0:S], pT[0:S, 3 * P:3 * P + S], ACT.Copy).then_inc(s_T, 1)

                def z(i):
                    evac(8 + i)
                    act.wait_ge(s_ga, 2 * g + 2)
                    act.wait_ge(s_cv, 4 * g + 3 + i)
                    act.activation(th[:, i, :], u_cols(i, 0, T), ACT.Tanh, scale=0.5).then_inc(s_z, 1)
                    act.activation(zc[:, i, :], u_cols(i, 0, T), ACT.Copy).then_inc(s_ufree, 1)

                def gate(i):
                    evac(10 + i)
                    act.wait_ge(s_gc, g + 1)
                    act.wait_ge(s_gst, 32 * g + 16 * i + 1)
                    act.activation(gbuf[:, :], u_cols(i, 0, T), ACT.Tanh, bias=gc[:, R_GB + i:R_GB + i + 1],
                                   scale=0.5).then_inc(s_g, 1)
                    act.wait_ge(s_g, 2 * g + i + 2)
                    act.sem_inc(s_ufree, 1)
                    act.dma_start(keep["gates"][i, g], gbuf[:, :]).then_inc(s_gst, 16)

                def h0_copy(r):
                    act.wait_ge(s_h0t, 4 * g + r + 1)
                    act.wait_ge(s_pe2, 6 * g + 1)
                    act.activation(h0T[:, r // 2, 4 * (r % 2):4 * (r % 2) + 4, :].rearrange("p b m -> p (b m)"),
                                   (pS, pT)[r % 2][:, :], ACT.Copy).then_inc(s_h0tev, 1)

                chunk(0)
                z(0)
                chunk(1)
                chunk(2)
                z(1)
                chunk(3)
                chunk(4)
                gate(0)
                chunk(5)
                for r in range(4):
                    h0_copy(r)
                gate(1)
                act.wait_ge(s_yz, g + 1)
                act.activation(th[:, :, :], ybuf[:, :, :], ACT.Square).then_inc(s_sq2, 1)
                act.wait_ge(s_out, 2 * g + 2)
                act.wait_ge(s_st_pk, 96 * g + 1)
                act.wait_ge(s_st_pa, 80 * g + 1)
                act.wait_ge(s_st_hp, 16 * g + 1)
                act.activation(pk_rows[:, :, :].rearrange("r q c -> r (q c)"), pC[0:27, :], ACT.Copy).then_inc(s_outev, 1)
                act.wait_ge(s_out, 2 * g + 2 + 1)
                act.activation(hout[:, :, :].rearrange("p i n -> p (i n)"), pY[:, 0:2 * P], ACT.Copy).then_inc(s_outev, 1)
                act.activation(pa_rows[:, :], pY[0:62, 2 * P:3 * P], ACT.Copy).then_inc(s_outev, 1)
                act.wait_ge(s_outev, 3 * g + 3 + 1)
                pks = pk_rows[:, :, :]
                for dst, r0, n in ((O["new_sconv_prompt"][0, 0], 0, 3),
                                   (O["new_sconv_sample"][0].rearrange("b r c -> (b r) c"), 3, 24)):
                    act.dma_start(dst[:, bass.ds(2 * P * g, 2 * P)].rearrange("r (q c) -> r q c", q=2),
                                  pks[r0:r0 + n, 0:2, :]).then_inc(s_st_pk, 16)
                    for q in range(2):
                        act.dma_start(dst[:, bass.ds(DI + D * q + P * g, P)],
                                      pks[r0:r0 + n, 2 + q, :]).then_inc(s_st_pk, 16)
                act.dma_start(O["new_conf_prompt"][0, 0][:, bass.ds(P * g, P)],
                              pa_rows[0:CK - 1, :]).then_inc(s_st_pa, 16)
                act.dma_start(O["new_ssm_prompt"][0, 0].rearrange("(g i h) p n -> g (h p) i n", i=2, h=2)[g],
                              hout[:, :, :]).then_inc(s_st_hp, 16)
                for r in range(TSAMP):
                    act.dma_start(O["new_conf_sample"][0][:, CK - 1 - TSAMP + r, bass.ds(P * g, P)],
                                  pa_rows[CK - 1 + NSAMP * r:CK - 1 + NSAMP * r + NSAMP, :]).then_inc(s_st_pa, 16)
                for r in range(2):
                    evac(12 + r)
                    act.activation(zc[:, 0, 280 * r:280 * r + 280], pu[r][:, 0:280], ACT.Identity,
                                   scale=1.0 / (2 * P), bias=EPS).then_inc(s_ufree, 1)
                act.wait_ge(s_rec, g + 1)
                act.activation(zc[:, 0, :], zc[:, 1, :], ACT.Sqrt).then_inc(s_r, 1)
            act.wait_ge(s_st_pk, 96 * G + 1)
            act.wait_ge(s_st_pa, 80 * G + 1)
            act.wait_ge(s_st_hp, 16 * G + 1)
            act.wait_ge(s_gst, 32 * G + 1)

        @block.tensor
        def _(pe):
            fill_no = [0]

            def fill(parts):
                n = fill_no[0]
                bank = (pS, pT)[n % 2]
                if n >= 2:
                    pe.wait_ge(s_fillfree, n - 1)
                for col, src in parts:
                    R, C = src.shape
                    last = pe.transpose(bank[0:C, col:col + R], src, ident[0:R, 0:R])
                last.then_inc(s_fill, 1)
                fill_no[0] += 1

            pe.wait_ge(s_ident, 1)
            pe.wait_ge(s_crow, 16 * N_CROW)
            pe.wait_ge(s_dsr, 1)
            fill([(64 * j, crow[:, P * j:P * j + P]) for j in range(KD)]
                 + [(64 * g + R_DS + i, dsrow[:, P * (2 * g + i):P * (2 * g + i) + P])
                    for g in range(G) for i in range(2)])
            for t, (c, S) in enumerate(TILES):
                pe.wait_ge(s_xs, t + 1)
                for h in range(2):
                    fill([(P * q, xin[0:S, t, P * (4 * h + q):P * (4 * h + q) + P]) for q in range(4)])
            pe.wait_ge(s_conf, 32)
            for t in range(2):
                for h in range(2):
                    fill([(P * q, confrow[:, t, P * (4 * h + q):P * (4 * h + q) + P]) for q in range(4)])
            pe.wait_ge(s_ssm, 16)
            for f in range(2):
                fill([(32 * q, ssmrow[:, P * (16 * f + q):P * (16 * f + q) + P]) for q in range(16)])
            pe.wait_ge(s_wdt, 16)
            pe.wait_ge(s_fillfree, 11)
            for ci, (c, S) in enumerate(CHUNKS):
                for j in range(KD):
                    last = pe.matmul(pC[0:S, NH * ci:NH * ci + NH], xnT[:, j, c:c + S], wdt[:, j, :],
                                     start=(j == 0), stop=(j == KD - 1))
            last.then_inc(s_dtp, 1)
            pe.wait_ge(s_a, 1)
            for ci, (c, S) in enumerate(CHUNKS):
                pe.matmul(pY[0:S, NH * ci:NH * ci + NH], (SLb if ci == 0 else SL)[0:S, 0:S], aa[0:S, ci, :],
                          start=True, stop=True)
            for ci, (c, S) in enumerate(CHUNKS[1:], 1):
                last = pe.matmul(pY[:, NH * (6 + ci):NH * (7 + ci)], ones[0:S, :], aa[0:S, ci, :],
                                 start=True, stop=True)
            last.then_inc(s_tp, 1)
            pe.wait_ge(s_te, 7)
            pe.wait_ge(s_fillfree, 17)

            with pe.Fori(0, G) as g:
                U0 = U_TILES * g

                def free(r):
                    pe.wait_ge(s_ufree, U0 + max(r, 1))

                def block(k, halves=(0, 1)):
                    r = U_OF[k]
                    for h in halves:
                        if h == 0:
                            free(r)
                            pe.wait_ge(s_w[k % RING], 32 * g + 16 * (k // RING + 1))
                        for j in range(4 * h, 4 * h + 4):
                            for a, b in ((0, USPLIT), (USPLIT, T)):
                                last = pe.matmul(u_cols(r, a, b), ring[:, k % RING, j, :], xnT[:, j, a:b],
                                                 start=(j == 0), stop=(j == KD - 1))
                        if h == 1:
                            last.then_inc(s_u, 1)

                def stage1(j):
                    ci = ORDER[j]
                    c, S = CHUNKS[ci]
                    pe.wait_ge(s_pre, 6 * g + j + 1)
                    if j == 0:
                        pe.wait_ge(s_hnew, 4 * g + 1)
                    else:
                        pe.wait_ge(s_L, 6 * g + j)
                    if S < P:
                        settled(pe)
                    pe.matmul(pS[0:S, :].rearrange("s (h t) -> s h t", h=HG)[:, :, 0:S],
                              (SLb if ci == 0 else SL)[0:S, 0:S], aU[0:S, :, 0:S], start=True, stop=True)
                    if j == 0:
                        pe.wait_ge(s_cv, 4 * g + 4)
                    else:
                        pe.wait_ge(s_T, 6 * g + j)
                    for q in range(3):
                        pe.transpose(pT[0:S, P * q:P * q + P], cv[:, q, c:c + S], ident[:, :])
                    pe.matmul(pT[0:S, 3 * P:3 * P + S], cv[:, 2, c:c + S], cv[:, 3, c:c + S],
                              start=True, stop=True).then_inc(s_pe1, 1)

                def stage2(j):
                    ci = ORDER[j]
                    c, S = CHUNKS[ci]
                    pe.wait_ge(s_W, 6 * g + j + 2)
                    pe.wait_ge(s_xtl, 6 * g + j + 2)
                    pe.wait_ge(s_y, 6 * g + j + 1)
                    pe.wait_ge(s_outev, 3 * g + 1)
                    yv = pY[:, 0:2 * P].rearrange("p (i t) -> p i t", i=2)
                    for h in range(HG):
                        half = HD * (h % 2)
                        last = pe.matmul(yv[half:half + HD, h // 2, 0:S], xdt[0:S, h, :], Lx[0:S, h, 0:S],
                                         start=True, stop=True)
                    if ci >= 2:
                        for i in range(2):
                            pe.matmul(pC[:, P * i:P * i + S], hT[:, 2 * i:2 * i + 2, :], cv[:, 3, c:c + S],
                                      start=True, stop=True)
                    if ci == 0:
                        pe.wait_ge(s_h0tev, 4 * g + 4)
                        for i in range(2):
                            for b in range(NSAMP):
                                last = pe.matmul(pC[:, P * i + TSAMP * b:P * i + TSAMP * b + TSAMP],
                                                 h0T[:, i, b, :], cv[:, 3, TSAMP * b:TSAMP * b + TSAMP],
                                                 start=True, stop=True)
                    else:
                        last = pe.matmul(pC[:, 2 * P:4 * P], Tt[0:S, 2, :], xtl[0:S, :, :], start=True, stop=True)
                    last.then_inc(s_pe2, 1)

                def states_turned(r):
                    if r == 0:
                        pe.wait_ge(s_h0, 32 * g + 32)
                    if r < 2:
                        pe.wait_ge((s_L, s_T)[r], 6 * g + 6)
                    else:
                        pe.wait_ge(s_h0tev, 4 * g + r - 1)
                    for b in range(4):
                        last = pe.transpose((pS, pT)[r % 2][:, P * b:P * b + P], h0[:, r // 2, 4 * (r % 2) + b, :],
                                            ident[:, :])
                    last.then_inc(s_h0t, 1)

                def states_added(r):
                    pe.wait_ge(s_Bblk, g + 1)
                    if r < 2:
                        pe.wait_ge(s_h0tev, 4 * g + r + 3)
                    else:
                        pe.wait_ge(s_hnew, 4 * g + r)
                    i, q = r // 2, r % 2
                    pe.matmul((pS, pT)[r % 2][:, :], xtl[0:SAMP, 2 * i:2 * i + 2, :],
                              Bblk[:, 4 * q:4 * q + 4, :], start=True, stop=True).then_inc(s_hs, 1)

                for k in range(6):
                    block(k)
                free(7)
                pe.wait_ge(s_ab, 6 * g + 6)
                for i in range(2):
                    for ci, (c, S) in enumerate(CHUNKS):
                        last = pe.matmul(u_cols(i, c, c + S), ab[0:S, ci, P * i:P * i + P],
                                         (Ub if ci == 0 else U)[0:S, 0:S], start=True, stop=True)
                    last.then_inc(s_u, 1)
                block(6, (0,))
                stage1(0)
                block(6, (1,))
                stage2(0)
                stage1(1)
                block(7, (0,))
                stage2(1)
                stage1(2)
                block(7, (1,))
                stage2(2)
                stage1(3)
                block(8, (0,))
                stage2(3)
                stage1(4)
                block(8, (1,))
                stage2(4)
                stage1(5)
                states_turned(0)
                states_turned(1)
                block(9, (0,))
                states_turned(2)
                states_turned(3)
                block(9, (1,))
                stage2(5)
                for r in range(4):
                    states_added(r)
                pe.wait_ge(s_y, 6 * g + 6 + 1)
                pe.wait_ge(s_pk, 7 * g + 7 + 1)
                for q in range(4):
                    last = pe.transpose(pC[0:27, P * q:P * q + P], pk[:, q, :], ident[:, :])
                last.then_inc(s_out, 1)
                for i in range(2):
                    pe.transpose(pY[:, P * i:P * i + P], hT[:, 2 * i:2 * i + 2, :].rearrange("n h p -> n (h p)"), ident[:, :])
                pe.transpose(pY[0:62, 2 * P:3 * P], pa[:, :], ident[:, :]).then_inc(s_out, 1)
                pe.wait_ge(s_sq2, g + 1)
                for r in range(2):
                    free(12 + r)
                    for i in range(2):
                        last = pe.matmul(pu[r][:, 0:280], ones[:, :], th[:, i, 280 * r:280 * r + 280],
                                         start=(i == 0), stop=(i == 1))
                    last.then_inc(s_u, 1)

        @block.vector
        def _(dve):
            k = Steps(dve, c_dve)

            def stt(out, in0, scalar, in1, op0=ALU.mult, op1=ALU.add):
                return dve.scalar_tensor_tensor(out=out, in0=in0, scalar=scalar, in1=in1, op0=op0, op1=op1)

            dve.memset(ss[:, :], 1.0).then_inc(s_ss, 1)
            dve.wait_ge(s_ds0, 16)
            dve.tensor_copy(dsrow.rearrange("p (h c) -> p h c", h=NH),
                            ds0[:, :].unsqueeze(2).broadcast_to([1, NH, HD])).then_inc(s_dsr, 1)
            dve.wait_ge(s_fill, 1)
            k.link(dve.tensor_copy(cs[:, :, :], pS[:, :].rearrange("p (g r) -> p g r", g=G)[:, :, 0:NR]))
            dve.sem_inc(s_fillfree, 1)
            k.link(dve.tensor_scalar(cs[:, :, R_X:R_X + 20], cs[:, :, R_X:R_X + 20], 0.5, None, ALU.mult))
            k.link(dve.tensor_scalar(cs[:, :, R_GB:R_GB + 2], cs[:, :, R_GB:R_GB + 2], 0.5, None, ALU.mult))
            dve.wait_ge(s_sq, 1)
            dve.tensor_scalar(ss[:, 0:5], ss[:, 0:5], 1.0 / D, EPS, ALU.mult, ALU.add).then_inc(s_var, 1)
            dve.wait_ge(s_sqrt, 1)
            k.link(dve.reciprocal(ss[:, 0:5], ss[:, 0:5]))
            for t, (c, S) in enumerate(TILES):
                dve.tensor_scalar(xin[0:S, t, :], xin[0:S, t, :], ss[0:S, t:t + 1], None, ALU.mult).then_inc(s_xs, 1)
            n = 1
            for t, (c, S) in enumerate(TILES):
                for h in range(2):
                    dve.wait_ge(s_fill, n + 1)
                    w = cs[:, 4 * h:4 * h + 4, R_NMIX].unsqueeze(2).broadcast_to([P, 4, S])
                    dve.tensor_tensor(xnT[:, 4 * h:4 * h + 4, c:c + S],
                                      (pS, pT)[n % 2][:, :].rearrange("p (q s) -> p q s", q=4)[:, :, 0:S], w,
                                      ALU.mult).then_inc(s_fillfree, 1)
                    n += 1
            for t in range(2):
                for h in range(2):
                    dve.wait_ge(s_fill, n + 1)
                    dve.tensor_copy(stC[:, 4 * h:4 * h + 4, 120 * t:120 * t + 120],
                                    (pS, pT)[n % 2][:, :].rearrange("p (q s) -> p q s", q=4)[:, :, 0:120])\
                       .then_inc(s_fillfree, 1)
                    n += 1
            for f in range(2):
                dve.wait_ge(s_fill, n + 1)
                dve.tensor_copy(stS[:, 16 * f:16 * f + 16, :],
                                (pS, pT)[n % 2][:, :].rearrange("p (q s) -> p q s", q=16)[:, :, 0:24])\
                   .then_inc(s_fillfree, 1)
                n += 1
            dve.wait_ge(s_const, 4)
            dve.wait_ge(s_dtb, 32)
            dve.wait_ge(s_dtp, 1)
            for ci, (c, S) in enumerate(CHUNKS):
                last = dve.tensor_tensor(dtt[0:S, ci, :], pC[0:S, NH * ci:NH * ci + NH], dtb[0:S, :], ALU.add)
            k.link(last)
            k.link(dve.tensor_scalar(tmp1[:, :, :], dtt[:, :, :], 0.0, None, ALU.max))
            stt(tmp2[:, :, :], tmp1[:, :, :], -2.0, dtt[:, :, :]).then_inc(s_dte, 1)
            dve.wait_ge(s_dtl, 1)
            dve.wait_ge(s_expA, 1)
            k.link(dve.tensor_tensor(dtt[:, :, :], tmp1[:, :, :], tmp2[:, :, :], ALU.add))
            stt(aa[:, :, :], dtt[:, :, :], -1.0, expA[:, :].unsqueeze(1).broadcast_to([P, 6, NH]),
                ALU.mult, ALU.mult).then_inc(s_a, 1)
            dve.wait_ge(s_te, 7)
            dve.tensor_tensor(tail[:, :, :], tail[:, :, :], dtt[:, :, :], ALU.mult).then_inc(s_pro, 1)
            dve.wait_ge(s_pro, 1)

            with dve.Fori(0, G) as g:
                k.enter(g, DVE_STEPS)
                win3 = a_s[:, :, :]

                def conf_tap(j):
                    wj = gc[:, R_CW + j:R_CW + j + 1]
                    outs = ((aconv[:, g, :] if j == CK - 1 else cacc[:, :]))
                    o_s = outs[:, 0:SAMP].rearrange("p (b r) -> p b r", b=NSAMP)
                    o_p = outs[:, SAMP:T]
                    i_s, i_p = a_s[:, :, j:j + TSAMP], a_p[:, j:j + PROMPT]
                    if j == 0:
                        bias = gc[:, R_CB:R_CB + 1]
                        dve.tensor_scalar(o_s, i_s, wj, bias, ALU.mult, ALU.add)
                        k.link(dve.tensor_scalar(o_p, i_p, wj, bias, ALU.mult, ALU.add))
                    else:
                        stt(o_s, i_s, wj, cacc[:, 0:SAMP].rearrange("p (b r) -> p b r", b=NSAMP))
                        ins = stt(o_p, i_p, wj, cacc[:, SAMP:T])
                        if j == CK - 1:
                            ins.then_inc(s_cconv, 1)
                        else:
                            k.link(ins)

                def ssm_conv(q):
                    r = R_X + 5 * q
                    dve.wait_ge(s_ufree, U_TILES * g + 3 + q + 1)
                    dve.wait_ge(s_raw, 4 * g + q + 1)
                    dve.wait_ge(s_sts, 4 * g + q + 1)
                    o_s = cv[:, q, 0:SAMP].rearrange("p (b r) -> p b r", b=NSAMP)
                    o_p = cv[:, q, SAMP:T]
                    for j in range(SK):
                        wj = gc[:, r + j:r + j + 1]
                        i_s, i_p = raw_s[:, q, :, j:j + TSAMP], raw_p[:, q, j:j + PROMPT]
                        if j == 0:
                            bias = gc[:, r + SK:r + SK + 1]
                            dve.tensor_scalar(o_s, i_s, wj, bias, ALU.mult, ALU.add)
                            k.link(dve.tensor_scalar(o_p, i_p, wj, bias, ALU.mult, ALU.add))
                        else:
                            stt(o_s, i_s, wj, o_s)
                            ins = stt(o_p, i_p, wj, o_p)
                            if j == SK - 1:
                                ins.then_inc(s_conv, 1)
                            else:
                                k.link(ins)

                def silu(q):
                    dve.wait_ge(s_thx, 4 * g + q + 1)
                    stt(cv[:, q, :], th[:, q % 2, :], 1.0, cv[:, q, :], ALU.add, ALU.mult).then_inc(s_cv, 1)

                def stage1(j):
                    ci = ORDER[j]
                    S = CHUNKS[ci][1]
                    um = (Ub if ci == 0 else U)[0:S, 0:S]
                    dve.wait_ge(s_T, 6 * g + j + 1)
                    k.link(dve.tensor_tensor(cbm[0:S, 0:S], Tt[0:S, 3, 0:S], um, ALU.mult))
                    dt4 = dtt[0:S, ci, bass.ds(HG * g, HG)].unsqueeze(2).broadcast_to([S, HG, HD])
                    dve.tensor_tensor(xdt[0:S, :, :], Tt[0:S, 0:2, :].rearrange("s i (h p) -> s (i h) p", h=2),
                                      dt4, ALU.mult)
                    dve.tensor_tensor(Lx[0:S, :, 0:S], Lx[0:S, :, 0:S],
                                      cbm[0:S, 0:S].unsqueeze(1).broadcast_to([S, HG, S]),
                                      ALU.mult).then_inc(s_W, 1)

                def stage2(j):
                    ci = ORDER[j]
                    c, S = CHUNKS[ci]
                    dve.wait_ge(s_pe2, 6 * g + j + 2)
                    yv = pY[:, 0:2 * P].rearrange("p (i t) -> p i t", i=2)[:, :, 0:S]
                    if ci == 1:
                        for i in range(2):
                            stt(ybuf[:, i, c:c + S], cv[:, i, c:c + S], gc[:, R_DS + i:R_DS + i + 1], yv[:, i, :])
                    else:
                        v = yi[:, :, 0:S]
                        k.link(dve.tensor_tensor(v, pC[:, 0:2 * P].rearrange("p (i t) -> p i t", i=2)[:, :, 0:S],
                                                 Ed[:, :, c:c + S], ALU.mult))
                        k.link(dve.tensor_tensor(v, v, yv, ALU.add))
                        for i in range(2):
                            last = stt(ybuf[:, i, c:c + S], cv[:, i, c:c + S], gc[:, R_DS + i:R_DS + i + 1],
                                       yi[:, i, 0:S])
                    st = pC[:, 2 * P:4 * P].rearrange("p (h q) -> p h q", h=HG)
                    if ci == 1:
                        last = dve.tensor_copy(hT[:, :, :], st)
                    elif ci > 1:
                        dve.wait_ge(s_hTd, 4 * g + j)
                        last = dve.tensor_tensor(hT[:, :, :], hTd[:, :, :], st, ALU.add)
                    last.then_inc(s_y, 1)

                dve.wait_ge(s_gc, g + 1)
                dve.wait_ge(s_ufree, U_TILES * g + 2 + 1)
                dve.wait_ge(s_stc, g + 1)
                dve.wait_ge(s_pk, 7 * g + 1)
                dve.wait_ge(s_cconv, g + 1)
                stt(a_s[:, :, CK - 1:], zc[:, 1, 0:SAMP].rearrange("p (b r) -> p b r", b=NSAMP), 1.0,
                    zc[:, 0, 0:SAMP].rearrange("p (b r) -> p b r", b=NSAMP), ALU.add, ALU.mult).then_inc(s_ga, 1)
                stt(a_p[:, CK - 1:], zc[:, 1, SAMP:T], 1.0, zc[:, 0, SAMP:T], ALU.add, ALU.mult).then_inc(s_ga, 1)
                dve.wait_ge(s_ga, 2 * g + 2)
                tap = iter(range(CK))
                for q in range(4):
                    for _ in range(4):
                        conf_tap(next(tap))
                    if q == 0:
                        dve.wait_ge(s_y, 6 * g + 1)
                    ssm_conv(q)
                    if q:
                        silu(q - 1)
                silu(3)
                stage1(0)
                conf_tap(next(tap))
                conf_tap(next(tap))
                conf_tap(next(tap))
                stage2(0)
                for j in range(1, 6):
                    stage1(j)
                    if j < 5:
                        for _ in range(3):
                            conf_tap(next(tap))
                        stage2(j)
                dve.wait_ge(s_z, 2 * g + 2)
                dve.wait_ge(s_ufree, U_TILES * g + 10 + 1)
                k.link(stt(zc[:, :, :], th[:, :, :], 1.0, zc[:, :, :], ALU.add, ALU.mult))
                stage2(5)
                dve.wait_ge(s_y, 6 * g + 6 + 1)
                stt(ybuf[:, :, :], ybuf[:, :, :], 0.5, zc[:, :, :], ALU.mult, ALU.mult).then_inc(s_yz, 1)
                for r in range(4):
                    dve.wait_ge(s_hs, 4 * g + r + 2)
                    dve.wait_ge(s_h0t, 4 * g + 4)
                    for b in range(4):
                        bb, i = 4 * (r % 2) + b, r // 2
                        last = stt(h0[:, i, bb, :], h0[:, i, bb, :],
                                   Ed[:, i, TSAMP * bb + TSAMP - 1:TSAMP * bb + TSAMP],
                                   (pS, pT)[r % 2][:, P * b:P * b + P])
                    last.then_inc(s_hnew, 1)
                dve.wait_ge(s_ufree, U_TILES * g + 14 + 1)
                dve.reciprocal(zc[:, 1, :], zc[:, 0, :]).then_inc(s_rec, 1)
                dve.wait_ge(s_r, g + 1)
                for i in range(2):
                    stt(yn[:, 2 * g + i, :], ybuf[:, i, :], gc[:, R_NW + i:R_NW + i + 1], zc[:, 0, :],
                        ALU.mult, ALU.mult).then_inc(s_yn, 1)
                k.leave(G)


OT = [(0, SAMP)] + CHUNKS[2:]
NT = len(OT)
ROW = [0] + [SAMP + P * t for t in range(NT - 1)]
NE, NGR, EPG, DE = 32, 4, 8, 256
SLOT = 128
PAIRS = 2 * (SAMP + SEQ)
NTILE = NE + (PAIRS - NE) // SLOT
MAXT = -(-(SAMP + SEQ) // SLOT)
BIG = 3.0e38


def mixer(nc, A, O, keep):
    aconv, yn, cs, x1, ones = keep["aconv"], keep["yn"], keep["cs"], keep["x1"], keep["ones"]
    with ExitStack() as ctx:
        def sb(name, shape, dt=F32):
            return ctx.enter_context(nc.sbuf_tensor(name, shape, dt))

        sem = ctx.enter_context(semaphores(nc))

        RW = 3
        wring = sb("wring", [P, RW, 2 * D])
        wo = sb("wo", [P, KD, D])
        mg = sb("mg", [P, KD, T])
        gt = sb("gt", [P, 4, T])
        sq = sb("sq", [P, 2, T])
        mean = sb("mean", [P, T])
        rs = sb("rs", [P, T])
        rr = sb("rr", [P, T])
        ya = sb("ya", [P, 2, T])
        ss2 = sb("ss2", [P, 8])
        pm = [ctx.enter_context(nc.psum_tensor(f"pm{i}", [P, 1024], F32)) for i in range(2)]
        pst = ctx.enter_context(nc.psum_tensor("pst", [P, 1024], F32))
        po = ctx.enter_context(nc.psum_tensor("po", [P, 1024], F32))
        s_w = [sem(f"m_w{i}") for i in range(RW)]
        s_g = [sem(f"m_g{i}") for i in range(4)]
        s_wo, s_xr, s_p, s_stat, s_mean, s_cen, s_sq, s_eps, s_inv, s_root, s_tan, s_act, s_ya, s_gfree, s_mg, s_o, \
            s_x1, s_ssq, s_var, s_sd = map(sem, (
                "m_wo", "m_xr", "m_p", "m_stat", "m_mean", "m_cen", "m_sq", "m_eps", "m_inv", "m_root",
                "m_tan", "m_act", "m_ya", "m_gfree", "m_mg", "m_o", "m_x1", "m_ssq", "m_var", "m_sd"))
        s_lin, s_rinv, s_sqf, s_xs, s_ss = sem("m_lin"), sem("m_rinv"), sem("m_sqf"), sem("m_xs"), sem("m_ss")
        c_dve = sem("m_dve")
        block = ctx.enter_context(nc.Block())

        def cols(ps, a, b):
            return ps[:, UO + a:UO + b]

        def unread(S):
            return gt[0:S, :, :].rearrange("p a b -> p (a b)")[:, 0:D]

        @block.sync
        def _(sp):
            for n in range(KD):
                if n >= RW:
                    sp.wait_ge(s_p, n - RW + 1)
                src = A["ssm_out_w"][0].rearrange("(k p) n -> p k n", p=P)[:, :, P * n:P * n + P]
                sp.dma_start(wring[:, n % RW, :].rearrange("p (k n) -> p k n", n=P), src).then_inc(s_w[n % RW], 16)
            for n in range(KD // 2):
                m = KD + n
                sp.wait_ge(s_p, (m - RW + 1) if m - RW < KD else KD + 2 * (m - RW - KD + 1))
                src = A["conf_out_w"][0].rearrange("(k p) n -> p k n", p=P)[:, :, 2 * P * n:2 * P * n + 2 * P]
                sp.dma_start(wring[:, m % RW, :].rearrange("p (k n) -> p k n", n=2 * P), src).then_inc(s_w[m % RW], 16)
                if n == 1:
                    sp.dma_start(wo[:, :, :], A["w_o"][0].rearrange("(k p) n -> p k n", p=P)).then_inc(s_wo, 16)
                    sp.dma_start(x1[0:SAMP, 0, :], A["x_sample"].rearrange("b t d -> (b t) d")).then_inc(s_xr, 16)
                    sp.dma_start(x1[:, 1:NT, :],
                                 A["x_prompt"][0].rearrange("(t p) d -> p t d", p=P)).then_inc(s_xr, 16)

        @block.gpsimd
        def _(pool):
            for n in range(2 * KD):
                if n >= 4:
                    pool.wait_ge(s_gfree, n - 3)
                pool.dma_start(gt[:, n % 4, :], keep["gates"][1 - n // KD, n % KD]).then_inc(s_g[n % 4], 16)

        @block.tensor
        def _(pe):
            def sum_block(bank, j, rhs):
                for a, b in ((0, USPLIT), (USPLIT, T)):
                    last = pe.matmul(cols(bank, a, b), ones[:, :], rhs[:, a:b], start=(j == 0), stop=(j == KD - 1))
                return last

            def product(r, weights, K, act, w_sem, w_val):
                if 2 <= r < KD + 2:
                    pe.wait_ge(s_gfree, r - 1)
                elif r >= KD + 2:
                    pe.wait_ge(s_ya, r - KD - 1)
                pe.wait_ge(w_sem, w_val)
                for j in range(K):
                    for a, b in ((0, USPLIT), (USPLIT, T)):
                        last = pe.matmul(cols(pm[r % 2], a, b), weights(j), act[:, j, a:b],
                                         start=(j == 0), stop=(j == K - 1))
                last.then_inc(s_p, 1)

            for j in range(KD):
                last = sum_block(pst, j, aconv[:, j, :])
            last.then_inc(s_stat, 1)
            for n in range(KD):
                product(n, lambda j, n=n: wring[:, n % RW, P * j:P * j + P], 2 * KD, yn, s_w[n % RW], 16 * (n // RW + 1))
                if n == 0:
                    for j in range(KD):
                        pe.wait_ge(s_sq, j + 1)
                        sum_block(po, j, sq[:, j % 2, :]).then_inc(s_sqf, 1)
            pe.wait_ge(s_act, KD)
            for n in range(KD):
                m = KD + n // 2
                product(KD + n, lambda j, n=n, m=m: wring[:, m % RW, 2 * P * j + P * (n % 2):2 * P * j + P * (n % 2) + P],
                        KD, aconv, s_w[m % RW], 16 * (m // RW + 1))
            pe.wait_ge(s_wo, 16)
            pe.wait_ge(s_mg, KD)
            pe.wait_ge(s_ya, KD)
            for t, (c, S) in enumerate(OT):
                bank = (pm[0], pm[1], po)[t % 3]
                if t >= 3:
                    pe.wait_ge(s_x1, 2 * (t - 2))
                for h in range(2):
                    for j in range(KD):
                        last = pe.matmul(bank[0:S, 512 * h:512 * h + 512], mg[:, j, c:c + S],
                                         wo[:, j, 512 * h:512 * h + 512], start=(j == 0), stop=(j == KD - 1))
                    last.then_inc(s_o, 1)

        @block.scalar
        def _(act):
            act.wait_ge(s_stat, 1)
            act.activation(mean[:, :], cols(pst, 0, T), ACT.Copy, scale=1.0 / D).then_inc(s_mean, 1)
            for j in range(KD):
                act.wait_ge(s_cen, j + 1)
                if j >= 2:
                    act.wait_ge(s_sqf, j - 1)
                act.activation(sq[:, j % 2, :], aconv[:, j, :], ACT.Square).then_inc(s_sq, 1)
            act.wait_ge(s_inv, 1)
            act.activation(rs[:, :], rr[:, :], ACT.Sqrt).then_inc(s_root, 1)
            for j in range(KD):
                act.wait_ge(s_lin, j + 1)
                if j >= 2:
                    act.wait_ge(s_act, j - 1)
                act.activation(sq[:, j % 2, :], aconv[:, j, :], ACT.Tanh, scale=0.5).then_inc(s_tan, 1)
            for n in range(KD):
                act.wait_ge(s_p, KD + n + 1)
                if n >= 2:
                    act.wait_ge(s_mg, n - 1)
                act.activation(ya[:, n % 2, :], cols(pm[n % 2], 0, T), ACT.Identity, scale=0.5,
                               bias=cs[:, n, R_OB:R_OB + 1]).then_inc(s_ya, 1)
            act.wait_ge(s_ss, 1)
            for t, (c, S) in enumerate(OT):
                act.wait_ge(s_x1, 2 * t + 2)
                if t:
                    act.wait_ge(s_ssq, t)
                act.activation(unread(S), x1[0:S, t, :], ACT.Square, accum_out=ss2[0:S, t:t + 1]).then_inc(s_ssq, 1)
            act.wait_ge(s_var, 1)
            act.activation(ss2[:, 0:NT], ss2[:, 0:NT], ACT.Sqrt).then_inc(s_sd, 1)

        @block.vector
        def _(dve):
            k = Steps(dve, c_dve)

            def stt(out, in0, scalar, in1, op0=ALU.mult, op1=ALU.add):
                return dve.scalar_tensor_tensor(out=out, in0=in0, scalar=scalar, in1=in1, op0=op0, op1=op1)

            dve.memset(ss2[:, :], 1.0).then_inc(s_ss, 1)
            dve.wait_ge(s_mean, 1)
            for j in range(KD):
                dve.tensor_tensor(aconv[:, j, :], aconv[:, j, :], mean[:, :], ALU.subtract).then_inc(s_cen, 1)
            dve.wait_ge(s_sqf, KD)
            k.link(dve.tensor_scalar(rs[:, :], cols(po, 0, T), 1.0 / D, EPS, ALU.mult, ALU.add))
            dve.reciprocal(rr[:, :], rs[:, :]).then_inc(s_inv, 1)
            dve.wait_ge(s_root, 1)

            def ssm_block(n):
                dve.wait_ge(s_p, n + 1)
                dve.wait_ge(s_g[n % 4], 16 * (n // 4 + 1))
                stt(mg[:, n, :], gt[:, n % 4, :], 1.0, cols(pm[n % 2], 0, T), ALU.add, ALU.mult).then_inc(s_gfree, 1)

            for j in range(KD):
                k.link(stt(aconv[:, j, :], aconv[:, j, :], cs[:, j, R_LG:R_LG + 1], rs[:, :], ALU.mult, ALU.mult))
                dve.tensor_scalar(aconv[:, j, :], aconv[:, j, :], cs[:, j, R_LB:R_LB + 1], None,
                                  ALU.add).then_inc(s_lin, 1)
                if j:
                    dve.wait_ge(s_tan, j)
                    stt(aconv[:, j - 1, :], sq[:, (j - 1) % 2, :], 1.0, aconv[:, j - 1, :],
                        ALU.add, ALU.mult).then_inc(s_act, 1)
                if j % 2 == 1:
                    ssm_block(j // 2)
            dve.wait_ge(s_tan, KD)
            stt(aconv[:, KD - 1, :], sq[:, (KD - 1) % 2, :], 1.0, aconv[:, KD - 1, :],
                ALU.add, ALU.mult).then_inc(s_act, 1)
            for n in range(KD // 2, KD):
                ssm_block(n)
            for n in range(KD):
                dve.wait_ge(s_ya, n + 1)
                m = KD + n
                dve.wait_ge(s_g[m % 4], 16 * (m // 4 + 1))
                k.link(stt(ya[:, n % 2, :], gt[:, m % 4, :], 1.0, ya[:, n % 2, :], ALU.add, ALU.mult))
                dve.sem_inc(s_gfree, 1)
                dve.wait_ge(s_gfree, KD)
                dve.tensor_tensor(mg[:, n, :], mg[:, n, :], ya[:, n % 2, :], ALU.add).then_inc(s_mg, 1)
            dve.wait_ge(s_xr, 32)
            for t, (c, S) in enumerate(OT):
                bank = (pm[0], pm[1], po)[t % 3]
                for h in range(2):
                    dve.wait_ge(s_o, 2 * t + h + 1)
                    v = x1[0:S, t, 512 * h:512 * h + 512]
                    stt(v, bank[0:S, 512 * h:512 * h + 512], 0.5, v).then_inc(s_x1, 1)
            dve.wait_ge(s_ssq, NT)
            dve.tensor_scalar(ss2[:, 0:NT], ss2[:, 0:NT], 1.0 / D, EPS, ALU.mult, ALU.add).then_inc(s_var, 1)
            dve.wait_ge(s_sd, 1)
            dve.reciprocal(keep["rstd"][:, 0:NT], ss2[:, 0:NT]).then_inc(s_rinv, 1)


def route(nc, A, O, keep):
    x1, ident, ones, cs, pos, wgt = (keep[n] for n in ("x1", "ident", "ones", "cs", "pos", "wgt"))
    with ExitStack() as ctx:
        def sb(name, shape, dt=F32):
            return ctx.enter_context(nc.sbuf_tensor(name, shape, dt))

        sem = ctx.enter_context(semaphores(nc))

        NL = NGR + NE
        xs = sb("xs", [P, 2, D])
        xT = sb("xT", [P, 2, KD, P])
        wr = sb("wr", [P, KD, NL])
        rb = sb("rb", [P, NL])
        lg = sb("lg", [P, NT, NL])
        gm = sb("gm", [P, NT])
        sg = sb("sg", [P, NT, NGR])
        eqg = sb("eqg", [P, NT, NGR])
        og = sb("og", [P, NT, NGR])
        gp = sb("gp", [P, NT])
        ei = sb("ei", [P, NT, EPG])
        et = sb("et", [P, NT, EPG])
        m12 = sb("m12", [P, 2, NT])
        sc = sb("sc", [P, NT, EPG])
        ok = sb("ok", [P, 2, NT, EPG])
        rank = sb("rank", [P, EPG])
        valid = sb("valid", [P, NT])
        OH = sb("OH", [P, 2, NT, NE])
        pre = sb("pre", [P, 2 * NT, NE])
        run = sb("run", [P, 2 * NT + 1, NE])
        ntl = sb("ntl", [P, NE])
        tend = sb("tend", [P, NE])
        base = sb("base", [P, NE])
        zer = sb("zer", [P, NE])
        posf = sb("posf", [P, 2 * NT])
        ti = sb("ti", [1, NTILE])
        cmp = sb("cmp", [1, NTILE, NE])
        exf = sb("exf", [1, NTILE])
        SU = sb("SU", [P, P])
        tokid = sb("tokid", [P, NT], U32)
        zu = sb("zu", [NTILE, P], U32)
        srow = sb("srow", [NTILE, P], U32)
        srowf = sb("srowf", [NTILE, P])
        px = [ctx.enter_context(nc.psum_tensor(f"rx{i}", [P, 512], F32)) for i in range(2)]
        pl, pc, pt = (ctx.enter_context(nc.psum_tensor(n, [P, 512], F32)) for n in ("rl", "rc", "rt"))
        pc2 = ctx.enter_context(nc.psum_tensor("rc2", [P, 512], F32))
        s_wr, s_rb, s_cst, s_id, s_xs, s_t, s_tf, s_l, s_lg, s_e, s_x, s_oh, s_cnt, s_pos, s_z, s_sct, s_row, s_rowf, \
            s_rt, s_done, s_tok = map(sem, (
                "r_wr", "r_rb", "r_cst", "r_id", "r_xs", "r_t", "r_tf", "r_l", "r_lg", "r_e", "r_x", "r_oh",
                "r_cnt", "r_pos", "r_z", "r_sct", "r_row", "r_rowf", "r_rt", "r_done", "r_tok"))
        s_xst = [sem(f"r_xst{b}") for b in range(2)]
        c_dve, c_pool = sem("r_dve"), sem("r_pool")
        block = ctx.enter_context(nc.Block())

        @block.sync
        def _(sp):
            for a, b, w, bias in ((0, NGR, A["router_group_w"], A["router_group_b"]),
                                  (NGR, NL, A["router_expert_w"], A["router_expert_b"])):
                sp.dma_start(wr[:, :, a:b], w[0].rearrange("(k p) n -> p k n", p=P)).then_inc(s_wr, 16)
                sp.dma_start(rb[:, a:b], bias[0].partition_broadcast(P)).then_inc(s_rb, 16)
            for t, (c, S) in enumerate(OT):
                sp.wait_ge(s_xs, t + 1)
                sp.dma_start(keep["xs"][ROW[t]:ROW[t] + S, :], xs[0:S, t % 2, :]).then_inc(s_xst[t % 2], 16)
            for b in range(2):
                sp.wait_ge(s_xst[b], 16 * ((NT + 1 - b) // 2))

        @block.gpsimd
        def _(pool):
            k = Steps(pool, c_pool)
            pool.iota(rank[:, :], [[-1, EPG]], base=EPG, channel_multiplier=0, allow_small_or_imprecise_dtypes=True).then_inc(s_cst, 1)
            pool.iota(ti[:, :], [[1, NTILE]], base=0, channel_multiplier=0, allow_small_or_imprecise_dtypes=True).then_inc(s_cst, 1)
            pool.iota(tokid[:, 0:1], [[0, 1]], base=0, channel_multiplier=1).then_inc(s_cst, 1)
            pool.iota(tokid[:, 1:NT], [[P, NT - 1]], base=ROW[1], channel_multiplier=1).then_inc(s_cst, 1)
            k.link(pool.memset(valid[:, :], 1.0))
            pool.affine_select(out=valid[:, 0:1], in_=valid[:, 0:1], compare_op=ALU.is_ge, fill=0.0,
                               base=SAMP - 1, pattern=[[0, 1]], channel_multiplier=-1).then_inc(s_cst, 1)
            k.link(pool.memset(SU[:, :], 1.0))
            pool.affine_select(out=SU[:, :], in_=SU[:, :], compare_op=ALU.is_gt, fill=0.0, base=0,
                               pattern=[[1, P]], channel_multiplier=-1).then_inc(s_cst, 1)
            pool.memset(lg[:, 0, :], 0.0).then_inc(s_cst, 1)
            pool.memset(zer[:, :], 0.0).then_inc(s_cst, 1)
            k.link(pool.memset(zu[:, :], 0))
            pool.dma_start(keep["slots"].rearrange("(i p) o -> i (p o)", p=P), zu[:, :]).then_inc(s_z, 16)
            pool.wait_ge(s_z, 16)
            pool.wait_ge(s_cst, 8)
            pool.wait_ge(s_pos, 1)
            for q in range(2):
                for t, (c, S) in enumerate(OT):
                    pool.indirect_dma_start(
                        out=keep["slots"], out_offset=bass.IndirectOffsetOnAxis(ap=pos[0:S, NT * q + t:NT * q + t + 1], axis=0),
                        in_=tokid[0:S, t:t + 1], in_offset=None).then_inc(s_sct, 16)
            pool.wait_ge(s_sct, 16 * 2 * NT)
            pool.dma_start(srow[:, :], keep["slots"].rearrange("(i p) o -> i (p o)", p=P)).then_inc(s_row, 16)

        @block.tensor
        def _(pe):
            for t, (c, S) in enumerate(OT):
                pe.wait_ge(s_xs, t + 1)
                for h in range(2):
                    n = 2 * t + h
                    if n >= 2:
                        pe.wait_ge(s_tf, n - 1)
                    for q in range(4):
                        last = pe.transpose(px[n % 2][:, P * q:P * q + S], xs[0:S, t % 2, P * (4 * h + q):P * (4 * h + q) + P],
                                            ident[0:S, 0:S])
                    last.then_inc(s_t, 1)
                pe.wait_ge(s_tf, 2 * t + 2)
                pe.wait_ge(s_wr, 32)
                for j in range(KD):
                    last = pe.matmul(pl[0:S, NL * t:NL * t + NL], xT[:, t % 2, j, 0:S], wr[:, j, :],
                                     start=(j == 0), stop=(j == KD - 1))
                last.then_inc(s_l, 1)
            pe.wait_ge(s_oh, 1)
            pe.wait_ge(s_cst, 8)
            ohv = OH[:, :, :, :].rearrange("p a t e -> p (a t e)")
            pe.matmul(pc[:, 0:2 * NT * NE], SU[:, :], ohv, start=True, stop=True)
            pe.matmul(pc2[:, 0:2 * NT * NE], ones[:, :], ohv, start=True, stop=True).then_inc(s_cnt, 1)
            pe.wait_ge(s_rowf, 1)
            pe.transpose(pt[:, 0:NTILE], srowf[:, :], ident[0:NTILE, 0:NTILE]).then_inc(s_rt, 1)

        @block.scalar
        def _(act):
            act.wait_ge(s_e, 1)
            act.activation(sg[:, :, :], sg[:, :, :], ACT.Exp).then_inc(s_x, 1)
            act.activation(gp[:, :], gp[:, :], ACT.Exp).then_inc(s_x, 1)

        @block.vector
        def _(dve):
            k = Steps(dve, c_dve)

            def tt(out, a, b, op):
                k.link(dve.tensor_tensor(out, a, b, op))

            def stt(out, in0, scalar, in1, op0=ALU.mult, op1=ALU.add):
                k.link(dve.scalar_tensor_tensor(out=out, in0=in0, scalar=scalar, in1=in1, op0=op0, op1=op1))

            def red(out, in_, op):
                k.link(dve.tensor_reduce(out, in_, AX_X, op))

            def normed(t):
                S = OT[t][1]
                if t >= 2:
                    dve.wait_ge(s_xst[t % 2], 16 * (t // 2))
                    dve.wait_ge(s_t, 2 * t - 2)
                dve.tensor_scalar(xs[0:S, t % 2, :], x1[0:S, t, :], keep["rstd"][0:S, t:t + 1], None,
                                  ALU.mult).then_inc(s_xs, 1)

            normed(0)
            for t, (c, S) in enumerate(OT):
                if t + 1 < NT:
                    normed(t + 1)
                for h in range(2):
                    n = 2 * t + h
                    dve.wait_ge(s_t, n + 1)
                    if t >= 2:
                        dve.wait_ge(s_l, t - 1)
                    w = cs[:, 4 * h:4 * h + 4, R_NFFN].unsqueeze(2).broadcast_to([P, 4, S])
                    dve.tensor_tensor(xT[:, t % 2, 4 * h:4 * h + 4, 0:S],
                                      px[n % 2][:, :].rearrange("p (q s) -> p q s", q=4)[:, :, 0:S], w,
                                      ALU.mult).then_inc(s_tf, 1)
            dve.wait_ge(s_rb, 32)
            dve.wait_ge(s_l, NT)
            dve.wait_ge(s_cst, 8)
            for t, (c, S) in enumerate(OT):
                tt(lg[0:S, t, :], pl[0:S, NL * t:NL * t + NL], rb[0:S, :], ALU.add)

            def bc(ap, n):
                return ap.unsqueeze(2).broadcast_to([P, NT, n])

            def first_of(onehot, equal, n):
                r = rank[:, EPG - n:EPG].unsqueeze(1).broadcast_to([P, NT, n])
                tt(equal, equal, r, ALU.mult)
                red(gm[:, :], equal, ALU.max)
                tt(onehot, equal, bc(gm[:, :], n), ALU.is_equal)

            g = lg[:, :, 0:NGR]
            red(gm[:, :], g, ALU.max)
            tt(sg[:, :, :], g, bc(gm[:, :], NGR), ALU.subtract)
            tt(eqg[:, :, :], g, bc(gm[:, :], NGR), ALU.is_equal)
            first_of(og[:, :, :], eqg[:, :, :], NGR)
            for q in range(NGR):
                e = lg[:, :, NGR + EPG * q:NGR + EPG * q + EPG]
                if q == 0:
                    tt(ei[:, :, :], e, bc(og[:, :, q], EPG), ALU.mult)
                else:
                    tt(et[:, :, :], e, bc(og[:, :, q], EPG), ALU.mult)
                    tt(ei[:, :, :], ei[:, :, :], et[:, :, :], ALU.add)
            red(m12[:, 0, :], ei[:, :, :], ALU.max)
            tt(sc[:, :, :], ei[:, :, :], bc(m12[:, 0, :], EPG), ALU.is_equal)
            first_of(ok[:, 0], sc[:, :, :], EPG)
            stt(ei[:, :, :], ok[:, 0], -BIG, ei[:, :, :])
            red(m12[:, 1, :], ei[:, :, :], ALU.max)
            tt(sc[:, :, :], ei[:, :, :], bc(m12[:, 1, :], EPG), ALU.is_equal)
            first_of(ok[:, 1], sc[:, :, :], EPG)
            dve.tensor_tensor(gp[:, :], m12[:, 1, :], m12[:, 0, :], ALU.subtract).then_inc(s_e, 1)
            for q in range(2):
                for b in range(NGR):
                    tt(OH[:, q, :, EPG * b:EPG * b + EPG], ok[:, q], bc(og[:, :, b], EPG), ALU.mult)
                tt(OH[:, q], OH[:, q], bc(valid[:, :], NE), ALU.mult)
            dve.sem_inc(s_oh, 1)
            dve.wait_ge(s_x, 2)
            red(gm[:, :], sg[:, :, :], ALU.add)
            stt(gm[:, :], gp[:, :], 1.0, gm[:, :], ALU.add, ALU.mult)
            k.link(dve.reciprocal(wgt[:, 0, :], gm[:, :]))
            k.link(dve.tensor_scalar(wgt[:, 0, :], wgt[:, 0, :], 0.5, None, ALU.mult))
            tt(wgt[:, 1, :], wgt[:, 0, :], gp[:, :], ALU.mult)
            dve.wait_ge(s_cnt, 1)
            k.link(dve.memset(run[:, 0, :], 0.0))
            for n in range(2 * NT):
                tt(run[:, n + 1, :], run[:, n, :], pc2[:, NE * n:NE * n + NE], ALU.add)
            cnt = run[:, 2 * NT, :]
            k.link(dve.tensor_scalar(ntl[:, :], cnt, 0.0, None, ALU.is_gt))
            for n in range(1, MAXT):
                stt(ntl[:, :], cnt, float(SLOT * n), ntl[:, :], ALU.is_gt, ALU.add)
            k.link(dve.tensor_tensor_scan(tend[:, :], ntl[:, :], zer[:, :], 0.0, ALU.add, ALU.add))
            tt(base[:, :], tend[:, :], ntl[:, :], ALU.subtract)
            k.link(dve.tensor_scalar(base[:, :], base[:, :], float(SLOT), None, ALU.mult))
            tt(pre[:, :, :], run[:, 0:2 * NT, :], pc[:, 0:2 * NT * NE].rearrange("p (n e) -> p n e", e=NE), ALU.add)
            tt(pre[:, :, :], pre[:, :, :], base[:, :].unsqueeze(1).broadcast_to([P, 2 * NT, NE]), ALU.add)
            tt(pre[:, :, :], pre[:, :, :], OH[:, :, :, :].rearrange("p a t e -> p (a t) e"), ALU.mult)
            red(posf[:, :], pre[:, :, :], ALU.add)
            dve.tensor_copy(pos[:, :], posf[:, :]).then_inc(s_pos, 1)
            tt(cmp[:, :, :], ti[:, :].unsqueeze(2).broadcast_to([1, NTILE, NE]),
               tend[0:1, :].unsqueeze(1).broadcast_to([1, NTILE, NE]), ALU.is_ge)
            red(exf[:, :], cmp[:, :, :], ALU.add)
            k.link(dve.tensor_scalar(exf[:, :], exf[:, :], float(NE - 1), None, ALU.min))
            dve.tensor_copy(keep["expert"][:, :], exf[:, :]).then_inc(s_done, 1)
            dve.wait_ge(s_row, 16)
            dve.tensor_copy(srowf[:, :], srow[:, :]).then_inc(s_rowf, 1)
            dve.wait_ge(s_rt, 1)
            dve.tensor_copy(keep["tok"][:, :], pt[:, 0:NTILE]).then_inc(s_tok, 1)


def experts(nc, A, O, keep):
    ident, cs = keep["ident"], keep["cs"]
    with ExitStack() as ctx:
        def sb(name, shape, dt=F32):
            return ctx.enter_context(nc.sbuf_tensor(name, shape, dt))

        sem = ctx.enter_context(semaphores(nc))

        W13 = sb("W13", [P, 2, KD, 2 * DE])
        W2 = sb("W2", [P, 2, DE // P, D])
        xg = sb("xg", [P, 2, D])
        xgT = sb("xgT", [P, 2, KD, P])
        idx = sb("idx", [P, 2], U32)
        thh = sb("thh", [P, 2, DE])
        ac = sb("ac", [P, 2, DE])
        acT = sb("acT", [P, 2, DE])
        yo = sb("yo", [P, 2, D])
        px = [ctx.enter_context(nc.psum_tensor(f"ex{i}", [P, 512], F32)) for i in range(2)]
        ph = [ctx.enter_context(nc.psum_tensor(f"eh{i}", [P, 512], F32)) for i in range(2)]
        pa = ctx.enter_context(nc.psum_tensor("ea", [P, 512], F32))
        py = ctx.enter_context(nc.psum_tensor("ey", [P, 1024], F32))
        s_w13 = [sem(f"e_w13{b}") for b in range(2)]
        s_w2 = [sem(f"e_w2{b}") for b in range(2)]
        s_xg = [sem(f"e_xg{b}") for b in range(2)]
        s_yst = [sem(f"e_yst{b}") for b in range(2)]
        s_idx, s_t, s_xT, s_h, s_th, s_s, s_act, s_at, s_acT, s_y, s_yev = map(sem, (
            "e_idx", "e_t", "e_xT", "e_h", "e_th", "e_s", "e_act", "e_at", "e_acT", "e_y", "e_yev"))
        s_settled = sem("e_settled")
        block = ctx.enter_context(nc.Block())
        started = ((s_t, 2), (s_xT, 2), (s_h, 2), (s_th, 2), (s_act, 2), (s_at, 2), (s_acT, 2), (s_y, 2), (s_yev, 2),
                   (s_yst[0], 1), (s_yst[1], 1))

        @block.sync
        def _(sp):
            with sp.Fori(0, NTILE // 2) as ii:
                for b in range(2):
                    i = 2 * ii + b
                    e = sp.value_load(keep["expert"][0:1, bass.ds(i, 1)], min_val=0, max_val=NE - 1)
                    sp.wait_ge(s_h, i + 1)
                    for a, w in ((0, A["exp_w1"]), (1, A["exp_w3"])):
                        sp.dma_start(W13[:, b, :, DE * a:DE * a + DE],
                                     w[0][e].rearrange("(k p) f -> p k f", p=P)).then_inc(s_w13[b], 16)
                    sp.wait_ge(s_y, i + 1)
                    sp.dma_start(W2[:, b], A["exp_w2"][0][e].rearrange("(k p) d -> p k d", p=P)).then_inc(s_w2[b], 16)

        @block.gpsimd
        def _(pool):
            for s, n in started:
                for _ in range(n):
                    pool.sem_inc(s, 1)
            with pool.Fori(0, NTILE // 2) as ii:
                for b in range(2):
                    i = 2 * ii + b
                    pool.wait_ge(s_t, i + 1)
                    pool.sem_inc(s_settled, 1)
                    pool.tensor_copy(idx[:, b:b + 1], keep["tok"][:, bass.ds(i, 1)]).then_inc(s_idx, 1)
                    pool.wait_ge(s_idx, i + 1)
                    pool.sem_inc(s_settled, 1)
                    pool.indirect_dma_start(out=xg[:, b, :], out_offset=None, in_=keep["xs"],
                                            in_offset=bass.IndirectOffsetOnAxis(ap=idx[:, b:b + 1], axis=0))\
                        .then_inc(s_xg[b], 16)

        def half(i, b):
            return 16 * ((i - b) // 2 + 1) if isinstance(i, int) else 8 * (i - b) + 16

        @block.tensor
        def _(pe):
            def turn(i, b):
                pe.wait_ge(s_xg[b], half(i, b))
                pe.wait_ge(s_xT, i + 2)
                for h in range(2):
                    for q in range(4):
                        last = pe.transpose(px[h][:, P * q:P * q + P], xg[:, b, P * (4 * h + q):P * (4 * h + q) + P],
                                            ident[:, :])
                last.then_inc(s_t, 1)

            def up(i, b):
                pe.wait_ge(s_xT, i + 3)
                pe.wait_ge(s_act, i + 1)
                pe.wait_ge(s_w13[b], 2 * half(i, b))
                for j in range(KD):
                    last = pe.matmul(ph[b][:, :], xgT[:, b, j, :], W13[:, b, j, :], start=(j == 0), stop=(j == KD - 1))
                last.then_inc(s_h, 1)

            def turn_act(i, b):
                pe.wait_ge(s_act, i + 3)
                pe.wait_ge(s_acT, i + 2)
                for q in range(2):
                    last = pe.transpose(pa[:, P * q:P * q + P], ac[:, b, P * q:P * q + P], ident[:, :])
                last.then_inc(s_at, 1)

            def down(i, b):
                pe.wait_ge(s_acT, i + 3)
                pe.wait_ge(s_yev, i + 2)
                pe.wait_ge(s_w2[b], half(i, b))
                for h in range(2):
                    for q in range(2):
                        last = pe.matmul(py[:, 512 * h:512 * h + 512], acT[:, b, P * q:P * q + P],
                                         W2[:, b, q, 512 * h:512 * h + 512], start=(q == 0), stop=(q == 1))
                last.then_inc(s_y, 1)

            turn(0, 0)
            up(0, 0)
            turn(1, 1)
            turn_act(0, 0)
            with pe.Fori(0, NTILE // 2 - 1) as ii:
                for o in (1, 2):
                    i = 2 * ii + o
                    up(i, o % 2)
                    turn(i + 1, 1 - o % 2)
                    turn_act(i, o % 2)
                    down(i - 1, 1 - o % 2)
            up(NTILE - 1, 1)
            turn_act(NTILE - 1, 1)
            down(NTILE - 2, 0)
            down(NTILE - 1, 1)

        @block.scalar
        def _(act):
            def tanh(i, b):
                act.wait_ge(s_h, i + 3)
                act.wait_ge(s_act, i + 1)
                act.activation(thh[:, b, :], ph[b][:, 0:DE], ACT.Tanh, scale=0.5).then_inc(s_th, 1)

            def turned(i, b):
                act.wait_ge(s_at, i + 3)
                act.wait_ge(s_y, i + 1)
                act.activation(acT[:, b, :], pa[:, 0:DE], ACT.Copy).then_inc(s_acT, 1)

            def store(i, b):
                act.wait_ge(s_y, i + 3)
                act.wait_ge(s_yst[b], half(i, b) - 15)
                act.activation(yo[:, b, :], py[:, :], ACT.Copy).then_inc(s_yev, 1)
                act.wait_ge(s_yev, i + 3)
                act.dma_start(keep["ysc"].rearrange("(i p) d -> i p d", p=P)[i], yo[:, b, :]).then_inc(s_yst[b], 16)

            tanh(0, 0)
            turned(0, 0)
            with act.Fori(0, NTILE // 2 - 1) as ii:
                for o in (1, 2):
                    i = 2 * ii + o
                    tanh(i, o % 2)
                    turned(i, o % 2)
                    store(i - 1, 1 - o % 2)
            tanh(NTILE - 1, 1)
            turned(NTILE - 1, 1)
            store(NTILE - 2, 0)
            store(NTILE - 1, 1)
            for b in range(2):
                act.wait_ge(s_yst[b], 16 * (NTILE // 2) + 1)

        @block.vector
        def _(dve):
            def rows_T(i, b):
                dve.wait_ge(s_t, i + 3)
                dve.wait_ge(s_h, i + 1)
                for h in range(2):
                    w = cs[:, 4 * h:4 * h + 4, R_NFFN].unsqueeze(2).broadcast_to([P, 4, P])
                    last = dve.tensor_tensor(xgT[:, b, 4 * h:4 * h + 4, :],
                                             px[h][:, :].rearrange("p (q s) -> p q s", q=4), w, ALU.mult)
                last.then_inc(s_xT, 1)

            def gated(i, b):
                dve.wait_ge(s_th, i + 3)
                dve.wait_ge(s_at, i + 1)
                dve.scalar_tensor_tensor(out=ac[:, b, :], in0=thh[:, b, :], scalar=1.0, in1=ph[b][:, 0:DE],
                                         op0=ALU.add, op1=ALU.mult).then_inc(s_s, 1)
                dve.wait_ge(s_s, i + 1)
                dve.tensor_tensor(ac[:, b, :], ac[:, b, :], ph[b][:, DE:2 * DE], ALU.mult).then_inc(s_act, 1)

            rows_T(0, 0)
            with dve.Fori(0, NTILE // 2 - 1) as ii:
                for b in range(2):
                    gated(2 * ii + b, b)
                    rows_T(2 * ii + b + 1, 1 - b)
            gated(NTILE - 2, 0)
            rows_T(NTILE - 1, 1)
            gated(NTILE - 1, 1)


def finish(nc, A, O, keep):
    x1, pos, wgt = keep["x1"], keep["pos"], keep["wgt"]
    with ExitStack() as ctx:
        def sb(name, shape, dt=F32):
            return ctx.enter_context(nc.sbuf_tensor(name, shape, dt))

        sem = ctx.enter_context(semaphores(nc))

        ye = sb("ye", [P, 2 * NT, D])
        nf = sb("nf", [P, D])
        junk = sb("junk", [P, D])
        ssf = sb("ssf", [P, NT])
        rsf = sb("rsf", [P, NT])
        s_nf, s_x2, s_sum, s_var, s_sd, s_out, s_st = map(sem, ("f_nf", "f_x2", "f_sum", "f_var", "f_sd", "f_out", "f_st"))
        s_ye = [sem(f"f_ye{n}") for n in range(2 * NT)]
        c_dve = sem("f_dve")
        block = ctx.enter_context(nc.Block())

        @block.sync
        def _(sp):
            sp.dma_start(nf[:, :], A["norm_final_w"].partition_broadcast(P)).then_inc(s_nf, 16)
            for t, (c, S) in enumerate(OT):
                sp.wait_ge(s_out, t + 1)
                dst = (O["y_sample"].rearrange("b t d -> (b t) d") if t == 0
                       else O["y_prompt"][0][P * (t - 1):P * t, :])
                sp.dma_start(dst, x1[0:S, t, :]).then_inc(s_st, 16)
            sp.wait_ge(s_st, 16 * NT)

        @block.gpsimd
        def _(pool):
            for t, (c, S) in enumerate(OT):
                for q in range(2):
                    n = NT * q + t
                    pool.indirect_dma_start(out=ye[0:S, n, :], out_offset=None, in_=keep["ysc"],
                                            in_offset=bass.IndirectOffsetOnAxis(ap=pos[0:S, n:n + 1], axis=0))\
                        .then_inc(s_ye[n], 16)

        @block.scalar
        def _(act):
            for t, (c, S) in enumerate(OT):
                act.wait_ge(s_x2, t + 1)
                if t:
                    act.wait_ge(s_sum, t)
                act.activation(junk[0:S, :], x1[0:S, t, :], ACT.Square, accum_out=ssf[0:S, t:t + 1]).then_inc(s_sum, 1)
            for t, (c, S) in enumerate(OT):
                act.wait_ge(s_var, t + 1)
                act.activation(ssf[0:S, t:t + 1], ssf[0:S, t:t + 1], ACT.Sqrt).then_inc(s_sd, 1)

        @block.vector
        def _(dve):
            k = Steps(dve, c_dve)
            for t, (c, S) in enumerate(OT):
                for q in range(2):
                    dve.wait_ge(s_ye[NT * q + t], 16)
                    ins = dve.scalar_tensor_tensor(out=x1[0:S, t, :], in0=ye[0:S, NT * q + t, :],
                                                   scalar=wgt[0:S, q, t:t + 1], in1=x1[0:S, t, :],
                                                   op0=ALU.mult, op1=ALU.add)
                    if q:
                        ins.then_inc(s_x2, 1)
                    else:
                        k.link(ins)
            for t, (c, S) in enumerate(OT):
                dve.wait_ge(s_sum, t + 1)
                dve.tensor_scalar(ssf[0:S, t:t + 1], ssf[0:S, t:t + 1], 1.0 / D, EPS, ALU.mult, ALU.add).then_inc(s_var, 1)
            dve.wait_ge(s_nf, 16)
            for t, (c, S) in enumerate(OT):
                dve.wait_ge(s_sd, t + 1)
                k.link(dve.reciprocal(rsf[0:S, t:t + 1], ssf[0:S, t:t + 1]))
                dve.scalar_tensor_tensor(out=x1[0:S, t, :], in0=x1[0:S, t, :], scalar=rsf[0:S, t:t + 1],
                                         in1=nf[0:S, :], op0=ALU.mult, op1=ALU.mult).then_inc(s_out, 1)


_OUTS = [("y_prompt", (1, SEQ, D)), ("y_sample", (NSAMP, TSAMP, D)), ("new_conf_prompt", (1, 1, CK - 1, D)),
         ("new_sconv_prompt", (1, 1, SK - 1, 4 * D)), ("new_ssm_prompt", (1, 1, NH, HD, N)),
         ("new_conf_sample", (1, NSAMP, CK - 1, D)), ("new_sconv_sample", (1, NSAMP, SK - 1, 4 * D)),
         ("new_ssm_sample", (1, NSAMP, NH, HD, N))]


def program(nc, A, O):
    with ExitStack() as ctx:
        def sb(name, shape, dt=F32):
            return ctx.enter_context(nc.sbuf_tensor(name, shape, dt))

        keep = {"aconv": sb("aconv", [P, KD, T]), "yn": sb("yn", [P, 2 * KD, T]), "cs": sb("cs", [P, KD, NR]),
                "ident": sb("ident", [P, P]), "ones": sb("ones", [P, P]),
                "gates": nc.dram_tensor("gates", (2, KD, P, T), F32, kind="Internal").ap(),
                "xs": nc.dram_tensor("xs_rows", (SAMP + SEQ, D), F32, kind="Internal").ap(),
                "slots": nc.dram_tensor("slots", (NTILE * SLOT, 1), U32, kind="Internal").ap(),
                "ysc": nc.dram_tensor("slot_rows", (NTILE * SLOT, D), F32, kind="Internal").ap()}
        trunk(nc, A, O, keep)
        keep["x1"], keep["rstd"] = sb("x1", [P, NT, D]), sb("rstd", [P, 8])
        mixer(nc, A, O, keep)
        keep["pos"], keep["wgt"] = sb("pos", [P, 2 * NT], U32), sb("wgt", [P, 2, NT])
        keep["expert"], keep["tok"] = sb("expert", [1, NTILE], U32), sb("tok", [P, NTILE], U32)
        route(nc, A, O, keep)
        experts(nc, A, O, keep)
        finish(nc, A, O, keep)


def kernel(**inputs):
    import numpy as _np
    import concourse.bacc as _bacc
    from concourse import mybir as _mybir
    from concourse.bass_utils import run_bass_kernel_spmd as _run

    nc = _bacc.Bacc("TRN2", target_bir_lowering=False, num_devices=1)
    arrays, A, O = {}, {}, {}
    for name, value in inputs.items():
        a = _np.ascontiguousarray(value)
        arrays[f"in_{name}"] = a
        A[name] = nc.dram_tensor(f"in_{name}", a.shape, _mybir.dt.float32, kind="ExternalInput").ap()
    for name, shape in _OUTS:
        O[name] = nc.dram_tensor(f"out_{name}", shape, _mybir.dt.float32, kind="ExternalOutput").ap()
    program(nc, A, O)
    r = _run(nc, [arrays], core_ids=[0])
    return tuple(r.results[0][f"out_{name}"] for name, _ in _OUTS)
```

```python
from contextlib import ExitStack, contextmanager

import concourse.bass as bass
from concourse import mybir

F32 = mybir.dt.float32
F32R = mybir.dt.float32r
U32 = mybir.dt.uint32
ALU = mybir.AluOpType
ACT = mybir.ActivationFunctionType
AX_X = mybir.AxisListType.X

P = 128
D = 1024
KD = D // P
NSAMP, TSAMP = 8, 4
META, SEQ = 16, 512
SAMP = NSAMP * TSAMP
PROMPT = META + SEQ
T = SAMP + PROMPT
CK, SK = 31, 4
G = 8
HG = 4
NH = G * HG
HD = 64
N = 128
DI = 2 * D
EPS = 1e-6
CHUNK = 128
CHUNKS = [(0, SAMP), (SAMP, META)] + [(SAMP + META + CHUNK * i, CHUNK) for i in range(SEQ // CHUNK)]
ORDER = [1, 2, 3, 4, 5, 0]
TILES = [(0, SAMP + META)] + CHUNKS[2:]
W_GV, W_GG, W_Z, W_X, W_B, W_C = 0, D, 2 * D, 4 * D, 6 * D, 7 * D
W_DT, W_GATE = 8 * D, 8 * D + NH
R_CW, R_CB, R_LG, R_LB, R_OB, R_NMIX = 0, CK, CK + 1, CK + 2, CK + 3, CK + 4
R_X, R_BC = CK + 5, CK + 15
R_NW = CK + 25
R_GB = CK + 27
R_DS = CK + 29
NR = CK + 31
UO = 208
USPLIT = 512 - UO
RING = 2
POOL_LOW = 6
DVE_STEPS = 59
N_CROW = 18
U_TILES = 14
BLOCKS = 10
U_OF = [0, 1, 2, 3, 4, 5, 8, 9, 10, 11]


class Steps:

    def __init__(self, eng, sem):
        self.eng, self.sem, self.base, self.n = eng, sem, 0, 0

    def link(self, ins):
        ins.then_inc(self.sem, 1)
        self.n += 1
        self.eng.wait_ge(self.sem, self.base + self.n)

    def enter(self, g, per):
        self.start, self.per = self.n, per
        self.base, self.n = g * per + self.n, 0

    def leave(self, trips):
        assert self.n == self.per, self.n
        self.n, self.base = self.start + trips * self.per, 0


@contextmanager
def semaphores(nc):
    held = []

    def sem(name):
        held.append(nc.alloc_semaphore(name=name))
        return held[-1]

    yield sem
    nc.clear_and_free_semaphores(held)
    nc.all_engine_barrier()


def trunk(nc, A, O, keep):
    yn, cs = keep["yn"], keep["cs"]
    ident, ones = keep["ident"], keep["ones"]
    w_in = A["w_in"][0]
    with ExitStack() as ctx:
        def sb(name, shape, dt=F32):
            return ctx.enter_context(nc.sbuf_tensor(name, shape, dt))

        sem = ctx.enter_context(semaphores(nc))

        xh, xl = sb("xh", [P, KD, T], F32R), sb("xl", [P, KD, T], F32R)
        wh, wl = sb("wh", [P, RING, KD, P], F32R), sb("wl", [P, RING, KD, P], F32R)
        wdh, wdl = sb("wdh", [P, KD, NH], F32R), sb("wdl", [P, KD, NH], F32R)
        ring = sb("ring", [P, RING, KD, P])
        aout = sb("aout", [P, T])
        eps = sb("eps", [P, 1])
        xin = keep["x1"][:, :, :]
        scr = xin.rearrange("p t d -> p (t d)")
        h0 = scr[:, 0:2048].rearrange("p (i b n) -> p i b n", i=2, b=NSAMP)
        h0T = scr[:, 2048:4096].rearrange("p (i b m) -> p i b m", i=2, b=NSAMP)
        Bblk = scr[0:SAMP, 4096:5120].rearrange("p (b n) -> p b n", b=NSAMP)
        stage = yn[:, :, :].rearrange("p a b -> p (a b)")
        crow = stage[0:R_DS, 0:D]
        confrow = stage[0:120, D:3 * D].rearrange("p (t d) -> p t d", t=2)
        ssmrow = stage[0:NSAMP * (SK - 1), 3 * D:7 * D]
        wdt = stage[:, 7 * D:7 * D + 256].rearrange("p (k m) -> p k m", k=KD)
        stC = sb("stC", [P, KD, NSAMP * (CK - 1)])
        stS = sb("stS", [P, 32, NSAMP * (SK - 1)])
        gc = sb("gc", [P, NR])
        U = sb("U", [P, P])
        SL = sb("SL", [P, P])
        Ub = sb("Ub", [SAMP, SAMP])
        SLb = sb("SLb", [SAMP, SAMP])
        Bm = sb("Bm", [SAMP, NSAMP])
        dtb = sb("dtb", [P, NH])
        expA = sb("expA", [P, NH])
        dtt = sb("dtt", [P, 6, NH])
        tmp1 = sb("tmp1", [P, 6, NH])
        tmp2 = sb("tmp2", [P, 6, NH])
        aa = sb("aa", [P, 6, NH])
        tail = sb("tail", [P, 6, NH])
        Dl = sb("Dl", [P, 6, NH])
        ss = sb("ss", [P, 8])
        raw_p = sb("raw_p", [P, 4, SK - 1 + PROMPT])
        raw_s = sb("raw_s", [P, 4, NSAMP, SK - 1 + TSAMP])
        cv = sb("cv", [P, 4, T])
        th = sb("th", [P, 2, T])
        a_p = sb("a_p", [P, CK - 1 + PROMPT])
        a_s = sb("a_s", [P, NSAMP, CK - 1 + TSAMP])
        cacc = sb("cacc", [P, T])
        ybuf = sb("ybuf", [P, 2, T])
        zc = sb("zc", [P, 2, T])
        Ed = sb("Ed", [P, 2, T])
        ab = sb("ab", [P, 6, HG * HD])
        ds0 = sb("ds0", [1, NH])
        dsrow = cv[0:1, :, :].rearrange("p q t -> p (q t)")[:, 0:DI]
        gbuf = sb("gbuf", [P, T])
        aU = sb("aU", [P, HG, P])
        Lx = sb("Lx", [P, HG, P])
        Tt = sb("Tt", [P, 4, P])
        cbm = sb("cbm", [P, P])
        xdt = sb("xdt", [P, HG, HD])
        xtl = sb("xtl", [P, HG, HD])
        hT = sb("hT", [P, HG, HD])
        hTd = sb("hTd", [P, HG, HD])
        yi = sb("yi", [P, 2, P])
        pk = sb("pk", [P, 4, 27])
        pk_rows = sb("pk_rows", [27, 4, P])
        pa = sb("pa", [P, 62])
        pa_rows = sb("pa_rows", [62, P])
        hout = sb("hout", [P, 2, P])
        xt = (Tt, Lx)
        pu = [ctx.enter_context(nc.psum_tensor(f"pu{i}", [P, 1024], F32)) for i in range(2)]
        pS, pT, pC, pY = (ctx.enter_context(nc.psum_tensor(n, [P, 512], F32)) for n in ("pS", "pT", "pC", "pY"))

        s_x, s_meta, s_crow, s_conf, s_ssm, s_wdt, s_dtb = map(
            sem, ("s_x", "s_meta", "s_crow", "s_conf", "s_ssm", "s_wdt", "s_dtb"))
        s_w = [sem(f"s_w{i}") for i in range(RING)]
        s_xt, s_xh, s_xl, s_wdh, s_wdl, s_wh, s_wlp, s_wld, s_ast = map(
            sem, ("s_xt", "s_xh", "s_xl", "s_wdh", "s_wdl", "s_wh", "s_wlp", "s_wld", "s_ast"))
        s_h0 = sem("s_h0")
        s_st_conf, s_st_ssm, s_st_h, s_st_pk, s_st_pa, s_st_hp = map(
            sem, ("s_st_conf", "s_st_ssm", "s_st_h", "s_st_pk", "s_st_pa", "s_st_hp"))
        s_zero, s_const, s_sq, s_var, s_sqrt, s_xs, s_fill, s_fillfree = map(
            sem, ("s_zero", "s_const", "s_sq", "s_var", "s_sqrt", "s_xs", "s_fill", "s_fillfree"))
        s_cs, s_dtp, s_dtraw, s_dte, s_dtl, s_a, s_tp, s_te, s_pro = map(
            sem, ("s_cs", "s_dtp", "s_dtraw", "s_dte", "s_dtl", "s_a", "s_tp", "s_te", "s_pro"))
        s_gc, s_u, s_ufree, s_raw, s_st, s_conv, s_thx, s_cv = map(
            sem, ("s_gc", "s_u", "s_ufree", "s_raw", "s_st", "s_conv", "s_thx", "s_cv"))
        s_pre, s_ab, s_pe1, s_L, s_T, s_W, s_xtl, s_hTd, s_pe2, s_y = map(
            sem, ("s_pre", "s_ab", "s_pe1", "s_L", "s_T", "s_W", "s_xtl", "s_hTd", "s_pe2", "s_y"))
        s_gv, s_ga, s_confst, s_cconv, s_z, s_yz, s_sq2, s_ms, s_rec, s_yn = map(
            sem, ("s_gv", "s_ga", "s_confst", "s_cconv", "s_z", "s_yz", "s_sq2", "s_ms", "s_rec", "s_yn"))
        s_h0t, s_h0tev, s_Bblk, s_hs, s_hnew = map(sem, ("s_h0t", "s_h0tev", "s_Bblk", "s_hs", "s_hnew"))
        s_pk, s_out, s_outev = map(sem, ("s_pk", "s_out", "s_outev"))
        s_ident, s_ss, s_expA, s_stc, s_sts, s_g, s_gst = map(
            sem, ("s_ident", "s_ss", "s_expA", "s_stc", "s_sts", "s_g", "s_gst"))
        s_ds0, s_dsr, s_settled = sem("s_ds0"), sem("s_dsr"), sem("s_settled")
        c_dve, c_act, c_pool = map(sem, ("c_dve", "c_act", "c_pool"))
        block = ctx.enter_context(nc.Block())

        def settled(eng):
            eng.sem_inc(s_settled, 1)

        def low_done(eng, g, k):
            if k < POOL_LOW:
                eng.wait_ge(s_wlp, POOL_LOW * g + k + 1)
            else:
                eng.wait_ge(s_wld, (BLOCKS - POOL_LOW) * g + k - POOL_LOW + 1)

        def split_next(g, k):
            return (g, k + RING) if k + RING < BLOCKS else (g + 1, k + RING - BLOCKS)

        def multiplied(eng, g, k):
            eng.wait_ge(s_u, U_TILES * g + U_OF[k] + 2)

        def low(eng, k):
            return eng.tensor_tensor(wl[:, k % RING], ring[:, k % RING], wh[:, k % RING].bitcast(F32), ALU.subtract)

        @block.sync
        def _(sp):
            sp.dma_start(crow[0:CK, :], A["conf_dw_w"][0]).then_inc(s_crow, 16)
            loads = [(R_CB, A["conf_dw_b"]), (R_LG, A["conf_ln_g"]), (R_LB, A["conf_ln_b"]),
                     (R_OB, A["conf_out_b"]), (R_NMIX, A["norm_mix_w"])]
            for r, ap in loads:
                sp.dma_start(crow[r:r + 1, :], ap).then_inc(s_crow, 16)
            cw, cb = A["ssm_conv_w"][0], A["ssm_conv_b"]
            for i in range(2):
                dst = crow[R_X + 5 * i:R_X + 5 * i + 5, :].rearrange("r (g c) -> r g c", g=G)
                src = cw[:, 0:DI].rearrange("k (g i c) -> i k g c", i=2, g=G)[i]
                sp.dma_start(dst[0:SK], src).then_inc(s_crow, 16)
                src = cb[:, 0:DI].rearrange("k (g i c) -> i k g c", i=2, g=G)[i]
                sp.dma_start(dst[SK:SK + 1], src).then_inc(s_crow, 16)
                r = R_BC + 5 * i
                sp.dma_start(crow[r:r + SK, :], cw[:, DI + D * i:DI + D * i + D]).then_inc(s_crow, 16)
                sp.dma_start(crow[r + SK:r + SK + 1, :], cb[:, DI + D * i:DI + D * i + D]).then_inc(s_crow, 16)
                dst = crow[R_NW + i:R_NW + i + 1, :].rearrange("r (g c) -> r g c", g=G)
                src = A["ssm_norm_w"].rearrange("k (g i c) -> i k g c", i=2, g=G)[i]
                sp.dma_start(dst, src).then_inc(s_crow, 16)
                sp.dma_start(crow[R_GB + i:R_GB + i + 1, :], A["gate_b"][:, D * i:D * i + D]).then_inc(s_crow, 16)
            sp.dma_start(ds0[:, :], A["d_skip"]).then_inc(s_ds0, 16)
            def w_block(g, k):
                first = [W_GV + P * g, W_GG + P * g, W_X + 2 * P * g, W_X + 2 * P * g + P, W_B + P * g,
                         W_C + P * g, W_Z + 2 * P * g, W_Z + 2 * P * g + P, W_GATE + P * g,
                         W_GATE + D + P * g][k]
                src = w_in.rearrange("(k p) n -> p k n", p=P)[:, :, bass.ds(first, P)]
                sp.dma_start(ring[:, k % RING], src).then_inc(s_w[k % RING], 16)

            sp.dma_start(dtb[:, :], A["dt_bias"][0].partition_broadcast(P)).then_inc(s_dtb, 16)
            sp.dma_start(expA[:, :], A["a_log"][0].partition_broadcast(P)).then_inc(s_dtb, 16)
            sp.dma_start(wdt, w_in.rearrange("(k p) n -> p k n", p=P)[:, :, W_DT:W_DT + NH]).then_inc(s_wdt, 16)
            for k in range(RING):
                w_block(0, k)
            for t in range(2):
                src = A["state_conf_conv"][0].rearrange("(t b) r c -> t (b r) c", t=2)[t]
                sp.dma_start(confrow[:, t], src).then_inc(s_conf, 16)
            sp.dma_start(ssmrow, A["state_ssm_conv"][0].rearrange("b r c -> (b r) c")).then_inc(s_ssm, 16)
            sp.dma_start(O["new_conf_sample"][0][:, 0:CK - 1 - TSAMP, :],
                         A["state_conf_conv"][0][:, TSAMP:CK - 1, :]).then_inc(s_st_conf, 16)

            def states_in(g):
                sp.wait_ge(s_pro, 1)
                sp.wait_ge(s_st_h, 32 * g + 1)
                src = A["state_ssm"][0].rearrange("b (g i h) p n -> g i (h p) b n", i=2, h=2)
                for i in range(2):
                    sp.dma_start(h0[:, i], src[g, i]).then_inc(s_h0, 16)

            def results_out(g):
                sp.wait_ge(s_cconv, g + 1 + 1)
                sp.dma_start(keep["aconv"][g], aout[:, :]).then_inc(s_ast, 16)
                sp.wait_ge(s_hnew, 4 * g + 4 + 1)
                dst = O["new_ssm_sample"][0].rearrange("b (g i h) p n -> g i (h p) b n", i=2, h=2)
                for i in range(2):
                    sp.dma_start(dst[g, i], h0[:, i]).then_inc(s_st_h, 16)
                sp.wait_ge(s_outev, 3 * g + 3 + 1)
                pks = pk_rows[:, :, :]
                for dst, r0, n in ((O["new_sconv_prompt"][0, 0], 0, 3),
                                   (O["new_sconv_sample"][0].rearrange("b r c -> (b r) c"), 3, 24)):
                    sp.dma_start(dst[:, bass.ds(2 * P * g, 2 * P)].rearrange("r (q c) -> r q c", q=2),
                                 pks[r0:r0 + n, 0:2, :]).then_inc(s_st_pk, 16)
                    for q in range(2):
                        sp.dma_start(dst[:, bass.ds(DI + D * q + P * g, P)],
                                     pks[r0:r0 + n, 2 + q, :]).then_inc(s_st_pk, 16)
                sp.dma_start(O["new_conf_prompt"][0, 0][:, bass.ds(P * g, P)],
                             pa_rows[0:CK - 1, :]).then_inc(s_st_pa, 16)
                sp.dma_start(O["new_ssm_prompt"][0, 0].rearrange("(g i h) p n -> g (h p) i n", i=2, h=2)[g],
                             hout[:, :, :]).then_inc(s_st_hp, 16)
                for r in range(TSAMP):
                    sp.dma_start(O["new_conf_sample"][0][:, CK - 1 - TSAMP + r, bass.ds(P * g, P)],
                                 pa_rows[CK - 1 + NSAMP * r:CK - 1 + NSAMP * r + NSAMP, :]).then_inc(s_st_pa, 16)

            def blocks(g, ks):
                for k in ks:
                    low_done(sp, *((g, k - RING) if k >= RING else (g - 1, k - RING + BLOCKS)))
                    w_block(g, k)

            def group(g, last=False):
                blocks(g, range(RING, 6))
                if not isinstance(g, int) or g > 0:
                    results_out(g - 1)
                blocks(g, range(6, 8))
                states_in(g)
                blocks(g, range(8, BLOCKS))
                if not last:
                    blocks(g + 1, range(RING))

            group(0)
            with sp.Fori(0, G - 2) as g1:
                group(g1 + 1)
            group(G - 1, last=True)
            results_out(G - 1)
            sp.wait_ge(s_st_h, 32 * G + 1)
            sp.wait_ge(s_ast, 16 * G + 1)
            sp.wait_ge(s_st_pk, 96 * G + 1)
            sp.wait_ge(s_st_pa, 80 * G + 1)
            sp.wait_ge(s_st_hp, 16 * G + 1)
            sp.wait_ge(s_st_conf, 16)

        @block.gpsimd
        def _(pool):
            for started in (s_st_h, s_pe1, s_pe2, s_yn, s_u, s_g, s_cconv, s_conv, s_y, s_hs, s_out, s_hnew, s_ufree, s_pk, s_xtl, s_W, s_gst, s_st_pk, s_st_pa, s_st_hp, s_outev, s_ast):
                pool.sem_inc(started, 1)
            k = Steps(pool, c_pool)
            for m in (U, SL, ones, Ub, SLb, Bm):
                pool.memset(m[:, :], 1.0).then_inc(s_zero, 1)
            pool.memset(ident[:, :], 0.0).then_inc(s_zero, 1)
            pool.wait_ge(s_zero, 7)

            def mask(m, cond, base, pattern, mult, fill=0.0):
                k.link(pool.affine_select(out=m, in_=m, compare_op=cond, fill=fill, base=base,
                                          pattern=pattern, channel_multiplier=mult))

            mask(ident[:, :], ALU.not_equal, 0, [[-1, P]], 1, 1.0)
            pool.sem_inc(s_ident, 1)
            mask(U[:, :], ALU.is_ge, 0, [[1, P]], -1)
            mask(SL[:, :], ALU.is_gt, 0, [[-1, P]], 1)
            Ub3 = Ub[:, :].rearrange("k (b r) -> k b r", b=NSAMP)
            mask(Ub3, ALU.is_ge, 0, [[TSAMP, NSAMP], [1, TSAMP]], -1)
            mask(Ub3, ALU.is_ge, 0, [[-TSAMP, NSAMP], [0, TSAMP]], 1)
            SLb3 = SLb[:, :].rearrange("k (b r) -> k b r", b=NSAMP)
            mask(SLb3, ALU.is_gt, 0, [[-TSAMP, NSAMP], [-1, TSAMP]], 1)
            mask(SLb3, ALU.is_ge, TSAMP - 1, [[TSAMP, NSAMP], [0, TSAMP]], -1)
            mask(Bm[:, :], ALU.is_ge, 0, [[-TSAMP, NSAMP]], 1)
            mask(Bm[:, :], ALU.is_ge, TSAMP - 1, [[TSAMP, NSAMP]], -1)
            pool.memset(tail[:, :, :], 0.0).then_inc(s_const, 1)
            pool.memset(dtt[:, :, :], 0.0).then_inc(s_const, 1)
            pool.memset(raw_p[:, :, 0:SK - 1], 0.0).then_inc(s_const, 1)
            pool.memset(a_p[:, 0:CK - 1], 0.0).then_inc(s_const, 1)
            def split(g, k):
                pool.wait_ge(s_wh, BLOCKS * g + k + 1)
                settled(pool)
                low(pool, k).then_inc(s_wlp, 1)

            split(0, 0)
            split(0, 1)
            pool.wait_ge(s_pro, 1)

            def a_over_channels(g, js):
                for j in js:
                    S = CHUNKS[j][1]
                    a4 = aa[0:S, j, bass.ds(HG * g, HG)].unsqueeze(2)
                    pool.tensor_copy(ab[0:S, j, :].rearrange("s (h p) -> s h p", h=HG),
                                     a4.broadcast_to([S, HG, HD])).then_inc(s_ab, 1)

            def group(g, is_last=False):
                split(g, 2)
                pool.wait_ge(s_yn, 2 * g + 1)
                pool.wait_ge(s_u, U_TILES * g + 1)
                pool.wait_ge(s_g, 2 * g + 1)
                pool.wait_ge(s_cconv, g + 1)
                settled(pool)
                pool.tensor_copy(gc[:, :], cs[:, g, :]).then_inc(s_gc, 1)
                pool.tensor_copy(a_s[:, :, 0:CK - 1],
                                 stC[:, g, :].rearrange("p (b r) -> p b r", b=NSAMP)).then_inc(s_stc, 1)
                pool.wait_ge(s_conv, 4 * g + 1)
                settled(pool)
                for q, m in enumerate((2 * g, 2 * g + 1, G * 2 + g, G * 3 + g)):
                    pool.tensor_copy(raw_s[:, q, :, 0:SK - 1],
                                     stS[:, m, :].rearrange("p (b r) -> p b r", b=NSAMP)).then_inc(s_sts, 1)
                split(g, 3)
                a_over_channels(g, range(3))
                split(g, 4)
                a_over_channels(g, range(3, 6))
                split(g, 5)

                def decay_rows(j):
                    ci = ORDER[j]
                    S = CHUNKS[ci][1]
                    a4 = aa[0:S, ci, bass.ds(HG * g, HG)].unsqueeze(2)
                    um = (Ub if ci == 0 else U)[0:S, 0:S].unsqueeze(1).broadcast_to([S, HG, S])
                    pool.wait_ge(s_pe1, 6 * g + j + 1)
                    settled(pool)
                    pool.tensor_tensor(aU[0:S, :, 0:S], a4.broadcast_to([S, HG, S]), um,
                                       ALU.mult).then_inc(s_pre, 1)

                decay_rows(0)
                for j in range(6):
                    ci = ORDER[j]
                    S = CHUNKS[ci][1]
                    t4 = tail[0:S, ci, bass.ds(HG * g, HG)].unsqueeze(2).broadcast_to([S, HG, HD])
                    pool.wait_ge(s_T, 6 * g + j + 1)
                    settled(pool)
                    pool.tensor_tensor(xtl[0:S, :, :],
                                       Tt[0:S, 0:2, :].rearrange("s i (h p) -> s (i h) p", h=2), t4,
                                       ALU.mult).then_inc(s_xtl, 1)
                    if 0 < j < 5:
                        d4 = Dl[:, ci, bass.ds(HG * g, HG)].unsqueeze(2).broadcast_to([P, HG, HD])
                        pool.wait_ge(s_y, 6 * g + j + 1)
                        settled(pool)
                        pool.tensor_tensor(hTd[:, :, :], hT[:, :, :], d4, ALU.mult).then_inc(s_hTd, 1)
                    if j == 5:
                        pool.wait_ge(s_hs, 4 * g + 1)
                        settled(pool)
                        pool.tensor_tensor(Bblk, Tt[0:SAMP, 2, :].unsqueeze(1).broadcast_to([SAMP, NSAMP, N]),
                                           Bm[:, :].unsqueeze(2).broadcast_to([SAMP, NSAMP, N]),
                                           ALU.mult).then_inc(s_Bblk, 1)
                    if j < 5:
                        decay_rows(j + 1)
                    if j == 0:
                        pool.wait_ge(s_out, 2 * g + 1)
                        settled(pool)
                        pool.tensor_copy(pk[:, :, 0:3], raw_p[:, :, PROMPT:PROMPT + 3]).then_inc(s_pk, 1)
                        for q in range(4):
                            pool.tensor_copy(pk[:, q, 3:27].rearrange("p (b r) -> p b r", b=NSAMP),
                                             raw_s[:, q, :, TSAMP:TSAMP + 3]).then_inc(s_pk, 1)
                        pool.tensor_copy(pa[:, 0:CK - 1], a_p[:, PROMPT:PROMPT + CK - 1]).then_inc(s_pk, 1)
                        pool.tensor_copy(pa[:, CK - 1:62].rearrange("p (r b) -> p b r", b=NSAMP),
                                         a_s[:, :, CK - 1:CK - 1 + TSAMP]).then_inc(s_pk, 1)
                if not is_last:
                    split(g + 1, 0)
                    split(g + 1, 1)

            with pool.Fori(0, G - 1) as g:
                group(g)
            group(G - 1, is_last=True)

        def u_cols(i, a, b):
            return pu[i % 2][:, UO + a:UO + b]

        @block.scalar
        def _(act):
            k = Steps(act, c_act)
            act.dma_start(xin[0:SAMP, 0, :], A["x_sample"].rearrange("b t d -> (b t) d")).then_inc(s_x, 16)
            act.dma_start(xin[SAMP:SAMP + META, 0, :], A["meta_tokens"]).then_inc(s_x, 16)
            act.dma_start(xin[:, 1:5, :], A["x_prompt"][0].rearrange("(t p) d -> p t d", p=P)).then_inc(s_x, 16)
            act.wait_ge(s_x, 48)
            act.wait_ge(s_ss, 1)
            for t, (c, S) in enumerate(TILES):
                k.link(act.activation(ybuf[0:S, :, :].rearrange("p a b -> p (a b)")[:, 0:D], xin[0:S, t, :],
                                      ACT.Square, accum_out=ss[0:S, t:t + 1]))
            act.sem_inc(s_sq, 1)
            act.wait_ge(s_var, 1)
            act.activation(ss[:, 0:5], ss[:, 0:5], ACT.Sqrt).then_inc(s_sqrt, 1)

            def split(g, k):
                act.wait_ge(s_w[k % RING], BLOCKS // RING * 16 * g + 16 * (k // RING + 1))
                act.activation(wh[:, k % RING].rearrange("p k m -> p (k m)"),
                               ring[:, k % RING].rearrange("p k m -> p (k m)"), ACT.Copy).then_inc(s_wh, 1)

            for n in range(2 * len(TILES)):
                (c, S), h = TILES[n // 2], n % 2
                act.wait_ge(s_xt, n + 1)
                act.activation(xh[:, 4 * h:4 * h + 4, c:c + S], xt[n % 2][:, :, 0:S], ACT.Copy).then_inc(s_xh, 1)
                if n == 4:
                    act.wait_ge(s_wdt, 16)
                    act.activation(wdh[:, :, :], wdt, ACT.Copy).then_inc(s_wdh, 1)
            split(0, 0)
            split(0, 1)
            act.wait_ge(s_dtb, 32)
            act.activation(expA[:, :], expA[:, :], ACT.Exp).then_inc(s_expA, 1)
            act.wait_ge(s_dte, 1)
            k.link(act.activation(tmp2[:, :, :], tmp2[:, :, :], ACT.Exp))
            act.activation(tmp2[:, :, :], tmp2[:, :, :], ACT.Ln, bias=1.0).then_inc(s_dtl, 1)
            act.wait_ge(s_tp, 1)
            for ci, (c, S) in enumerate(CHUNKS):
                act.activation(tail[0:S, ci, :], pY[0:S, NH * ci:NH * ci + NH], ACT.Exp).then_inc(s_te, 1)
            act.activation(Dl[:, 1:6, :], pY[:, 7 * NH:12 * NH].rearrange("p (c h) -> p c h", c=5),
                           ACT.Exp).then_inc(s_te, 1)

            def group(g, is_last=False):
                U0 = U_TILES * g

                def split_behind(k):
                    if k + RING < BLOCKS or not is_last:
                        multiplied(act, g, k)
                        split(*split_next(g, k))

                def evac(r):
                    act.wait_ge(s_u, U0 + r + 2)

                split_behind(0)
                evac(0)
                act.wait_ge(s_yn, 2 * g + 1)
                act.activation(zc[:, 0, :], u_cols(0, 0, T), ACT.Copy, scale=0.5).then_inc(s_ufree, 1)
                split_behind(1)
                evac(1)
                act.activation(zc[:, 1, :], u_cols(1, 0, T), ACT.Tanh, scale=0.5).then_inc(s_ufree, 1)

                def raw(q):
                    split_behind(2 + q)
                    evac(2 + q)
                    act.wait_ge(s_conv, 4 * g + 1)
                    act.wait_ge(s_pk, 7 * g + 1)
                    act.activation(raw_p[:, q, SK - 1:], u_cols(q, SAMP, T), ACT.Copy).then_inc(s_raw, 1)
                    act.activation(raw_s[:, q, :, SK - 1:], u_cols(q, 0, SAMP).rearrange("p (b r) -> p b r", b=NSAMP),
                                   ACT.Copy).then_inc(s_ufree, 1)

                def silu(q):
                    act.wait_ge(s_conv, 4 * g + q + 2)
                    if q < 2:
                        act.wait_ge(s_u, U0 + 1)
                    else:
                        act.wait_ge(s_cv, 4 * g + q - 1)
                    act.activation(th[:, q % 2, :], cv[:, q, :], ACT.Tanh).then_inc(s_thx, 1)

                raw(0)
                raw(1)
                silu(0)
                raw(2)
                silu(1)
                raw(3)
                silu(2)
                for i in range(2):
                    evac(6 + i)
                    act.wait_ge(s_hnew, 4 * g + 1)
                    act.activation(Ed[:, i, :], u_cols(i, 0, T), ACT.Exp).then_inc(s_ufree, 1)
                silu(3)

                def chunk(j):
                    ci = ORDER[j]
                    S = CHUNKS[ci][1]
                    act.wait_ge(s_pe1, 6 * g + j + 2)
                    act.wait_ge(s_pe2, 6 * g + j + 1)
                    act.activation(Lx[0:S, :, 0:S], pS[0:S, :].rearrange("s (h t) -> s h t", h=HG)[:, :, 0:S],
                                   ACT.Exp).then_inc(s_L, 1)
                    act.wait_ge(s_W, 6 * g + j + 1)
                    act.wait_ge(s_xtl, 6 * g + j + 1)
                    act.wait_ge(s_hs, 4 * g + 1)
                    if S == P:
                        act.activation(Tt[:, :, :].rearrange("s a t -> s (a t)"), pT[:, :], ACT.Copy).then_inc(s_T, 1)
                    else:
                        act.activation(Tt[0:S, 0:3, :].rearrange("s a t -> s (a t)"), pT[0:S, 0:3 * P], ACT.Copy)
                        act.activation(Tt[0:S, 3, 0:S], pT[0:S, 3 * P:3 * P + S], ACT.Copy).then_inc(s_T, 1)

                def z(i):
                    split_behind(6 + i)
                    evac(8 + i)
                    act.wait_ge(s_ga, 2 * g + 2)
                    act.wait_ge(s_cv, 4 * g + 3 + i)
                    act.activation(th[:, i, :], u_cols(i, 0, T), ACT.Tanh, scale=0.5).then_inc(s_z, 1)
                    act.activation(zc[:, i, :], u_cols(i, 0, T), ACT.Copy).then_inc(s_ufree, 1)

                def gate(i):
                    split_behind(8 + i)
                    evac(10 + i)
                    act.wait_ge(s_gc, g + 1)
                    act.wait_ge(s_gst, 32 * g + 16 * i + 1)
                    act.activation(gbuf[:, :], u_cols(i, 0, T), ACT.Tanh, bias=gc[:, R_GB + i:R_GB + i + 1],
                                   scale=0.5).then_inc(s_g, 1)
                    act.wait_ge(s_g, 2 * g + i + 2)
                    act.sem_inc(s_ufree, 1)
                    act.dma_start(keep["gates"][i, g], gbuf[:, :]).then_inc(s_gst, 16)

                def h0_copy(r):
                    act.wait_ge(s_h0t, 4 * g + r + 1)
                    act.wait_ge(s_pe2, 6 * g + 1)
                    act.activation(h0T[:, r // 2, 4 * (r % 2):4 * (r % 2) + 4, :].rearrange("p b m -> p (b m)"),
                                   (pS, pT)[r % 2][:, :], ACT.Copy).then_inc(s_h0tev, 1)

                chunk(0)
                z(0)
                chunk(1)
                chunk(2)
                z(1)
                chunk(3)
                chunk(4)
                gate(0)
                chunk(5)
                for r in range(4):
                    h0_copy(r)
                gate(1)
                act.wait_ge(s_yz, g + 1)
                act.activation(th[:, :, :], ybuf[:, :, :], ACT.Square).then_inc(s_sq2, 1)
                act.wait_ge(s_out, 2 * g + 2)
                act.wait_ge(s_st_pk, 96 * g + 1)
                act.wait_ge(s_st_pa, 80 * g + 1)
                act.wait_ge(s_st_hp, 16 * g + 1)
                act.activation(pk_rows[:, :, :].rearrange("r q c -> r (q c)"), pC[0:27, :], ACT.Copy).then_inc(s_outev, 1)
                act.wait_ge(s_out, 2 * g + 2 + 1)
                act.activation(hout[:, :, :].rearrange("p i n -> p (i n)"), pY[:, 0:2 * P], ACT.Copy).then_inc(s_outev, 1)
                act.activation(pa_rows[:, :], pY[0:62, 2 * P:3 * P], ACT.Copy).then_inc(s_outev, 1)
                for r in range(2):
                    evac(12 + r)
                    act.activation(zc[:, 0, 280 * r:280 * r + 280], pu[r][:, 0:280], ACT.Sqrt,
                                   scale=1.0 / (2 * P), bias=eps[:, :]).then_inc(s_ufree, 1)

            with act.Fori(0, G - 1) as g:
                group(g)
            group(G - 1, is_last=True)
            act.wait_ge(s_gst, 32 * G + 1)

        @block.tensor
        def _(pe):
            fill_no = [0]

            def fill(parts):
                n = fill_no[0]
                bank = (pS, pT)[n % 2]
                if n >= 2:
                    pe.wait_ge(s_fillfree, n - 1)
                for col, src in parts:
                    R, C = src.shape
                    last = pe.transpose(bank[0:C, col:col + R], src, ident[0:R, 0:R])
                last.then_inc(s_fill, 1)
                fill_no[0] += 1

            pe.wait_ge(s_ident, 1)
            pe.wait_ge(s_crow, 16 * N_CROW)
            pe.wait_ge(s_dsr, 1)
            fill([(64 * j, crow[:, P * j:P * j + P]) for j in range(KD)]
                 + [(64 * g + R_DS + i, dsrow[:, P * (2 * g + i):P * (2 * g + i) + P])
                    for g in range(G) for i in range(2)])
            for t, (c, S) in enumerate(TILES):
                pe.wait_ge(s_xs, t + 1)
                for h in range(2):
                    fill([(P * q, xin[0:S, t, P * (4 * h + q):P * (4 * h + q) + P]) for q in range(4)])
            pe.wait_ge(s_conf, 32)
            for t in range(2):
                for h in range(2):
                    fill([(P * q, confrow[:, t, P * (4 * h + q):P * (4 * h + q) + P]) for q in range(4)])
            pe.wait_ge(s_ssm, 16)
            for f in range(2):
                fill([(32 * q, ssmrow[:, P * (16 * f + q):P * (16 * f + q) + P]) for q in range(16)])
            pe.wait_ge(s_wdl, 1)
            pe.wait_ge(s_xl, 2 * len(TILES))
            for ci, (c, S) in enumerate(CHUNKS):
                for j in range(KD):
                    for n, (x, w) in enumerate(((xh, wdh), (xl, wdh), (xh, wdl))):
                        last = pe.matmul(pC[0:S, NH * ci:NH * ci + NH], x[:, j, c:c + S], w[:, j, :],
                                         start=(j == 0 and n == 0), stop=(j == KD - 1 and n == 2))
            last.then_inc(s_dtp, 1)
            pe.wait_ge(s_a, 1)
            for ci, (c, S) in enumerate(CHUNKS):
                pe.matmul(pY[0:S, NH * ci:NH * ci + NH], (SLb if ci == 0 else SL)[0:S, 0:S], aa[0:S, ci, :],
                          start=True, stop=True)
            for ci, (c, S) in enumerate(CHUNKS[1:], 1):
                last = pe.matmul(pY[:, NH * (6 + ci):NH * (7 + ci)], ones[0:S, :], aa[0:S, ci, :],
                                 start=True, stop=True)
            last.then_inc(s_tp, 1)
            pe.wait_ge(s_te, 7)
            pe.wait_ge(s_fillfree, 17)

            with pe.Fori(0, G) as g:
                U0 = U_TILES * g

                def free(r):
                    pe.wait_ge(s_ufree, U0 + max(r, 1))

                def block(k, halves=(0, 1)):
                    r = U_OF[k]
                    for h in halves:
                        if h == 0:
                            free(r)
                            low_done(pe, g, k)
                        for j in range(4 * h, 4 * h + 4):
                            for n, (w, x) in enumerate(((wh, xh), (wh, xl), (wl, xh))):
                                for a, b in ((0, USPLIT), (USPLIT, T)):
                                    last = pe.matmul(u_cols(r, a, b), w[:, k % RING, j, :], x[:, j, a:b],
                                                     start=(j == 0 and n == 0), stop=(j == KD - 1 and n == 2))
                        if h == 1:
                            last.then_inc(s_u, 1)

                def stage1(j):
                    ci = ORDER[j]
                    c, S = CHUNKS[ci]
                    pe.wait_ge(s_pre, 6 * g + j + 1)
                    if j == 0:
                        pe.wait_ge(s_hnew, 4 * g + 1)
                    else:
                        pe.wait_ge(s_L, 6 * g + j)
                    if S < P:
                        settled(pe)
                    pe.matmul(pS[0:S, :].rearrange("s (h t) -> s h t", h=HG)[:, :, 0:S],
                              (SLb if ci == 0 else SL)[0:S, 0:S], aU[0:S, :, 0:S], start=True, stop=True)
                    if j == 0:
                        pe.wait_ge(s_cv, 4 * g + 4)
                    else:
                        pe.wait_ge(s_T, 6 * g + j)
                    for q in range(3):
                        pe.transpose(pT[0:S, P * q:P * q + P], cv[:, q, c:c + S], ident[:, :])
                    pe.matmul(pT[0:S, 3 * P:3 * P + S], cv[:, 2, c:c + S], cv[:, 3, c:c + S],
                              start=True, stop=True).then_inc(s_pe1, 1)

                def stage2(j):
                    ci = ORDER[j]
                    c, S = CHUNKS[ci]
                    pe.wait_ge(s_W, 6 * g + j + 2)
                    pe.wait_ge(s_xtl, 6 * g + j + 2)
                    pe.wait_ge(s_y, 6 * g + j + 1)
                    pe.wait_ge(s_outev, 3 * g + 1)
                    yv = pY[:, 0:2 * P].rearrange("p (i t) -> p i t", i=2)
                    for h in range(HG):
                        half = HD * (h % 2)
                        last = pe.matmul(yv[half:half + HD, h // 2, 0:S], xdt[0:S, h, :], Lx[0:S, h, 0:S],
                                         start=True, stop=True)
                    if ci >= 2:
                        for i in range(2):
                            pe.matmul(pC[:, P * i:P * i + S], hT[:, 2 * i:2 * i + 2, :], cv[:, 3, c:c + S],
                                      start=True, stop=True)
                    if ci == 0:
                        pe.wait_ge(s_h0tev, 4 * g + 4)
                        for i in range(2):
                            for b in range(NSAMP):
                                last = pe.matmul(pC[:, P * i + TSAMP * b:P * i + TSAMP * b + TSAMP],
                                                 h0T[:, i, b, :], cv[:, 3, TSAMP * b:TSAMP * b + TSAMP],
                                                 start=True, stop=True)
                    else:
                        last = pe.matmul(pC[:, 2 * P:4 * P], Tt[0:S, 2, :], xtl[0:S, :, :], start=True, stop=True)
                    last.then_inc(s_pe2, 1)

                def states_turned(r):
                    if r == 0:
                        pe.wait_ge(s_h0, 32 * g + 32)
                    if r < 2:
                        pe.wait_ge((s_L, s_T)[r], 6 * g + 6)
                    else:
                        pe.wait_ge(s_h0tev, 4 * g + r - 1)
                    for b in range(4):
                        last = pe.transpose((pS, pT)[r % 2][:, P * b:P * b + P], h0[:, r // 2, 4 * (r % 2) + b, :],
                                            ident[:, :])
                    last.then_inc(s_h0t, 1)

                def states_added(r):
                    pe.wait_ge(s_Bblk, g + 1)
                    if r < 2:
                        pe.wait_ge(s_h0tev, 4 * g + r + 3)
                    else:
                        pe.wait_ge(s_hnew, 4 * g + r)
                    i, q = r // 2, r % 2
                    pe.matmul((pS, pT)[r % 2][:, :], xtl[0:SAMP, 2 * i:2 * i + 2, :],
                              Bblk[:, 4 * q:4 * q + 4, :], start=True, stop=True).then_inc(s_hs, 1)

                for k in range(6):
                    block(k)
                free(7)
                pe.wait_ge(s_ab, 6 * g + 6)
                for i in range(2):
                    for ci, (c, S) in enumerate(CHUNKS):
                        last = pe.matmul(u_cols(i, c, c + S), ab[0:S, ci, P * i:P * i + P],
                                         (Ub if ci == 0 else U)[0:S, 0:S], start=True, stop=True)
                    last.then_inc(s_u, 1)
                block(6, (0,))
                stage1(0)
                block(6, (1,))
                stage2(0)
                stage1(1)
                block(7, (0,))
                stage2(1)
                stage1(2)
                block(7, (1,))
                stage2(2)
                stage1(3)
                block(8, (0,))
                stage2(3)
                stage1(4)
                block(8, (1,))
                stage2(4)
                stage1(5)
                states_turned(0)
                states_turned(1)
                block(9, (0,))
                states_turned(2)
                states_turned(3)
                block(9, (1,))
                stage2(5)
                for r in range(4):
                    states_added(r)
                pe.wait_ge(s_y, 6 * g + 6 + 1)
                pe.wait_ge(s_pk, 7 * g + 7 + 1)
                for q in range(4):
                    last = pe.transpose(pC[0:27, P * q:P * q + P], pk[:, q, :], ident[:, :])
                last.then_inc(s_out, 1)
                for i in range(2):
                    pe.transpose(pY[:, P * i:P * i + P], hT[:, 2 * i:2 * i + 2, :].rearrange("n h p -> n (h p)"), ident[:, :])
                pe.transpose(pY[0:62, 2 * P:3 * P], pa[:, :], ident[:, :]).then_inc(s_out, 1)
                pe.wait_ge(s_sq2, g + 1)
                for r in range(2):
                    free(12 + r)
                    for i in range(2):
                        last = pe.matmul(pu[r][:, 0:280], ones[:, :], th[:, i, 280 * r:280 * r + 280],
                                         start=(i == 0), stop=(i == 1))
                    last.then_inc(s_u, 1)

        @block.vector
        def _(dve):
            k = Steps(dve, c_dve)

            def stt(out, in0, scalar, in1, op0=ALU.mult, op1=ALU.add):
                return dve.scalar_tensor_tensor(out=out, in0=in0, scalar=scalar, in1=in1, op0=op0, op1=op1)

            dve.memset(ss[:, :], 1.0).then_inc(s_ss, 1)
            k.link(dve.memset(eps[:, :], EPS))
            dve.wait_ge(s_ds0, 16)
            dve.tensor_copy(dsrow.rearrange("p (h c) -> p h c", h=NH),
                            ds0[:, :].unsqueeze(2).broadcast_to([1, NH, HD])).then_inc(s_dsr, 1)
            dve.wait_ge(s_fill, 1)
            k.link(dve.tensor_copy(cs[:, :, :], pS[:, :].rearrange("p (g r) -> p g r", g=G)[:, :, 0:NR]))
            dve.sem_inc(s_fillfree, 1)
            k.link(dve.tensor_scalar(cs[:, :, R_X:R_X + 20], cs[:, :, R_X:R_X + 20], 0.5, None, ALU.mult))
            k.link(dve.tensor_scalar(cs[:, :, R_GB:R_GB + 2], cs[:, :, R_GB:R_GB + 2], 0.5, None, ALU.mult))
            dve.wait_ge(s_sq, 1)
            dve.tensor_scalar(ss[:, 0:5], ss[:, 0:5], 1.0 / D, EPS, ALU.mult, ALU.add).then_inc(s_var, 1)
            dve.wait_ge(s_sqrt, 1)
            k.link(dve.reciprocal(ss[:, 0:5], ss[:, 0:5]))
            for t, (c, S) in enumerate(TILES):
                dve.tensor_scalar(xin[0:S, t, :], xin[0:S, t, :], ss[0:S, t:t + 1], None, ALU.mult).then_inc(s_xs, 1)
            n = 1

            def x_low(m):
                (c, S), h = TILES[m // 2], m % 2
                dve.wait_ge(s_xh, m + 1)
                dve.tensor_tensor(xl[:, 4 * h:4 * h + 4, c:c + S], xt[m % 2][:, :, 0:S],
                                  xh[:, 4 * h:4 * h + 4, c:c + S].bitcast(F32), ALU.subtract).then_inc(s_xl, 1)

            for t, (c, S) in enumerate(TILES):
                for h in range(2):
                    dve.wait_ge(s_fill, n + 1)
                    if n > 2:
                        dve.wait_ge(s_xl, n - 2)
                    w = cs[:, 4 * h:4 * h + 4, R_NMIX].unsqueeze(2).broadcast_to([P, 4, S])
                    dve.tensor_tensor(xt[(n - 1) % 2][:, :, 0:S],
                                      (pS, pT)[n % 2][:, :].rearrange("p (q s) -> p q s", q=4)[:, :, 0:S], w,
                                      ALU.mult).then_inc(s_xt, 1)
                    dve.wait_ge(s_xt, n)
                    dve.sem_inc(s_fillfree, 1)
                    if n > 1:
                        x_low(n - 2)
                    n += 1
            x_low(n - 2)
            dve.wait_ge(s_wdh, 1)
            dve.tensor_tensor(wdl[:, :, :], wdt, wdh[:, :, :].bitcast(F32), ALU.subtract).then_inc(s_wdl, 1)
            for t in range(2):
                for h in range(2):
                    dve.wait_ge(s_fill, n + 1)
                    dve.tensor_copy(stC[:, 4 * h:4 * h + 4, 120 * t:120 * t + 120],
                                    (pS, pT)[n % 2][:, :].rearrange("p (q s) -> p q s", q=4)[:, :, 0:120])\
                       .then_inc(s_fillfree, 1)
                    n += 1
            for f in range(2):
                dve.wait_ge(s_fill, n + 1)
                dve.tensor_copy(stS[:, 16 * f:16 * f + 16, :],
                                (pS, pT)[n % 2][:, :].rearrange("p (q s) -> p q s", q=16)[:, :, 0:24])\
                   .then_inc(s_fillfree, 1)
                n += 1
            dve.wait_ge(s_const, 4)
            dve.wait_ge(s_dtb, 32)
            dve.wait_ge(s_dtp, 1)
            for ci, (c, S) in enumerate(CHUNKS):
                last = dve.tensor_tensor(dtt[0:S, ci, :], pC[0:S, NH * ci:NH * ci + NH], dtb[0:S, :], ALU.add)
            k.link(last)
            k.link(dve.tensor_scalar(tmp1[:, :, :], dtt[:, :, :], 0.0, None, ALU.max))
            stt(tmp2[:, :, :], tmp1[:, :, :], -2.0, dtt[:, :, :]).then_inc(s_dte, 1)
            dve.wait_ge(s_dtl, 1)
            dve.wait_ge(s_expA, 1)
            k.link(dve.tensor_tensor(dtt[:, :, :], tmp1[:, :, :], tmp2[:, :, :], ALU.add))
            stt(aa[:, :, :], dtt[:, :, :], -1.0, expA[:, :].unsqueeze(1).broadcast_to([P, 6, NH]),
                ALU.mult, ALU.mult).then_inc(s_a, 1)
            dve.wait_ge(s_te, 7)
            dve.tensor_tensor(tail[:, :, :], tail[:, :, :], dtt[:, :, :], ALU.mult).then_inc(s_pro, 1)
            dve.wait_ge(s_pro, 1)

            with dve.Fori(0, G) as g:
                k.enter(g, DVE_STEPS)

                def split(kk):
                    dve.wait_ge(s_wh, BLOCKS * g + kk + 1)
                    low(dve, kk).then_inc(s_wld, 1)

                def conf_tap(j):
                    wj = gc[:, R_CW + j:R_CW + j + 1]
                    outs = (aout if j == CK - 1 else cacc)
                    o_s = outs[:, 0:SAMP].rearrange("p (b r) -> p b r", b=NSAMP)
                    o_p = outs[:, SAMP:T]
                    i_s, i_p = a_s[:, :, j:j + TSAMP], a_p[:, j:j + PROMPT]
                    if j == CK - 1:
                        dve.wait_ge(s_ast, 16 * g + 1)
                    if j == 0:
                        bias = gc[:, R_CB:R_CB + 1]
                        dve.tensor_scalar(o_s, i_s, wj, bias, ALU.mult, ALU.add)
                        k.link(dve.tensor_scalar(o_p, i_p, wj, bias, ALU.mult, ALU.add))
                    else:
                        stt(o_s, i_s, wj, cacc[:, 0:SAMP].rearrange("p (b r) -> p b r", b=NSAMP))
                        ins = stt(o_p, i_p, wj, cacc[:, SAMP:T])
                        if j == CK - 1:
                            ins.then_inc(s_cconv, 1)
                        else:
                            k.link(ins)

                def ssm_conv(q):
                    r = R_X + 5 * q
                    dve.wait_ge(s_ufree, U_TILES * g + 3 + q + 1)
                    dve.wait_ge(s_raw, 4 * g + q + 1)
                    dve.wait_ge(s_sts, 4 * g + q + 1)
                    o_s = cv[:, q, 0:SAMP].rearrange("p (b r) -> p b r", b=NSAMP)
                    o_p = cv[:, q, SAMP:T]
                    for j in range(SK):
                        wj = gc[:, r + j:r + j + 1]
                        i_s, i_p = raw_s[:, q, :, j:j + TSAMP], raw_p[:, q, j:j + PROMPT]
                        if j == 0:
                            bias = gc[:, r + SK:r + SK + 1]
                            dve.tensor_scalar(o_s, i_s, wj, bias, ALU.mult, ALU.add)
                            k.link(dve.tensor_scalar(o_p, i_p, wj, bias, ALU.mult, ALU.add))
                        else:
                            stt(o_s, i_s, wj, o_s)
                            ins = stt(o_p, i_p, wj, o_p)
                            if j == SK - 1:
                                ins.then_inc(s_conv, 1)
                            else:
                                k.link(ins)

                def silu(q):
                    dve.wait_ge(s_thx, 4 * g + q + 1)
                    stt(cv[:, q, :], th[:, q % 2, :], 1.0, cv[:, q, :], ALU.add, ALU.mult).then_inc(s_cv, 1)

                def stage1(j):
                    ci = ORDER[j]
                    S = CHUNKS[ci][1]
                    um = (Ub if ci == 0 else U)[0:S, 0:S]
                    dve.wait_ge(s_T, 6 * g + j + 1)
                    k.link(dve.tensor_tensor(cbm[0:S, 0:S], Tt[0:S, 3, 0:S], um, ALU.mult))
                    dt4 = dtt[0:S, ci, bass.ds(HG * g, HG)].unsqueeze(2).broadcast_to([S, HG, HD])
                    dve.tensor_tensor(xdt[0:S, :, :], Tt[0:S, 0:2, :].rearrange("s i (h p) -> s (i h) p", h=2),
                                      dt4, ALU.mult)
                    dve.tensor_tensor(Lx[0:S, :, 0:S], Lx[0:S, :, 0:S],
                                      cbm[0:S, 0:S].unsqueeze(1).broadcast_to([S, HG, S]),
                                      ALU.mult).then_inc(s_W, 1)

                def stage2(j):
                    ci = ORDER[j]
                    c, S = CHUNKS[ci]
                    dve.wait_ge(s_pe2, 6 * g + j + 2)
                    yv = pY[:, 0:2 * P].rearrange("p (i t) -> p i t", i=2)[:, :, 0:S]
                    if ci == 1:
                        for i in range(2):
                            stt(ybuf[:, i, c:c + S], cv[:, i, c:c + S], gc[:, R_DS + i:R_DS + i + 1], yv[:, i, :])
                    else:
                        v = yi[:, :, 0:S]
                        k.link(dve.tensor_tensor(v, pC[:, 0:2 * P].rearrange("p (i t) -> p i t", i=2)[:, :, 0:S],
                                                 Ed[:, :, c:c + S], ALU.mult))
                        k.link(dve.tensor_tensor(v, v, yv, ALU.add))
                        for i in range(2):
                            last = stt(ybuf[:, i, c:c + S], cv[:, i, c:c + S], gc[:, R_DS + i:R_DS + i + 1],
                                       yi[:, i, 0:S])
                    st = pC[:, 2 * P:4 * P].rearrange("p (h q) -> p h q", h=HG)
                    if ci == 1:
                        last = dve.tensor_copy(hT[:, :, :], st)
                    elif ci > 1:
                        dve.wait_ge(s_hTd, 4 * g + j)
                        last = dve.tensor_tensor(hT[:, :, :], hTd[:, :, :], st, ALU.add)
                    last.then_inc(s_y, 1)

                dve.wait_ge(s_gc, g + 1)
                dve.wait_ge(s_ufree, U_TILES * g + 2 + 1)
                dve.wait_ge(s_stc, g + 1)
                dve.wait_ge(s_pk, 7 * g + 1)
                dve.wait_ge(s_cconv, g + 1)
                stt(a_s[:, :, CK - 1:], zc[:, 1, 0:SAMP].rearrange("p (b r) -> p b r", b=NSAMP), 1.0,
                    zc[:, 0, 0:SAMP].rearrange("p (b r) -> p b r", b=NSAMP), ALU.add, ALU.mult).then_inc(s_ga, 1)
                stt(a_p[:, CK - 1:], zc[:, 1, SAMP:T], 1.0, zc[:, 0, SAMP:T], ALU.add, ALU.mult).then_inc(s_ga, 1)
                dve.wait_ge(s_ga, 2 * g + 2)
                tap = iter(range(CK))

                def taps(n):
                    for _ in range(n):
                        conf_tap(next(tap))

                for q in range(4):
                    taps(2)
                    if q == 0:
                        dve.wait_ge(s_y, 6 * g + 1)
                    ssm_conv(q)
                    if q:
                        silu(q - 1)
                    if q >= 2:
                        split(4 + q)
                silu(3)
                stage1(0)
                taps(2)
                stage2(0)
                for j in range(1, 6):
                    stage1(j)
                    if j in (1, 3):
                        split(8 + j // 2)
                    if j < 5:
                        taps(2)
                        stage2(j)
                dve.wait_ge(s_z, 2 * g + 2)
                dve.wait_ge(s_ufree, U_TILES * g + 10 + 1)
                k.link(stt(zc[:, :, :], th[:, :, :], 1.0, zc[:, :, :], ALU.add, ALU.mult))
                stage2(5)
                dve.wait_ge(s_y, 6 * g + 6 + 1)
                stt(ybuf[:, :, :], ybuf[:, :, :], 0.5, zc[:, :, :], ALU.mult, ALU.mult).then_inc(s_yz, 1)
                for r in range(4):
                    dve.wait_ge(s_hs, 4 * g + r + 2)
                    dve.wait_ge(s_h0t, 4 * g + 4)
                    for b in range(4):
                        bb, i = 4 * (r % 2) + b, r // 2
                        last = stt(h0[:, i, bb, :], h0[:, i, bb, :],
                                   Ed[:, i, TSAMP * bb + TSAMP - 1:TSAMP * bb + TSAMP],
                                   (pS, pT)[r % 2][:, P * b:P * b + P])
                    last.then_inc(s_hnew, 1)
                taps(5)
                dve.wait_ge(s_ufree, U_TILES * g + 14 + 1)
                dve.reciprocal(zc[:, 1, :], zc[:, 0, :]).then_inc(s_rec, 1)
                dve.wait_ge(s_rec, g + 1)
                for i in range(2):
                    stt(yn[:, 2 * g + i, :], ybuf[:, i, :], gc[:, R_NW + i:R_NW + i + 1], zc[:, 1, :],
                        ALU.mult, ALU.mult).then_inc(s_yn, 1)
                taps(8)
                assert next(tap, None) is None
                k.leave(G)


OT = [(0, SAMP)] + CHUNKS[2:]
NT = len(OT)
ROW = [0] + [SAMP + P * t for t in range(NT - 1)]
NE, NGR, EPG, DE = 32, 4, 8, 256
SLOT = 128
PAIRS = 2 * (SAMP + SEQ)
NTILE = NE + (PAIRS - NE) // SLOT
NROW = SAMP + SEQ
MAXT = -(-(SAMP + SEQ) // SLOT)
BIG = 3.0e38


def mixer(nc, A, O, keep):
    yn, cs, x1, ones = keep["yn"], keep["cs"], keep["x1"], keep["ones"]
    with ExitStack() as ctx:
        def sb(name, shape, dt=F32):
            return ctx.enter_context(nc.sbuf_tensor(name, shape, dt))

        sem = ctx.enter_context(semaphores(nc))

        RW = 3
        aconv = sb("aconv", [P, KD, T])
        wring = sb("wring", [P, RW, 2 * D])
        wo = sb("wo", [P, KD, D])
        mg = sb("mg", [P, KD, T])
        gt = sb("gt", [P, 4, T])
        sq = sb("sq", [P, 2, T])
        mean = sb("mean", [P, T])
        rs = sb("rs", [P, T])
        rr = sb("rr", [P, T])
        ya = sb("ya", [P, 2, T])
        ss2 = sb("ss2", [P, 8])
        pm = [ctx.enter_context(nc.psum_tensor(f"pm{i}", [P, 1024], F32)) for i in range(2)]
        pst = ctx.enter_context(nc.psum_tensor("pst", [P, 1024], F32))
        po = ctx.enter_context(nc.psum_tensor("po", [P, 1024], F32))
        s_w = [sem(f"m_w{i}") for i in range(RW)]
        s_g = [sem(f"m_g{i}") for i in range(4)]
        s_wo, s_xr, s_p, s_stat, s_mean, s_cen, s_sq, s_eps, s_inv, s_root, s_tan, s_act, s_ya, s_gfree, s_mg, s_o, \
            s_x1, s_ssq, s_var, s_sd = map(sem, (
                "m_wo", "m_xr", "m_p", "m_stat", "m_mean", "m_cen", "m_sq", "m_eps", "m_inv", "m_root",
                "m_tan", "m_act", "m_ya", "m_gfree", "m_mg", "m_o", "m_x1", "m_ssq", "m_var", "m_sd"))
        s_lin, s_rinv, s_sqf, s_xs, s_ss = sem("m_lin"), sem("m_rinv"), sem("m_sqf"), sem("m_xs"), sem("m_ss")
        s_ac = sem("m_ac")
        c_dve = sem("m_dve")
        block = ctx.enter_context(nc.Block())

        def cols(ps, a, b):
            return ps[:, UO + a:UO + b]

        def unread(S):
            return gt[0:S, :, :].rearrange("p a b -> p (a b)")[:, 0:D]

        @block.sync
        def _(sp):
            sp.dma_start(aconv[:, :, :], keep["aconv"].rearrange("k p t -> p k t")).then_inc(s_ac, 16)
            for n in range(KD):
                if n >= RW:
                    sp.wait_ge(s_p, n - RW + 1)
                src = A["ssm_out_w"][0].rearrange("(k p) n -> p k n", p=P)[:, :, P * n:P * n + P]
                sp.dma_start(wring[:, n % RW, :].rearrange("p (k n) -> p k n", n=P), src).then_inc(s_w[n % RW], 16)
            for n in range(KD // 2):
                m = KD + n
                sp.wait_ge(s_p, (m - RW + 1) if m - RW < KD else KD + 2 * (m - RW - KD + 1))
                src = A["conf_out_w"][0].rearrange("(k p) n -> p k n", p=P)[:, :, 2 * P * n:2 * P * n + 2 * P]
                sp.dma_start(wring[:, m % RW, :].rearrange("p (k n) -> p k n", n=2 * P), src).then_inc(s_w[m % RW], 16)
                if n == 1:
                    sp.dma_start(wo[:, :, :], A["w_o"][0].rearrange("(k p) n -> p k n", p=P)).then_inc(s_wo, 16)
                    sp.dma_start(x1[0:SAMP, 0, :], A["x_sample"].rearrange("b t d -> (b t) d")).then_inc(s_xr, 16)
                    sp.dma_start(x1[:, 1:NT, :],
                                 A["x_prompt"][0].rearrange("(t p) d -> p t d", p=P)).then_inc(s_xr, 16)

        @block.gpsimd
        def _(pool):
            for n in range(2 * KD):
                if n >= 4:
                    pool.wait_ge(s_gfree, n - 3)
                pool.dma_start(gt[:, n % 4, :], keep["gates"][1 - n // KD, n % KD]).then_inc(s_g[n % 4], 16)

        @block.tensor
        def _(pe):
            def sum_block(bank, j, rhs):
                for a, b in ((0, USPLIT), (USPLIT, T)):
                    last = pe.matmul(cols(bank, a, b), ones[:, :], rhs[:, a:b], start=(j == 0), stop=(j == KD - 1))
                return last

            def product(r, weights, K, act, w_sem, w_val):
                if 2 <= r < KD + 2:
                    pe.wait_ge(s_gfree, r - 1)
                elif r >= KD + 2:
                    pe.wait_ge(s_ya, r - KD - 1)
                pe.wait_ge(w_sem, w_val)
                for j in range(K):
                    for a, b in ((0, USPLIT), (USPLIT, T)):
                        last = pe.matmul(cols(pm[r % 2], a, b), weights(j), act[:, j, a:b],
                                         start=(j == 0), stop=(j == K - 1))
                last.then_inc(s_p, 1)

            pe.wait_ge(s_ac, 16)
            for j in range(KD):
                last = sum_block(pst, j, aconv[:, j, :])
            last.then_inc(s_stat, 1)
            for n in range(KD):
                product(n, lambda j, n=n: wring[:, n % RW, P * j:P * j + P], 2 * KD, yn, s_w[n % RW], 16 * (n // RW + 1))
                if n == 0:
                    for j in range(KD):
                        pe.wait_ge(s_sq, j + 1)
                        sum_block(po, j, sq[:, j % 2, :]).then_inc(s_sqf, 1)
            pe.wait_ge(s_act, KD)
            for n in range(KD):
                m = KD + n // 2
                product(KD + n, lambda j, n=n, m=m: wring[:, m % RW, 2 * P * j + P * (n % 2):2 * P * j + P * (n % 2) + P],
                        KD, aconv, s_w[m % RW], 16 * (m // RW + 1))
            pe.wait_ge(s_wo, 16)
            pe.wait_ge(s_mg, KD)
            pe.wait_ge(s_ya, KD)
            for t, (c, S) in enumerate(OT):
                bank = (pm[0], pm[1], po)[t % 3]
                if t >= 3:
                    pe.wait_ge(s_x1, 2 * (t - 2))
                for h in range(2):
                    for j in range(KD):
                        last = pe.matmul(bank[0:S, 512 * h:512 * h + 512], mg[:, j, c:c + S],
                                         wo[:, j, 512 * h:512 * h + 512], start=(j == 0), stop=(j == KD - 1))
                    last.then_inc(s_o, 1)

        @block.scalar
        def _(act):
            act.wait_ge(s_stat, 1)
            act.activation(mean[:, :], cols(pst, 0, T), ACT.Copy, scale=1.0 / D).then_inc(s_mean, 1)
            for j in range(KD):
                act.wait_ge(s_cen, j + 1)
                if j >= 2:
                    act.wait_ge(s_sqf, j - 1)
                act.activation(sq[:, j % 2, :], aconv[:, j, :], ACT.Square).then_inc(s_sq, 1)
            act.wait_ge(s_inv, 1)
            act.activation(rs[:, :], rr[:, :], ACT.Sqrt).then_inc(s_root, 1)
            for j in range(KD):
                act.wait_ge(s_lin, j + 1)
                if j >= 2:
                    act.wait_ge(s_act, j - 1)
                act.activation(sq[:, j % 2, :], aconv[:, j, :], ACT.Tanh, scale=0.5).then_inc(s_tan, 1)
            for n in range(KD):
                act.wait_ge(s_p, KD + n + 1)
                if n >= 2:
                    act.wait_ge(s_mg, n - 1)
                act.activation(ya[:, n % 2, :], cols(pm[n % 2], 0, T), ACT.Identity, scale=0.5,
                               bias=cs[:, n, R_OB:R_OB + 1]).then_inc(s_ya, 1)
            act.wait_ge(s_ss, 1)
            for t, (c, S) in enumerate(OT):
                act.wait_ge(s_x1, 2 * t + 2)
                if t:
                    act.wait_ge(s_ssq, t)
                act.activation(unread(S), x1[0:S, t, :], ACT.Square, accum_out=ss2[0:S, t:t + 1]).then_inc(s_ssq, 1)
            act.wait_ge(s_var, 1)
            act.activation(ss2[:, 0:NT], ss2[:, 0:NT], ACT.Sqrt).then_inc(s_sd, 1)

        @block.vector
        def _(dve):
            k = Steps(dve, c_dve)

            def stt(out, in0, scalar, in1, op0=ALU.mult, op1=ALU.add):
                return dve.scalar_tensor_tensor(out=out, in0=in0, scalar=scalar, in1=in1, op0=op0, op1=op1)

            dve.memset(ss2[:, :], 1.0).then_inc(s_ss, 1)
            dve.wait_ge(s_mean, 1)
            for j in range(KD):
                dve.tensor_tensor(aconv[:, j, :], aconv[:, j, :], mean[:, :], ALU.subtract).then_inc(s_cen, 1)
            dve.wait_ge(s_sqf, KD)
            k.link(dve.tensor_scalar(rs[:, :], cols(po, 0, T), 1.0 / D, EPS, ALU.mult, ALU.add))
            dve.reciprocal(rr[:, :], rs[:, :]).then_inc(s_inv, 1)
            dve.wait_ge(s_root, 1)

            def ssm_block(n):
                dve.wait_ge(s_p, n + 1)
                dve.wait_ge(s_g[n % 4], 16 * (n // 4 + 1))
                stt(mg[:, n, :], gt[:, n % 4, :], 1.0, cols(pm[n % 2], 0, T), ALU.add, ALU.mult).then_inc(s_gfree, 1)

            for j in range(KD):
                k.link(stt(aconv[:, j, :], aconv[:, j, :], cs[:, j, R_LG:R_LG + 1], rs[:, :], ALU.mult, ALU.mult))
                dve.tensor_scalar(aconv[:, j, :], aconv[:, j, :], cs[:, j, R_LB:R_LB + 1], None,
                                  ALU.add).then_inc(s_lin, 1)
                if j:
                    dve.wait_ge(s_tan, j)
                    stt(aconv[:, j - 1, :], sq[:, (j - 1) % 2, :], 1.0, aconv[:, j - 1, :],
                        ALU.add, ALU.mult).then_inc(s_act, 1)
                if j % 2 == 1:
                    ssm_block(j // 2)
            dve.wait_ge(s_tan, KD)
            stt(aconv[:, KD - 1, :], sq[:, (KD - 1) % 2, :], 1.0, aconv[:, KD - 1, :],
                ALU.add, ALU.mult).then_inc(s_act, 1)
            for n in range(KD // 2, KD):
                ssm_block(n)
            for n in range(KD):
                dve.wait_ge(s_ya, n + 1)
                m = KD + n
                dve.wait_ge(s_g[m % 4], 16 * (m // 4 + 1))
                k.link(stt(ya[:, n % 2, :], gt[:, m % 4, :], 1.0, ya[:, n % 2, :], ALU.add, ALU.mult))
                dve.sem_inc(s_gfree, 1)
                dve.wait_ge(s_gfree, KD)
                dve.tensor_tensor(mg[:, n, :], mg[:, n, :], ya[:, n % 2, :], ALU.add).then_inc(s_mg, 1)
            dve.wait_ge(s_xr, 32)
            for t, (c, S) in enumerate(OT):
                bank = (pm[0], pm[1], po)[t % 3]
                for h in range(2):
                    dve.wait_ge(s_o, 2 * t + h + 1)
                    v = x1[0:S, t, 512 * h:512 * h + 512]
                    stt(v, bank[0:S, 512 * h:512 * h + 512], 0.5, v).then_inc(s_x1, 1)
            dve.wait_ge(s_ssq, NT)
            dve.tensor_scalar(ss2[:, 0:NT], ss2[:, 0:NT], 1.0 / D, EPS, ALU.mult, ALU.add).then_inc(s_var, 1)
            dve.wait_ge(s_sd, 1)
            dve.reciprocal(keep["rstd"][:, 0:NT], ss2[:, 0:NT]).then_inc(s_rinv, 1)


def route(nc, A, O, keep):
    x1, ident, ones, pos, wgt = (keep[n] for n in ("x1", "ident", "ones", "pos", "wgt"))
    with ExitStack() as ctx:
        def sb(name, shape, dt=F32):
            return ctx.enter_context(nc.sbuf_tensor(name, shape, dt))

        sem = ctx.enter_context(semaphores(nc))

        NL = NGR + NE
        xs = sb("xs", [P, 2, D])
        nw = sb("nw", [P, D])
        xT = sb("xT", [P, 2, KD, P])
        wr = sb("wr", [P, KD, NL])
        rb = sb("rb", [P, NL])
        lg = sb("lg", [P, NT, NL])
        gm = sb("gm", [P, NT])
        sg = sb("sg", [P, NT, NGR])
        eqg = sb("eqg", [P, NT, NGR])
        og = sb("og", [P, NT, NGR])
        gp = sb("gp", [P, NT])
        ei = sb("ei", [P, NT, EPG])
        et = sb("et", [P, NT, EPG])
        m12 = sb("m12", [P, 2, NT])
        sc = sb("sc", [P, NT, EPG])
        ok = sb("ok", [P, 2, NT, EPG])
        rank = sb("rank", [P, EPG])
        valid = sb("valid", [P, NT])
        OH = sb("OH", [P, 2, NT, NE])
        pre = sb("pre", [P, 2 * NT, NE])
        run = sb("run", [P, 2 * NT + 1, NE])
        ntl = sb("ntl", [P, NE])
        tend = sb("tend", [P, NE])
        base = sb("base", [P, NE])
        zer = sb("zer", [P, NE])
        posf = sb("posf", [P, 2 * NT])
        ti = sb("ti", [1, NTILE])
        cmp = sb("cmp", [1, NTILE, NE])
        exf = sb("exf", [1, NTILE])
        SU = sb("SU", [P, P])
        tokid = sb("tokid", [P, NT], U32)
        zu = sb("zu", [NTILE, P], U32)
        srow = sb("srow", [NTILE, P], U32)
        srowf = sb("srowf", [NTILE, P])
        px = [ctx.enter_context(nc.psum_tensor(f"rx{i}", [P, 512], F32)) for i in range(2)]
        pl, pc, pt = (ctx.enter_context(nc.psum_tensor(n, [P, 512], F32)) for n in ("rl", "rc", "rt"))
        pc2 = ctx.enter_context(nc.psum_tensor("rc2", [P, 512], F32))
        s_wr, s_rb, s_cst, s_id, s_xs, s_t, s_tf, s_l, s_lg, s_e, s_x, s_oh, s_cnt, s_pos, s_z, s_sct, s_row, s_rowf, \
            s_rt, s_done, s_tok = map(sem, (
                "r_wr", "r_rb", "r_cst", "r_id", "r_xs", "r_t", "r_tf", "r_l", "r_lg", "r_e", "r_x", "r_oh",
                "r_cnt", "r_pos", "r_z", "r_sct", "r_row", "r_rowf", "r_rt", "r_done", "r_tok"))
        s_nw = sem("r_nw")
        s_xst = [sem(f"r_xst{b}") for b in range(2)]
        c_dve, c_pool = sem("r_dve"), sem("r_pool")
        block = ctx.enter_context(nc.Block())

        @block.sync
        def _(sp):
            sp.dma_start(nw[:, :], A["norm_ffn_w"][0].partition_broadcast(P)).then_inc(s_nw, 16)
            for a, b, w, bias in ((0, NGR, A["router_group_w"], A["router_group_b"]),
                                  (NGR, NL, A["router_expert_w"], A["router_expert_b"])):
                sp.dma_start(wr[:, :, a:b], w[0].rearrange("(k p) n -> p k n", p=P)).then_inc(s_wr, 16)
                sp.dma_start(rb[:, a:b], bias[0].partition_broadcast(P)).then_inc(s_rb, 16)
            for t, (c, S) in enumerate(OT):
                sp.wait_ge(s_xs, t + 1)
                sp.dma_start(keep["xs"][ROW[t]:ROW[t] + S, :], xs[0:S, t % 2, :]).then_inc(s_xst[t % 2], 16)
            for b in range(2):
                sp.wait_ge(s_xst[b], 16 * ((NT + 1 - b) // 2))

        @block.gpsimd
        def _(pool):
            k = Steps(pool, c_pool)
            pool.iota(rank[:, :], [[-1, EPG]], base=EPG, channel_multiplier=0, allow_small_or_imprecise_dtypes=True).then_inc(s_cst, 1)
            pool.iota(ti[:, :], [[1, NTILE]], base=0, channel_multiplier=0, allow_small_or_imprecise_dtypes=True).then_inc(s_cst, 1)
            pool.iota(tokid[:, 0:1], [[0, 1]], base=0, channel_multiplier=1).then_inc(s_cst, 1)
            pool.iota(tokid[:, 1:NT], [[P, NT - 1]], base=ROW[1], channel_multiplier=1).then_inc(s_cst, 1)
            k.link(pool.memset(valid[:, :], 1.0))
            pool.affine_select(out=valid[:, 0:1], in_=valid[:, 0:1], compare_op=ALU.is_ge, fill=0.0,
                               base=SAMP - 1, pattern=[[0, 1]], channel_multiplier=-1).then_inc(s_cst, 1)
            k.link(pool.memset(SU[:, :], 1.0))
            pool.affine_select(out=SU[:, :], in_=SU[:, :], compare_op=ALU.is_gt, fill=0.0, base=0,
                               pattern=[[1, P]], channel_multiplier=-1).then_inc(s_cst, 1)
            pool.memset(lg[:, 0, :], 0.0).then_inc(s_cst, 1)
            pool.memset(zer[:, :], 0.0).then_inc(s_cst, 1)
            k.link(pool.memset(zu[:, :], NROW))
            pool.dma_start(keep["slots"].rearrange("(i p) o -> i (p o)", p=P), zu[:, :]).then_inc(s_z, 16)
            pool.wait_ge(s_z, 16)
            pool.wait_ge(s_cst, 8)
            pool.wait_ge(s_pos, 1)
            for q in range(2):
                for t, (c, S) in enumerate(OT):
                    pool.indirect_dma_start(
                        out=keep["slots"], out_offset=bass.IndirectOffsetOnAxis(ap=pos[0:S, NT * q + t:NT * q + t + 1], axis=0),
                        in_=tokid[0:S, t:t + 1], in_offset=None).then_inc(s_sct, 16)
            pool.wait_ge(s_sct, 16 * 2 * NT)
            pool.dma_start(srow[:, :], keep["slots"].rearrange("(i p) o -> i (p o)", p=P)).then_inc(s_row, 16)

        @block.tensor
        def _(pe):
            for t, (c, S) in enumerate(OT):
                pe.wait_ge(s_xs, t + 1)
                for h in range(2):
                    n = 2 * t + h
                    if n >= 2:
                        pe.wait_ge(s_tf, n - 1)
                    for q in range(4):
                        last = pe.transpose(px[n % 2][:, P * q:P * q + S], xs[0:S, t % 2, P * (4 * h + q):P * (4 * h + q) + P],
                                            ident[0:S, 0:S])
                    last.then_inc(s_t, 1)
                pe.wait_ge(s_tf, 2 * t + 2)
                pe.wait_ge(s_wr, 32)
                for j in range(KD):
                    last = pe.matmul(pl[0:S, NL * t:NL * t + NL], xT[:, t % 2, j, 0:S], wr[:, j, :],
                                     start=(j == 0), stop=(j == KD - 1))
                last.then_inc(s_l, 1)
            pe.wait_ge(s_oh, 1)
            pe.wait_ge(s_cst, 8)
            ohv = OH[:, :, :, :].rearrange("p a t e -> p (a t e)")
            pe.matmul(pc[:, 0:2 * NT * NE], SU[:, :], ohv, start=True, stop=True)
            pe.matmul(pc2[:, 0:2 * NT * NE], ones[:, :], ohv, start=True, stop=True).then_inc(s_cnt, 1)
            pe.wait_ge(s_rowf, 1)
            pe.transpose(pt[:, 0:NTILE], srowf[:, :], ident[0:NTILE, 0:NTILE]).then_inc(s_rt, 1)

        @block.scalar
        def _(act):
            act.wait_ge(s_e, 1)
            act.activation(sg[:, :, :], sg[:, :, :], ACT.Exp).then_inc(s_x, 1)
            act.activation(gp[:, :], gp[:, :], ACT.Exp).then_inc(s_x, 1)

        @block.vector
        def _(dve):
            k = Steps(dve, c_dve)

            def tt(out, a, b, op):
                k.link(dve.tensor_tensor(out, a, b, op))

            def stt(out, in0, scalar, in1, op0=ALU.mult, op1=ALU.add):
                k.link(dve.scalar_tensor_tensor(out=out, in0=in0, scalar=scalar, in1=in1, op0=op0, op1=op1))

            def red(out, in_, op):
                k.link(dve.tensor_reduce(out, in_, AX_X, op))

            def normed(t):
                S = OT[t][1]
                if t >= 2:
                    dve.wait_ge(s_xst[t % 2], 16 * (t // 2))
                    dve.wait_ge(s_t, 2 * t - 2)
                dve.scalar_tensor_tensor(out=xs[0:S, t % 2, :], in0=x1[0:S, t, :], scalar=keep["rstd"][0:S, t:t + 1],
                                         in1=nw[0:S, :], op0=ALU.mult, op1=ALU.mult).then_inc(s_xs, 1)

            dve.wait_ge(s_nw, 16)
            normed(0)
            for t, (c, S) in enumerate(OT):
                if t + 1 < NT:
                    normed(t + 1)
                for h in range(2):
                    n = 2 * t + h
                    dve.wait_ge(s_t, n + 1)
                    if t >= 2:
                        dve.wait_ge(s_l, t - 1)
                    dve.tensor_copy(xT[:, t % 2, 4 * h:4 * h + 4, 0:S],
                                    px[n % 2][:, :].rearrange("p (q s) -> p q s", q=4)[:, :, 0:S]).then_inc(s_tf, 1)
            dve.wait_ge(s_rb, 32)
            dve.wait_ge(s_l, NT)
            dve.wait_ge(s_cst, 8)
            for t, (c, S) in enumerate(OT):
                tt(lg[0:S, t, :], pl[0:S, NL * t:NL * t + NL], rb[0:S, :], ALU.add)

            def bc(ap, n):
                return ap.unsqueeze(2).broadcast_to([P, NT, n])

            def first_of(onehot, equal, n):
                r = rank[:, EPG - n:EPG].unsqueeze(1).broadcast_to([P, NT, n])
                tt(equal, equal, r, ALU.mult)
                red(gm[:, :], equal, ALU.max)
                tt(onehot, equal, bc(gm[:, :], n), ALU.is_equal)

            g = lg[:, :, 0:NGR]
            red(gm[:, :], g, ALU.max)
            tt(sg[:, :, :], g, bc(gm[:, :], NGR), ALU.subtract)
            tt(eqg[:, :, :], g, bc(gm[:, :], NGR), ALU.is_equal)
            first_of(og[:, :, :], eqg[:, :, :], NGR)
            for q in range(NGR):
                e = lg[:, :, NGR + EPG * q:NGR + EPG * q + EPG]
                if q == 0:
                    tt(ei[:, :, :], e, bc(og[:, :, q], EPG), ALU.mult)
                else:
                    tt(et[:, :, :], e, bc(og[:, :, q], EPG), ALU.mult)
                    tt(ei[:, :, :], ei[:, :, :], et[:, :, :], ALU.add)
            red(m12[:, 0, :], ei[:, :, :], ALU.max)
            tt(sc[:, :, :], ei[:, :, :], bc(m12[:, 0, :], EPG), ALU.is_equal)
            first_of(ok[:, 0], sc[:, :, :], EPG)
            stt(ei[:, :, :], ok[:, 0], -BIG, ei[:, :, :])
            red(m12[:, 1, :], ei[:, :, :], ALU.max)
            tt(sc[:, :, :], ei[:, :, :], bc(m12[:, 1, :], EPG), ALU.is_equal)
            first_of(ok[:, 1], sc[:, :, :], EPG)
            dve.tensor_tensor(gp[:, :], m12[:, 1, :], m12[:, 0, :], ALU.subtract).then_inc(s_e, 1)
            for q in range(2):
                for b in range(NGR):
                    tt(OH[:, q, :, EPG * b:EPG * b + EPG], ok[:, q], bc(og[:, :, b], EPG), ALU.mult)
                tt(OH[:, q], OH[:, q], bc(valid[:, :], NE), ALU.mult)
            dve.sem_inc(s_oh, 1)
            dve.wait_ge(s_x, 2)
            red(gm[:, :], sg[:, :, :], ALU.add)
            stt(gm[:, :], gp[:, :], 1.0, gm[:, :], ALU.add, ALU.mult)
            k.link(dve.reciprocal(wgt[:, 0, :], gm[:, :]))
            k.link(dve.tensor_scalar(wgt[:, 0, :], wgt[:, 0, :], 0.5, None, ALU.mult))
            tt(wgt[:, 1, :], wgt[:, 0, :], gp[:, :], ALU.mult)
            dve.wait_ge(s_cnt, 1)
            k.link(dve.memset(run[:, 0, :], 0.0))
            for n in range(2 * NT):
                tt(run[:, n + 1, :], run[:, n, :], pc2[:, NE * n:NE * n + NE], ALU.add)
            cnt = run[:, 2 * NT, :]
            k.link(dve.tensor_scalar(ntl[:, :], cnt, 0.0, None, ALU.is_gt))
            for n in range(1, MAXT):
                stt(ntl[:, :], cnt, float(SLOT * n), ntl[:, :], ALU.is_gt, ALU.add)
            k.link(dve.tensor_tensor_scan(tend[:, :], ntl[:, :], zer[:, :], 0.0, ALU.add, ALU.add))
            tt(base[:, :], tend[:, :], ntl[:, :], ALU.subtract)
            k.link(dve.tensor_scalar(base[:, :], base[:, :], float(SLOT), None, ALU.mult))
            tt(pre[:, :, :], run[:, 0:2 * NT, :], pc[:, 0:2 * NT * NE].rearrange("p (n e) -> p n e", e=NE), ALU.add)
            tt(pre[:, :, :], pre[:, :, :], base[:, :].unsqueeze(1).broadcast_to([P, 2 * NT, NE]), ALU.add)
            tt(pre[:, :, :], pre[:, :, :], OH[:, :, :, :].rearrange("p a t e -> p (a t) e"), ALU.mult)
            red(posf[:, :], pre[:, :, :], ALU.add)
            dve.tensor_copy(pos[:, :], posf[:, :]).then_inc(s_pos, 1)
            tt(cmp[:, :, :], ti[:, :].unsqueeze(2).broadcast_to([1, NTILE, NE]),
               tend[0:1, :].unsqueeze(1).broadcast_to([1, NTILE, NE]), ALU.is_ge)
            red(exf[:, :], cmp[:, :, :], ALU.add)
            k.link(dve.tensor_scalar(exf[:, :], exf[:, :], float(NE - 1), None, ALU.min))
            dve.tensor_copy(keep["expert"][:, :], exf[:, :]).then_inc(s_done, 1)
            dve.wait_ge(s_row, 16)
            dve.tensor_copy(srowf[:, :], srow[:, :]).then_inc(s_rowf, 1)
            dve.wait_ge(s_rt, 1)
            dve.tensor_copy(keep["tok"][:, :], pt[:, 0:NTILE]).then_inc(s_tok, 1)


def experts(nc, A, O, keep):
    ident = keep["ident"]
    with ExitStack() as ctx:
        def sb(name, shape, dt=F32):
            return ctx.enter_context(nc.sbuf_tensor(name, shape, dt))

        sem = ctx.enter_context(semaphores(nc))

        W13 = sb("W13", [P, 2, 2, KD * DE])
        W2 = sb("W2", [P, 2, 2 * D])
        W13h, W13l = sb("W13h", [P, 2, KD, 2 * DE], F32R), sb("W13l", [P, 2, KD, 2 * DE], F32R)
        W2h, W2l = sb("W2h", [P, 2, DE // P, D], F32R), sb("W2l", [P, 2, DE // P, D], F32R)
        xg = sb("xg", [P, 2, D])
        xh, xl = sb("xgh", [P, 2, D], F32R), sb("xgl", [P, 2, D], F32R)
        ix = sb("ix", [P, 2], U32)
        thh = sb("thh", [P, DE])
        ac = sb("ac", [P, 2, DE])
        ah, al = sb("ah", [P, 2, DE], F32R), sb("al", [P, 2, DE], F32R)
        yo = sb("yo", [P, 2, D])
        px = ctx.enter_context(nc.psum_tensor("ex", [P, 1024], F32))
        ph = [ctx.enter_context(nc.psum_tensor(f"eh{i}", [P, 512], F32)) for i in range(2)]
        pa = ctx.enter_context(nc.psum_tensor("ea", [P, 512], F32))
        py = ctx.enter_context(nc.psum_tensor("ey", [P, 1024], F32))
        s_w13 = [sem(f"e_w13{b}") for b in range(2)]
        s_w2 = [sem(f"e_w2{b}") for b in range(2)]
        s_xg = [sem(f"e_xg{b}") for b in range(2)]
        s_yst = [sem(f"e_yst{b}") for b in range(2)]
        s_ix, s_zero, s_t, s_xh, s_xl, s_h, s_th, s_s, s_act, s_at, s_ah, s_al, s_y, s_yev = map(sem, (
            "e_ix", "e_zero", "e_t", "e_xh", "e_xl", "e_h", "e_th", "e_s", "e_act", "e_at", "e_ah", "e_al", "e_y", "e_yev"))
        s_wh, s_wl, s_w2h, s_w2l = map(sem, ("e_wh", "e_wl", "e_w2h", "e_w2l"))
        s_settled = sem("e_settled")
        block = ctx.enter_context(nc.Block())
        CH, CH2 = 4, 2
        KC = KD // CH
        started = [(s, 2) for s in (s_t, s_xh, s_xl, s_h, s_th, s_act, s_at, s_ah, s_al, s_y, s_yev)]
        started += [(s_wh, 2 * CH), (s_wl, 2 * CH), (s_w2h, 2 * CH2), (s_w2l, 2 * CH2)]

        def finished(i, each=1):
            return each * (i + 3)

        def loads(i, b):
            return 16 * ((i - b) // 2 + 1) if isinstance(i, int) else 8 * (i - b) + 16

        def tiles(eng, step):
            for i in range(3):
                step(i, i % 2)
            with eng.Fori(0, NTILE // 2 - 2) as ii:
                step(2 * ii + 3, 1)
                step(2 * ii + 4, 0)
            step(NTILE - 1, 1)

        def w13_part(b, c):
            return W13[:, b].rearrange("p a (k f) -> p a k f", k=KD)[:, :, KC * c:KC * c + KC, :]

        def is_last(i):
            return isinstance(i, int) and i == NTILE - 1

        def is_first(i):
            return isinstance(i, int) and i == 0

        @block.sync
        def _(sp):
            def expert(i):
                return sp.value_load(keep["expert"][0:1, bass.ds(i, 1)], min_val=0, max_val=NE - 1)

            def up(i, b):
                e = expert(i)
                if not isinstance(i, int):
                    sp.wait_ge(s_wl, finished(i - 2, CH))
                for a, w in ((0, A["exp_w1"]), (1, A["exp_w3"])):
                    sp.dma_start(W13[:, b, a], w[0][e].rearrange("(p k) f -> p (k f)", p=P)).then_inc(s_w13[b], 16)

            def down(i, b):
                e = expert(i)
                sp.wait_ge(s_w2l, finished(i - 2, CH2))
                sp.dma_start(W2[:, b], A["exp_w2"][0][e].rearrange("(p k) d -> p (k d)", p=P)).then_inc(s_w2[b], 16)

            up(0, 0)
            up(1, 1)
            with sp.Fori(0, NTILE // 2 - 1) as ii:
                for b in range(2):
                    down(2 * ii + b, b)
                    up(2 * ii + 2 + b, b)
            down(NTILE - 2, 0)
            down(NTILE - 1, 1)

        @block.gpsimd
        def _(pool):
            for s, n in started:
                pool.sem_inc(s, n)
            pool.memset(xg[:, :, :], 0.0).then_inc(s_zero, 1)
            pool.wait_ge(s_zero, 1)

            def gather(i, b):
                if not isinstance(i, int):
                    pool.wait_ge(s_t, finished(i - 2))
                    pool.sem_inc(s_settled, 1)
                pool.tensor_copy(ix[:, b:b + 1], keep["tok"][:, bass.ds(i, 1)]).then_inc(s_ix, 1)
                pool.wait_ge(s_ix, i + 1)
                pool.sem_inc(s_settled, 1)
                pool.indirect_dma_start(out=xg[:, b, :], out_offset=None, in_=keep["xs"], bounds_check=NROW - 1,
                                        oob_is_err=False,
                                        in_offset=bass.IndirectOffsetOnAxis(ap=ix[:, b:b + 1], axis=0))\
                    .then_inc(s_xg[b], 16)

            gather(0, 0)
            gather(1, 1)
            with pool.Fori(0, NTILE // 2 - 1) as ii:
                for b in range(2):
                    gather(2 * ii + 2 + b, b)

        @block.tensor
        def _(pe):
            def turn(i, b):
                pe.wait_ge(s_xg[b], loads(i, b))
                pe.wait_ge(s_xl, finished(i - 1))
                for q in range(KD):
                    last = pe.transpose(px[:, P * q:P * q + P], xg[:, b, :].rearrange("s (p k) -> s k p", k=KD)[:, q, :], ident[:, :])
                last.then_inc(s_t, 1)

            def up(i, b):
                pe.wait_ge(s_xl, finished(i))
                pe.wait_ge(s_act, finished(i - 2))
                for c in range(CH):
                    pe.wait_ge(s_wl, finished(i - 1, CH) + c + 1)
                    for j in range(KC * c, KC * c + KC):
                        for n, (x, w) in enumerate(((xh, W13h), (xl, W13h), (xh, W13l))):
                            last = pe.matmul(ph[b][:, :], x[:, b, P * j:P * j + P], w[:, b, j, :],
                                             start=(j == 0 and n == 0), stop=(j == KD - 1 and n == 2))
                last.then_inc(s_h, 1)

            def turn_act(i, b):
                pe.wait_ge(s_act, finished(i))
                pe.wait_ge(s_al, finished(i - 1))
                for q in range(2):
                    last = pe.transpose(pa[:, P * q:P * q + P], ac[:, b, :].rearrange("s (p k) -> s k p", k=2)[:, q, :], ident[:, :])
                last.then_inc(s_at, 1)

            def down(i, b):
                pe.wait_ge(s_al, finished(i))
                pe.wait_ge(s_yev, finished(i - 1))
                pe.wait_ge(s_w2l, finished(i, CH2))
                for h in range(2):
                    for q in range(2):
                        for n, (x, w) in enumerate(((ah, W2h), (al, W2h), (ah, W2l))):
                            last = pe.matmul(py[:, 512 * h:512 * h + 512], x[:, b, P * q:P * q + P],
                                             w[:, b, q, 512 * h:512 * h + 512],
                                             start=(q == 0 and n == 0), stop=(q == 1 and n == 2))
                last.then_inc(s_y, 1)

            def step(i, b):
                up(i, b)
                if not is_last(i):
                    turn(i + 1, 1 - b)
                if not is_first(i):
                    down(i - 1, 1 - b)
                turn_act(i, b)

            turn(0, 0)
            tiles(pe, step)
            down(NTILE - 1, 1)

        @block.scalar
        def _(act):
            def split_up(i, b):
                act.wait_ge(s_w13[b], 2 * loads(i, b))
                act.wait_ge(s_h, finished(i - 2))
                for c in range(CH):
                    act.activation(W13h[:, b, KC * c:KC * c + KC, :].rearrange("p k (a f) -> p a k f", a=2),
                                   w13_part(b, c), ACT.Copy).then_inc(s_wh, 1)

            def split_down(i, b):
                act.wait_ge(s_w2[b], loads(i, b))
                act.wait_ge(s_y, finished(i - 2))
                for c in range(CH2):
                    act.activation(W2h[:, b, c, :], W2[:, b, D * c:D * c + D], ACT.Copy).then_inc(s_w2h, 1)

            def rows(i, b):
                act.wait_ge(s_t, finished(i))
                act.wait_ge(s_h, finished(i - 2))
                act.activation(xh[:, b, :], px[:, :], ACT.Copy).then_inc(s_xh, 1)

            def store(i, b):
                act.wait_ge(s_y, finished(i))
                if not isinstance(i, int) or i >= 2:
                    act.wait_ge(s_yst[b], loads(i, b) - 16)
                act.activation(yo[:, b, :], py[:, :], ACT.Copy).then_inc(s_yev, 1)
                act.wait_ge(s_yev, finished(i))
                act.dma_start(keep["ysc"].rearrange("(i p) d -> i p d", p=P)[i], yo[:, b, :]).then_inc(s_yst[b], 16)

            def step(i, b):
                if not is_last(i):
                    split_up(i + 1, 1 - b)
                act.wait_ge(s_h, finished(i))
                act.wait_ge(s_act, finished(i - 1))
                act.activation(thh[:, :], ph[b][:, 0:DE], ACT.Tanh, scale=0.5).then_inc(s_th, 1)
                split_down(i, b)
                if not is_last(i):
                    rows(i + 1, 1 - b)
                if not is_first(i):
                    store(i - 1, 1 - b)
                act.wait_ge(s_at, finished(i))
                act.wait_ge(s_y, finished(i - 2))
                act.activation(ah[:, b, :], pa[:, 0:DE], ACT.Copy).then_inc(s_ah, 1)

            split_up(0, 0)
            rows(0, 0)
            tiles(act, step)
            store(NTILE - 1, 1)
            for b in range(2):
                act.wait_ge(s_yst[b], 16 * (NTILE // 2))

        @block.vector
        def _(dve):
            def low(out, whole, high):
                return dve.tensor_tensor(out, whole, high.bitcast(F32), ALU.subtract)

            def split_up(i, b):
                dve.wait_ge(s_h, finished(i - 2))
                for c in range(CH):
                    dve.wait_ge(s_wh, finished(i - 1, CH) + c + 1)
                    l, h = (w[:, b, KC * c:KC * c + KC, :].rearrange("p k (a f) -> p a k f", a=2) for w in (W13l, W13h))
                    low(l, w13_part(b, c), h).then_inc(s_wl, 1)

            def split_down(i, b):
                dve.wait_ge(s_y, finished(i - 2))
                for c in range(CH2):
                    dve.wait_ge(s_w2h, finished(i - 1, CH2) + c + 1)
                    low(W2l[:, b, c, :], W2[:, b, D * c:D * c + D], W2h[:, b, c, :]).then_inc(s_w2l, 1)

            def rows(i, b):
                dve.wait_ge(s_xh, finished(i))
                dve.wait_ge(s_h, finished(i - 2))
                low(xl[:, b, :], px[:, :], xh[:, b, :]).then_inc(s_xl, 1)

            def step(i, b):
                if not is_last(i):
                    split_up(i + 1, 1 - b)
                dve.wait_ge(s_th, finished(i))
                dve.wait_ge(s_at, finished(i - 2))
                dve.scalar_tensor_tensor(out=ac[:, b, :], in0=thh[:, :], scalar=1.0, in1=ph[b][:, 0:DE],
                                         op0=ALU.add, op1=ALU.mult).then_inc(s_s, 1)
                dve.wait_ge(s_s, i + 1)
                dve.tensor_tensor(ac[:, b, :], ac[:, b, :], ph[b][:, DE:2 * DE], ALU.mult).then_inc(s_act, 1)
                split_down(i, b)
                if not is_last(i):
                    rows(i + 1, 1 - b)
                dve.wait_ge(s_ah, finished(i))
                dve.wait_ge(s_y, finished(i - 2))
                low(al[:, b, :], pa[:, 0:DE], ah[:, b, :]).then_inc(s_al, 1)

            split_up(0, 0)
            rows(0, 0)
            tiles(dve, step)


def finish(nc, A, O, keep):
    x1, pos, wgt = keep["x1"], keep["pos"], keep["wgt"]
    with ExitStack() as ctx:
        def sb(name, shape, dt=F32):
            return ctx.enter_context(nc.sbuf_tensor(name, shape, dt))

        sem = ctx.enter_context(semaphores(nc))

        ye = sb("ye", [P, 2 * NT, D])
        nf = sb("nf", [P, D])
        junk = sb("junk", [P, D])
        ssf = sb("ssf", [P, NT])
        rsf = sb("rsf", [P, NT])
        s_nf, s_x2, s_sum, s_var, s_sd, s_out, s_st = map(sem, ("f_nf", "f_x2", "f_sum", "f_var", "f_sd", "f_out", "f_st"))
        s_ye = [sem(f"f_ye{n}") for n in range(2 * NT)]
        c_dve = sem("f_dve")
        block = ctx.enter_context(nc.Block())

        @block.sync
        def _(sp):
            sp.dma_start(nf[:, :], A["norm_final_w"].partition_broadcast(P)).then_inc(s_nf, 16)
            for t, (c, S) in enumerate(OT):
                sp.wait_ge(s_out, t + 1)
                dst = (O["y_sample"].rearrange("b t d -> (b t) d") if t == 0
                       else O["y_prompt"][0][P * (t - 1):P * t, :])
                sp.dma_start(dst, x1[0:S, t, :]).then_inc(s_st, 16)
            sp.wait_ge(s_st, 16 * NT)

        @block.gpsimd
        def _(pool):
            for t, (c, S) in enumerate(OT):
                for q in range(2):
                    n = NT * q + t
                    pool.indirect_dma_start(out=ye[0:S, n, :], out_offset=None, in_=keep["ysc"],
                                            in_offset=bass.IndirectOffsetOnAxis(ap=pos[0:S, n:n + 1], axis=0))\
                        .then_inc(s_ye[n], 16)

        @block.scalar
        def _(act):
            for t, (c, S) in enumerate(OT):
                act.wait_ge(s_x2, t + 1)
                if t:
                    act.wait_ge(s_sum, t)
                act.activation(junk[0:S, :], x1[0:S, t, :], ACT.Square, accum_out=ssf[0:S, t:t + 1]).then_inc(s_sum, 1)
            for t, (c, S) in enumerate(OT):
                act.wait_ge(s_var, t + 1)
                act.activation(ssf[0:S, t:t + 1], ssf[0:S, t:t + 1], ACT.Sqrt).then_inc(s_sd, 1)

        @block.vector
        def _(dve):
            k = Steps(dve, c_dve)
            for t, (c, S) in enumerate(OT):
                for q in range(2):
                    dve.wait_ge(s_ye[NT * q + t], 16)
                    ins = dve.scalar_tensor_tensor(out=x1[0:S, t, :], in0=ye[0:S, NT * q + t, :],
                                                   scalar=wgt[0:S, q, t:t + 1], in1=x1[0:S, t, :],
                                                   op0=ALU.mult, op1=ALU.add)
                    if q:
                        ins.then_inc(s_x2, 1)
                    else:
                        k.link(ins)
            for t, (c, S) in enumerate(OT):
                dve.wait_ge(s_sum, t + 1)
                dve.tensor_scalar(ssf[0:S, t:t + 1], ssf[0:S, t:t + 1], 1.0 / D, EPS, ALU.mult, ALU.add).then_inc(s_var, 1)
            dve.wait_ge(s_nf, 16)
            for t, (c, S) in enumerate(OT):
                dve.wait_ge(s_sd, t + 1)
                k.link(dve.reciprocal(rsf[0:S, t:t + 1], ssf[0:S, t:t + 1]))
                dve.scalar_tensor_tensor(out=x1[0:S, t, :], in0=x1[0:S, t, :], scalar=rsf[0:S, t:t + 1],
                                         in1=nf[0:S, :], op0=ALU.mult, op1=ALU.mult).then_inc(s_out, 1)


_OUTS = [("y_prompt", (1, SEQ, D)), ("y_sample", (NSAMP, TSAMP, D)), ("new_conf_prompt", (1, 1, CK - 1, D)),
         ("new_sconv_prompt", (1, 1, SK - 1, 4 * D)), ("new_ssm_prompt", (1, 1, NH, HD, N)),
         ("new_conf_sample", (1, NSAMP, CK - 1, D)), ("new_sconv_sample", (1, NSAMP, SK - 1, 4 * D)),
         ("new_ssm_sample", (1, NSAMP, NH, HD, N))]


def program(nc, A, O):
    with ExitStack() as ctx:
        def sb(name, shape, dt=F32):
            return ctx.enter_context(nc.sbuf_tensor(name, shape, dt))

        keep = {"gates": nc.dram_tensor("gates", (2, KD, P, T), F32, kind="Internal").ap(),
                "aconv": nc.dram_tensor("conv_rows", (KD, P, T), F32, kind="Internal").ap(),
                "xs": nc.dram_tensor("xs_rows", (SAMP + SEQ, D), F32, kind="Internal").ap(),
                "slots": nc.dram_tensor("slots", (NTILE * SLOT, 1), U32, kind="Internal").ap(),
                "ysc": nc.dram_tensor("slot_rows", (NTILE * SLOT, D), F32, kind="Internal").ap()}
        keep["x1"], keep["rstd"] = sb("x1", [P, NT, D]), sb("rstd", [P, 8])
        keep["ident"], keep["ones"] = sb("ident", [P, P]), sb("ones", [P, P])
        with ExitStack() as inner:
            for name, shape in (("yn", [P, 2 * KD, T]), ("cs", [P, KD, NR])):
                keep[name] = inner.enter_context(nc.sbuf_tensor(name, shape, F32))
            trunk(nc, A, O, keep)
            mixer(nc, A, O, keep)
        keep["pos"], keep["wgt"] = sb("pos", [P, 2 * NT], U32), sb("wgt", [P, 2, NT])
        keep["expert"], keep["tok"] = sb("expert", [1, NTILE], U32), sb("tok", [P, NTILE], U32)
        route(nc, A, O, keep)
        experts(nc, A, O, keep)
        finish(nc, A, O, keep)


def kernel(**inputs):
    import numpy as _np
    import concourse.bacc as _bacc
    from concourse import mybir as _mybir
    from concourse.bass_utils import run_bass_kernel_spmd as _run

    nc = _bacc.Bacc("TRN2", target_bir_lowering=False, num_devices=1)
    arrays, A, O = {}, {}, {}
    for name, value in inputs.items():
        a = _np.ascontiguousarray(value)
        arrays[f"in_{name}"] = a
        A[name] = nc.dram_tensor(f"in_{name}", a.shape, _mybir.dt.float32, kind="ExternalInput").ap()
    for name, shape in _OUTS:
        O[name] = nc.dram_tensor(f"out_{name}", shape, _mybir.dt.float32, kind="ExternalOutput").ap()
    program(nc, A, O)
    r = _run(nc, [arrays], core_ids=[0])
    return tuple(r.results[0][f"out_{name}"] for name, _ in _OUTS)
```

```python
from contextlib import ExitStack, contextmanager

import concourse.bass as bass
from concourse import mybir

F32 = mybir.dt.float32
F32R = mybir.dt.float32r
U32 = mybir.dt.uint32
ALU = mybir.AluOpType
ACT = mybir.ActivationFunctionType
AX_X = mybir.AxisListType.X

P = 128
D = 1024
KD = D // P
NSAMP, TSAMP = 8, 4
META, SEQ = 16, 512
SAMP = NSAMP * TSAMP
PROMPT = META + SEQ
T = SAMP + PROMPT
CK, SK = 31, 4
G = 8
HG = 4
NH = G * HG
HD = 64
N = 128
DI = 2 * D
EPS = 1e-6
CHUNK = 128
CHUNKS = [(0, SAMP), (SAMP, META)] + [(SAMP + META + CHUNK * i, CHUNK) for i in range(SEQ // CHUNK)]
ORDER = [1, 2, 3, 4, 5, 0]
TILES = [(0, SAMP + META)] + CHUNKS[2:]
W_GV, W_GG, W_Z, W_X, W_B, W_C = 0, D, 2 * D, 4 * D, 6 * D, 7 * D
W_DT, W_GATE = 8 * D, 8 * D + NH
R_CW, R_CB, R_LG, R_LB, R_OB, R_NMIX = 0, CK, CK + 1, CK + 2, CK + 3, CK + 4
R_X, R_BC = CK + 5, CK + 15
R_NW = CK + 25
R_GB = CK + 27
R_DS = CK + 29
NR = CK + 31
UO = 208
USPLIT = 512 - UO
RING = 2
POOL_LOW = 6
DVE_STEPS = 59
N_CROW = 18
U_TILES = 14
BLOCKS = 10
U_OF = [0, 1, 2, 3, 4, 5, 8, 9, 10, 11]


class Steps:

    def __init__(self, eng, sem):
        self.eng, self.sem, self.base, self.n = eng, sem, 0, 0

    def link(self, ins):
        ins.then_inc(self.sem, 1)
        self.n += 1
        self.eng.wait_ge(self.sem, self.base + self.n)

    def enter(self, g, per):
        self.start, self.per = self.n, per
        self.base, self.n = g * per + self.n, 0

    def leave(self, trips):
        assert self.n == self.per, self.n
        self.n, self.base = self.start + trips * self.per, 0


@contextmanager
def semaphores(nc):
    held = []

    def sem(name):
        held.append(nc.alloc_semaphore(name=name))
        return held[-1]

    yield sem
    nc.clear_and_free_semaphores(held)
    nc.all_engine_barrier()


def trunk(nc, A, O, keep):
    cs = keep["cs"]
    ident, ones = keep["ident"], keep["ones"]
    w_in = A["w_in"][0]
    with ExitStack() as ctx:
        def sb(name, shape, dt=F32):
            return ctx.enter_context(nc.sbuf_tensor(name, shape, dt))

        sem = ctx.enter_context(semaphores(nc))

        xh, xl = sb("xh", [P, KD, T], F32R), sb("xl", [P, KD, T], F32R)
        wh, wl = sb("wh", [P, RING, KD, P], F32R), sb("wl", [P, RING, KD, P], F32R)
        wdh, wdl = sb("wdh", [P, KD, NH], F32R), sb("wdl", [P, KD, NH], F32R)
        ring = sb("ring", [P, RING, KD, P])
        aout = sb("aout", [P, T])
        yout = sb("yout", [P, 2, T])
        eps = sb("eps", [P, 1])
        xin = keep["x1"][:, :, :]
        scr = xin.rearrange("p t d -> p (t d)")
        h0 = scr[:, 0:2048].rearrange("p (i b n) -> p i b n", i=2, b=NSAMP)
        h0T = scr[:, 2048:4096].rearrange("p (i b m) -> p i b m", i=2, b=NSAMP)
        Bblk = scr[0:SAMP, 4096:5120].rearrange("p (b n) -> p b n", b=NSAMP)
        stage = sb("stage", [P, 3 * D + KD * NH])
        crow = stage[0:R_DS, 0:D]
        confrow = stage[0:120, D:3 * D].rearrange("p (t d) -> p t d", t=2)
        ssmrow = keep["wraw"][0:NSAMP * (SK - 1), :, :].rearrange("p a c -> p (a c)")
        wdt = stage[:, 3 * D:3 * D + KD * NH].rearrange("p (k m) -> p k m", k=KD)
        stC = sb("stC", [P, KD, NSAMP * (CK - 1)])
        stS = sb("stS", [P, 32, NSAMP * (SK - 1)])
        gc = sb("gc", [P, NR])
        U = sb("U", [P, P])
        SL = sb("SL", [P, P])
        Ub = sb("Ub", [SAMP, SAMP])
        SLb = sb("SLb", [SAMP, SAMP])
        Bm = sb("Bm", [SAMP, NSAMP])
        dtb = sb("dtb", [P, NH])
        expA = sb("expA", [P, NH])
        dtt = sb("dtt", [P, 6, NH])
        tmp1 = sb("tmp1", [P, 6, NH])
        tmp2 = sb("tmp2", [P, 6, NH])
        aa = sb("aa", [P, 6, NH])
        tail = sb("tail", [P, 6, NH])
        Dl = sb("Dl", [P, 6, NH])
        ss = sb("ss", [P, 8])
        raw_p = sb("raw_p", [P, 4, SK - 1 + PROMPT])
        raw_s = sb("raw_s", [P, 4, NSAMP, SK - 1 + TSAMP])
        cv = sb("cv", [P, 4, T])
        th = sb("th", [P, 2, T])
        a_p = sb("a_p", [P, CK - 1 + PROMPT])
        a_s = sb("a_s", [P, NSAMP, CK - 1 + TSAMP])
        cacc = sb("cacc", [P, T])
        ybuf = sb("ybuf", [P, 2, T])
        zc = sb("zc", [P, 2, T])
        Ed = sb("Ed", [P, 2, T])
        ab = sb("ab", [P, 6, HG * HD])
        ds0 = sb("ds0", [1, NH])
        dsrow = cv[0:1, :, :].rearrange("p q t -> p (q t)")[:, 0:DI]
        gbuf = sb("gbuf", [P, T])
        aah, aal = sb("aah", [P, 6, NH], F32R), sb("aal", [P, 6, NH], F32R)
        aUh, aUl = sb("aUh", [P, HG, P], F32R), sb("aUl", [P, HG, P], F32R)
        SLr, SLbr = sb("SLr", [P, P], F32R), sb("SLbr", [SAMP, SAMP], F32R)
        Lx = sb("Lx", [P, HG, P])
        Tt = sb("Tt", [P, 4, P])
        cbm = sb("cbm", [P, P])
        xdt = sb("xdt", [P, HG, HD])
        xtl = sb("xtl", [P, HG, HD])
        hT = sb("hT", [P, HG, HD])
        hTd = sb("hTd", [P, HG, HD])
        yi = sb("yi", [P, 2, P])
        pk = sb("pk", [P, 4, 27])
        pk_rows = sb("pk_rows", [27, 4, P])
        pa = sb("pa", [P, 62])
        pa_rows = sb("pa_rows", [62, P])
        hout = sb("hout", [P, 2, P])
        xt = (Tt, Lx)
        pu = [ctx.enter_context(nc.psum_tensor(f"pu{i}", [P, 1024], F32)) for i in range(2)]
        pS, pT, pC, pY = (ctx.enter_context(nc.psum_tensor(n, [P, 512], F32)) for n in ("pS", "pT", "pC", "pY"))

        s_x, s_crow, s_conf, s_ssm, s_wdt, s_dtb = map(
            sem, ("s_x", "s_crow", "s_conf", "s_ssm", "s_wdt", "s_dtb"))
        s_w = [sem(f"s_w{i}") for i in range(RING)]
        s_xt, s_xh, s_xl, s_wdh, s_wdl, s_wh, s_wlp, s_wld, s_ast, s_yst, s_slr, s_aah, s_wraw = map(
            sem, ("s_xt", "s_xh", "s_xl", "s_wdh", "s_wdl", "s_wh", "s_wlp", "s_wld", "s_ast", "s_yst", "s_slr", "s_aah", "s_wraw"))
        s_h0 = sem("s_h0")
        s_st_conf, s_st_h, s_st_pk, s_st_pa, s_st_hp = map(
            sem, ("s_st_conf", "s_st_h", "s_st_pk", "s_st_pa", "s_st_hp"))
        s_zero, s_const, s_sq, s_var, s_sqrt, s_xs, s_fill, s_fillfree = map(
            sem, ("s_zero", "s_const", "s_sq", "s_var", "s_sqrt", "s_xs", "s_fill", "s_fillfree"))
        s_dtp, s_dte, s_dtl, s_a, s_tp, s_te, s_pro = map(
            sem, ("s_dtp", "s_dte", "s_dtl", "s_a", "s_tp", "s_te", "s_pro"))
        s_gc, s_u, s_ufree, s_raw, s_st, s_conv, s_thx, s_cv = map(
            sem, ("s_gc", "s_u", "s_ufree", "s_raw", "s_st", "s_conv", "s_thx", "s_cv"))
        s_pre, s_ab, s_pe1, s_L, s_T, s_W, s_xtl, s_hTd, s_pe2, s_y = map(
            sem, ("s_pre", "s_ab", "s_pe1", "s_L", "s_T", "s_W", "s_xtl", "s_hTd", "s_pe2", "s_y"))
        s_ga, s_cconv, s_z, s_yz, s_sq2, s_rec, s_yn = map(
            sem, ("s_ga", "s_cconv", "s_z", "s_yz", "s_sq2", "s_rec", "s_yn"))
        s_h0t, s_h0tev, s_Bblk, s_hs, s_hnew = map(sem, ("s_h0t", "s_h0tev", "s_Bblk", "s_hs", "s_hnew"))
        s_pk, s_out, s_outev = map(sem, ("s_pk", "s_out", "s_outev"))
        s_ident, s_ss, s_expA, s_stc, s_sts, s_g, s_gst = map(
            sem, ("s_ident", "s_ss", "s_expA", "s_stc", "s_sts", "s_g", "s_gst"))
        s_ds0, s_dsr, s_settled = sem("s_ds0"), sem("s_dsr"), sem("s_settled")
        c_dve, c_act, c_pool = map(sem, ("c_dve", "c_act", "c_pool"))
        block = ctx.enter_context(nc.Block())

        def settled(eng):
            eng.sem_inc(s_settled, 1)

        def low_done(eng, g, k):
            if k < POOL_LOW:
                eng.wait_ge(s_wlp, POOL_LOW * g + k + 1)
            else:
                eng.wait_ge(s_wld, (BLOCKS - POOL_LOW) * g + k - POOL_LOW + 1)

        def split_next(g, k):
            return (g, k + RING) if k + RING < BLOCKS else (g + 1, k + RING - BLOCKS)

        def multiplied(eng, g, k):
            eng.wait_ge(s_u, U_TILES * g + U_OF[k] + 2)

        def low(eng, k):
            return eng.tensor_tensor(wl[:, k % RING], ring[:, k % RING], wh[:, k % RING].bitcast(F32), ALU.subtract)

        @block.sync
        def _(sp):
            sp.dma_start(crow[0:CK, :], A["conf_dw_w"][0]).then_inc(s_crow, 16)
            loads = [(R_CB, A["conf_dw_b"]), (R_LG, A["conf_ln_g"]), (R_LB, A["conf_ln_b"]),
                     (R_OB, A["conf_out_b"]), (R_NMIX, A["norm_mix_w"])]
            for r, ap in loads:
                sp.dma_start(crow[r:r + 1, :], ap).then_inc(s_crow, 16)
            cw, cb = A["ssm_conv_w"][0], A["ssm_conv_b"]
            for i in range(2):
                dst = crow[R_X + 5 * i:R_X + 5 * i + 5, :].rearrange("r (g c) -> r g c", g=G)
                src = cw[:, 0:DI].rearrange("k (g i c) -> i k g c", i=2, g=G)[i]
                sp.dma_start(dst[0:SK], src).then_inc(s_crow, 16)
                src = cb[:, 0:DI].rearrange("k (g i c) -> i k g c", i=2, g=G)[i]
                sp.dma_start(dst[SK:SK + 1], src).then_inc(s_crow, 16)
                r = R_BC + 5 * i
                sp.dma_start(crow[r:r + SK, :], cw[:, DI + D * i:DI + D * i + D]).then_inc(s_crow, 16)
                sp.dma_start(crow[r + SK:r + SK + 1, :], cb[:, DI + D * i:DI + D * i + D]).then_inc(s_crow, 16)
                dst = crow[R_NW + i:R_NW + i + 1, :].rearrange("r (g c) -> r g c", g=G)
                src = A["ssm_norm_w"].rearrange("k (g i c) -> i k g c", i=2, g=G)[i]
                sp.dma_start(dst, src).then_inc(s_crow, 16)
                sp.dma_start(crow[R_GB + i:R_GB + i + 1, :], A["gate_b"][:, D * i:D * i + D]).then_inc(s_crow, 16)
            sp.dma_start(ds0[:, :], A["d_skip"]).then_inc(s_ds0, 16)
            def w_block(g, k):
                first = [W_X + 2 * P * g, W_X + 2 * P * g + P, W_B + P * g, W_C + P * g, W_GV + P * g,
                         W_GG + P * g, W_Z + 2 * P * g, W_Z + 2 * P * g + P, W_GATE + P * g,
                         W_GATE + D + P * g][k]
                src = w_in.rearrange("(k p) n -> p k n", p=P)[:, :, bass.ds(first, P)]
                sp.dma_start(ring[:, k % RING], src).then_inc(s_w[k % RING], 16)

            sp.dma_start(dtb[:, :], A["dt_bias"][0].partition_broadcast(P)).then_inc(s_dtb, 16)
            sp.dma_start(expA[:, :], A["a_log"][0].partition_broadcast(P)).then_inc(s_dtb, 16)
            sp.dma_start(wdt, w_in.rearrange("(k p) n -> p k n", p=P)[:, :, W_DT:W_DT + NH]).then_inc(s_wdt, 16)
            for k in range(RING):
                w_block(0, k)
            for t in range(2):
                src = A["state_conf_conv"][0].rearrange("(t b) r c -> t (b r) c", t=2)[t]
                sp.dma_start(confrow[:, t], src).then_inc(s_conf, 16)
            sp.dma_start(ssmrow, A["state_ssm_conv"][0].rearrange("b r c -> (b r) c")).then_inc(s_ssm, 16)
            sp.dma_start(O["new_conf_sample"][0][:, 0:CK - 1 - TSAMP, :],
                         A["state_conf_conv"][0][:, TSAMP:CK - 1, :]).then_inc(s_st_conf, 16)

            def states_in(g):
                sp.wait_ge(s_pro, 1)
                sp.wait_ge(s_st_h, 32 * g + 1)
                src = A["state_ssm"][0].rearrange("b (g i h) p n -> g i (h p) b n", i=2, h=2)
                for i in range(2):
                    sp.dma_start(h0[:, i], src[g, i]).then_inc(s_h0, 16)

            def results_out(g):
                sp.wait_ge(s_hnew, 4 * g + 4 + 1)
                dst = O["new_ssm_sample"][0].rearrange("b (g i h) p n -> g i (h p) b n", i=2, h=2)
                for i in range(2):
                    sp.dma_start(dst[g, i], h0[:, i]).then_inc(s_st_h, 16)
                sp.wait_ge(s_outev, 3 * g + 3 + 1)
                pks = pk_rows[:, :, :]
                for dst, r0, n in ((O["new_sconv_prompt"][0, 0], 0, 3),
                                   (O["new_sconv_sample"][0].rearrange("b r c -> (b r) c"), 3, 24)):
                    sp.dma_start(dst[:, bass.ds(2 * P * g, 2 * P)].rearrange("r (q c) -> r q c", q=2),
                                 pks[r0:r0 + n, 0:2, :]).then_inc(s_st_pk, 16)
                    for q in range(2):
                        sp.dma_start(dst[:, bass.ds(DI + D * q + P * g, P)],
                                     pks[r0:r0 + n, 2 + q, :]).then_inc(s_st_pk, 16)
                sp.dma_start(O["new_conf_prompt"][0, 0][:, bass.ds(P * g, P)],
                             pa_rows[0:CK - 1, :]).then_inc(s_st_pa, 16)
                sp.dma_start(O["new_ssm_prompt"][0, 0].rearrange("(g i h) p n -> g (h p) i n", i=2, h=2)[g],
                             hout[:, :, :]).then_inc(s_st_hp, 16)
                for r in range(TSAMP):
                    sp.dma_start(O["new_conf_sample"][0][:, CK - 1 - TSAMP + r, bass.ds(P * g, P)],
                                 pa_rows[CK - 1 + NSAMP * r:CK - 1 + NSAMP * r + NSAMP, :]).then_inc(s_st_pa, 16)
                sp.wait_ge(s_yn, 2 * g + 2 + 1)
                sp.dma_start(keep["yrows"][g].rearrange("i p t -> p i t"), yout[:, :, :]).then_inc(s_yst, 16)
                sp.wait_ge(s_cconv, g + 1 + 1)
                sp.dma_start(keep["aconv"][g], aout[:, :]).then_inc(s_ast, 16)

            def blocks(g, ks):
                for k in ks:
                    low_done(sp, *((g, k - RING) if k >= RING else (g - 1, k - RING + BLOCKS)))
                    settled(sp)
                    w_block(g, k)

            def group(g, last=False):
                blocks(g, range(RING, 6))
                if not isinstance(g, int) or g > 0:
                    results_out(g - 1)
                blocks(g, range(6, 8))
                states_in(g)
                blocks(g, range(8, BLOCKS))
                if not last:
                    blocks(g + 1, range(RING))

            group(0)
            with sp.Fori(0, G - 2) as g1:
                group(g1 + 1)
            group(G - 1, last=True)
            for n in range(2):
                sp.dma_start(keep["wraw"][:, n, :].rearrange("p (k n) -> p k n", n=P),
                             A["ssm_out_w"][0].rearrange("(k p) n -> p k n", p=P)[:, :, P * n:P * n + P])\
                    .then_inc(s_wraw, 16)
            results_out(G - 1)
            sp.wait_ge(s_wraw, 32)
            sp.wait_ge(s_st_h, 32 * G + 1)
            sp.wait_ge(s_ast, 16 * G + 1)
            sp.wait_ge(s_yst, 16 * G + 1)
            sp.wait_ge(s_st_pk, 96 * G + 1)
            sp.wait_ge(s_st_pa, 80 * G + 1)
            sp.wait_ge(s_st_hp, 16 * G + 1)
            sp.wait_ge(s_st_conf, 16)

        @block.gpsimd
        def _(pool):
            for started in (s_st_h, s_pe1, s_pe2, s_yn, s_u, s_g, s_cconv, s_conv, s_y, s_hs,
                            s_out, s_hnew, s_ufree, s_pk, s_xtl, s_W,
                            s_gst, s_st_pk, s_st_pa, s_st_hp, s_outev, s_ast, s_yst):
                pool.sem_inc(started, 1)
            k = Steps(pool, c_pool)
            for m in (U, SL, ones, Ub, SLb, Bm):
                pool.memset(m[:, :], 1.0).then_inc(s_zero, 1)
            pool.memset(ident[:, :], 0.0).then_inc(s_zero, 1)
            pool.wait_ge(s_zero, 7)

            def mask(m, cond, base, pattern, mult, fill=0.0):
                k.link(pool.affine_select(out=m, in_=m, compare_op=cond, fill=fill, base=base,
                                          pattern=pattern, channel_multiplier=mult))

            mask(ident[:, :], ALU.not_equal, 0, [[-1, P]], 1, 1.0)
            pool.sem_inc(s_ident, 1)
            mask(U[:, :], ALU.is_ge, 0, [[1, P]], -1)
            mask(SL[:, :], ALU.is_gt, 0, [[-1, P]], 1)
            Ub3 = Ub[:, :].rearrange("k (b r) -> k b r", b=NSAMP)
            mask(Ub3, ALU.is_ge, 0, [[TSAMP, NSAMP], [1, TSAMP]], -1)
            mask(Ub3, ALU.is_ge, 0, [[-TSAMP, NSAMP], [0, TSAMP]], 1)
            SLb3 = SLb[:, :].rearrange("k (b r) -> k b r", b=NSAMP)
            mask(SLb3, ALU.is_gt, 0, [[-TSAMP, NSAMP], [-1, TSAMP]], 1)
            mask(SLb3, ALU.is_ge, TSAMP - 1, [[TSAMP, NSAMP], [0, TSAMP]], -1)
            mask(Bm[:, :], ALU.is_ge, 0, [[-TSAMP, NSAMP]], 1)
            mask(Bm[:, :], ALU.is_ge, TSAMP - 1, [[TSAMP, NSAMP]], -1)
            pool.memset(tail[:, :, :], 0.0).then_inc(s_const, 1)
            pool.memset(dtt[:, :, :], 0.0).then_inc(s_const, 1)
            pool.memset(raw_p[:, :, 0:SK - 1], 0.0).then_inc(s_const, 1)
            pool.memset(a_p[:, 0:CK - 1], 0.0).then_inc(s_const, 1)
            def split(g, k):
                pool.wait_ge(s_wh, BLOCKS * g + k + 1)
                settled(pool)
                low(pool, k).then_inc(s_wlp, 1)

            split(0, 0)
            split(0, 1)
            pool.wait_ge(s_pro, 1)

            def a_over_channels(g, js):
                for j in js:
                    S = CHUNKS[j][1]
                    a4 = aa[0:S, j, bass.ds(HG * g, HG)].unsqueeze(2)
                    pool.tensor_copy(ab[0:S, j, :].rearrange("s (h p) -> s h p", h=HG),
                                     a4.broadcast_to([S, HG, HD])).then_inc(s_ab, 1)

            def group(g, is_last=False):
                split(g, 2)
                split(g, 3)
                pool.wait_ge(s_yn, 2 * g + 1)
                pool.wait_ge(s_u, U_TILES * g + 1)
                pool.wait_ge(s_g, 2 * g + 1)
                pool.wait_ge(s_cconv, g + 1)
                settled(pool)
                pool.tensor_copy(gc[:, :], cs[:, g, :]).then_inc(s_gc, 1)
                pool.wait_ge(s_conv, 4 * g + 1)
                settled(pool)
                for q, m in enumerate((2 * g, 2 * g + 1, G * 2 + g, G * 3 + g)):
                    pool.tensor_copy(raw_s[:, q, :, 0:SK - 1],
                                     stS[:, m, :].rearrange("p (b r) -> p b r", b=NSAMP)).then_inc(s_sts, 1)
                pool.tensor_copy(a_s[:, :, 0:CK - 1],
                                 stC[:, g, :].rearrange("p (b r) -> p b r", b=NSAMP)).then_inc(s_stc, 1)
                split(g, 4)
                a_over_channels(g, range(3))
                a_over_channels(g, range(3, 6))
                split(g, 5)

                def decay_rows(j):
                    ci = ORDER[j]
                    S = CHUNKS[ci][1]
                    um = (Ub if ci == 0 else U)[0:S, 0:S].unsqueeze(1).broadcast_to([S, HG, S])
                    pool.wait_ge(s_pe1, 6 * g + j + 1)
                    settled(pool)
                    for rows, a in ((aUh, aah), (aUl, aal)):
                        a4 = a[0:S, ci, bass.ds(HG * g, HG)].bitcast(F32).unsqueeze(2)
                        pool.tensor_tensor(rows[0:S, :, 0:S], a4.broadcast_to([S, HG, S]), um,
                                           ALU.mult).then_inc(s_pre, 1)

                decay_rows(0)
                for j in range(6):
                    ci = ORDER[j]
                    S = CHUNKS[ci][1]
                    t4 = tail[0:S, ci, bass.ds(HG * g, HG)].unsqueeze(2).broadcast_to([S, HG, HD])
                    pool.wait_ge(s_T, 6 * g + j + 1)
                    settled(pool)
                    pool.tensor_tensor(xtl[0:S, :, :],
                                       Tt[0:S, 0:2, :].rearrange("s i (h p) -> s (i h) p", h=2), t4,
                                       ALU.mult).then_inc(s_xtl, 1)
                    if 0 < j < 5:
                        d4 = Dl[:, ci, bass.ds(HG * g, HG)].unsqueeze(2).broadcast_to([P, HG, HD])
                        pool.wait_ge(s_y, 6 * g + j + 1)
                        settled(pool)
                        pool.tensor_tensor(hTd[:, :, :], hT[:, :, :], d4, ALU.mult).then_inc(s_hTd, 1)
                    if j == 5:
                        pool.wait_ge(s_hs, 4 * g + 1)
                        settled(pool)
                        pool.tensor_tensor(Bblk, Tt[0:SAMP, 2, :].unsqueeze(1).broadcast_to([SAMP, NSAMP, N]),
                                           Bm[:, :].unsqueeze(2).broadcast_to([SAMP, NSAMP, N]),
                                           ALU.mult).then_inc(s_Bblk, 1)
                    if j < 5:
                        decay_rows(j + 1)
                    if j == 0:
                        pool.wait_ge(s_out, 2 * g + 1)
                        settled(pool)
                        pool.tensor_copy(pk[:, :, 0:3], raw_p[:, :, PROMPT:PROMPT + 3]).then_inc(s_pk, 1)
                        for q in range(4):
                            pool.tensor_copy(pk[:, q, 3:27].rearrange("p (b r) -> p b r", b=NSAMP),
                                             raw_s[:, q, :, TSAMP:TSAMP + 3]).then_inc(s_pk, 1)
                        pool.wait_ge(s_ga, 2 * g + 2)
                        settled(pool)
                        pool.tensor_copy(pa[:, 0:CK - 1], a_p[:, PROMPT:PROMPT + CK - 1]).then_inc(s_pk, 1)
                        pool.tensor_copy(pa[:, CK - 1:62].rearrange("p (r b) -> p b r", b=NSAMP),
                                         a_s[:, :, CK - 1:CK - 1 + TSAMP]).then_inc(s_pk, 1)
                if not is_last:
                    split(g + 1, 0)
                    split(g + 1, 1)

            with pool.Fori(0, G - 1) as g:
                group(g)
            group(G - 1, is_last=True)

        def u_cols(i, a, b):
            return pu[i % 2][:, UO + a:UO + b]

        @block.scalar
        def _(act):
            k = Steps(act, c_act)
            act.dma_start(xin[0:SAMP, 0, :], A["x_sample"].rearrange("b t d -> (b t) d")).then_inc(s_x, 16)
            act.dma_start(xin[SAMP:SAMP + META, 0, :], A["meta_tokens"]).then_inc(s_x, 16)
            act.dma_start(xin[:, 1:5, :], A["x_prompt"][0].rearrange("(t p) d -> p t d", p=P)).then_inc(s_x, 16)
            act.wait_ge(s_x, 48)
            act.wait_ge(s_ss, 1)
            for t, (c, S) in enumerate(TILES):
                k.link(act.activation(ybuf[0:S, :, :].rearrange("p a b -> p (a b)")[:, 0:D], xin[0:S, t, :],
                                      ACT.Square, accum_out=ss[0:S, t:t + 1]))
            act.sem_inc(s_sq, 1)
            act.wait_ge(s_var, 1)
            act.activation(ss[:, 0:5], ss[:, 0:5], ACT.Sqrt).then_inc(s_sqrt, 1)

            def split(g, k):
                act.wait_ge(s_w[k % RING], BLOCKS // RING * 16 * g + 16 * (k // RING + 1))
                act.activation(wh[:, k % RING].rearrange("p k m -> p (k m)"),
                               ring[:, k % RING].rearrange("p k m -> p (k m)"), ACT.Copy).then_inc(s_wh, 1)

            for n in range(2 * len(TILES)):
                (c, S), h = TILES[n // 2], n % 2
                act.wait_ge(s_xt, n + 1)
                act.activation(xh[:, 4 * h:4 * h + 4, c:c + S], xt[n % 2][:, :, 0:S], ACT.Copy).then_inc(s_xh, 1)
                if n == 4:
                    act.wait_ge(s_wdt, 16)
                    act.activation(wdh[:, :, :], wdt, ACT.Copy).then_inc(s_wdh, 1)
            split(0, 0)
            split(0, 1)
            act.wait_ge(s_dtb, 32)
            act.activation(expA[:, :], expA[:, :], ACT.Exp).then_inc(s_expA, 1)
            act.wait_ge(s_dte, 1)
            k.link(act.activation(tmp2[:, :, :], tmp2[:, :, :], ACT.Exp))
            act.activation(tmp2[:, :, :], tmp2[:, :, :], ACT.Ln, bias=1.0).then_inc(s_dtl, 1)
            act.wait_ge(s_const, 4)
            act.activation(SLr[:, :], SL[:, :], ACT.Copy).then_inc(s_slr, 1)
            act.activation(SLbr[:, :], SLb[:, :], ACT.Copy).then_inc(s_slr, 1)
            act.wait_ge(s_a, 1)
            act.activation(aah[:, :, :], aa[:, :, :], ACT.Copy).then_inc(s_aah, 1)
            act.wait_ge(s_tp, 1)
            for ci, (c, S) in enumerate(CHUNKS):
                act.activation(tail[0:S, ci, :], pY[0:S, NH * ci:NH * ci + NH], ACT.Exp).then_inc(s_te, 1)
            act.activation(Dl[:, 1:6, :], pY[:, 7 * NH:12 * NH].rearrange("p (c h) -> p c h", c=5),
                           ACT.Exp).then_inc(s_te, 1)

            def group(g, is_last=False):
                U0 = U_TILES * g

                def split_behind(k):
                    if k + RING < BLOCKS or not is_last:
                        multiplied(act, g, k)
                        split(*split_next(g, k))

                def evac(r):
                    act.wait_ge(s_u, U0 + r + 2)

                def raw(q):
                    split_behind(q)
                    evac(q)
                    act.wait_ge(s_conv, 4 * g + 1)
                    act.wait_ge(s_pk, 7 * g + 1)
                    act.activation(raw_p[:, q, SK - 1:], u_cols(q, SAMP, T), ACT.Copy).then_inc(s_raw, 1)
                    act.activation(raw_s[:, q, :, SK - 1:], u_cols(q, 0, SAMP).rearrange("p (b r) -> p b r", b=NSAMP),
                                   ACT.Copy).then_inc(s_ufree, 1)

                def silu(q):
                    act.wait_ge(s_conv, 4 * g + q + 2)
                    if q < 2:
                        act.wait_ge(s_u, U0 + 1)
                    else:
                        act.wait_ge(s_cv, 4 * g + q - 1)
                    act.activation(th[:, q % 2, :], cv[:, q, :], ACT.Tanh).then_inc(s_thx, 1)

                raw(0)
                raw(1)
                raw(2)
                silu(0)
                raw(3)
                silu(1)
                silu(2)
                split_behind(4)
                evac(4)
                act.wait_ge(s_yn, 2 * g + 1)
                act.activation(zc[:, 0, :], u_cols(0, 0, T), ACT.Copy, scale=0.5).then_inc(s_ufree, 1)
                silu(3)
                split_behind(5)
                evac(5)
                act.activation(zc[:, 1, :], u_cols(1, 0, T), ACT.Tanh, scale=0.5).then_inc(s_ufree, 1)
                for i in range(2):
                    evac(6 + i)
                    act.wait_ge(s_hnew, 4 * g + 1)
                    act.activation(Ed[:, i, :], u_cols(i, 0, T), ACT.Exp).then_inc(s_ufree, 1)

                def chunk(j):
                    ci = ORDER[j]
                    S = CHUNKS[ci][1]
                    act.wait_ge(s_pe1, 6 * g + j + 2)
                    act.wait_ge(s_pe2, 6 * g + j + 1)
                    act.activation(Lx[0:S, :, 0:S], pS[0:S, :].rearrange("s (h t) -> s h t", h=HG)[:, :, 0:S],
                                   ACT.Exp).then_inc(s_L, 1)
                    act.wait_ge(s_W, 6 * g + j + 1)
                    act.wait_ge(s_xtl, 6 * g + j + 1)
                    act.wait_ge(s_hs, 4 * g + 1)
                    if S == P:
                        act.activation(Tt[:, :, :].rearrange("s a t -> s (a t)"), pT[:, :], ACT.Copy).then_inc(s_T, 1)
                    else:
                        act.activation(Tt[0:S, 0:3, :].rearrange("s a t -> s (a t)"), pT[0:S, 0:3 * P], ACT.Copy)
                        act.activation(Tt[0:S, 3, 0:S], pT[0:S, 3 * P:3 * P + S], ACT.Copy).then_inc(s_T, 1)

                def z(i):
                    split_behind(6 + i)
                    evac(8 + i)
                    act.wait_ge(s_ga, 2 * g + 2)
                    act.wait_ge(s_cv, 4 * g + 3 + i)
                    act.activation(th[:, i, :], u_cols(i, 0, T), ACT.Tanh, scale=0.5).then_inc(s_z, 1)
                    act.activation(zc[:, i, :], u_cols(i, 0, T), ACT.Copy).then_inc(s_ufree, 1)

                def gate(i):
                    split_behind(8 + i)
                    evac(10 + i)
                    act.wait_ge(s_gc, g + 1)
                    act.wait_ge(s_gst, 32 * g + 16 * i + 1)
                    act.activation(gbuf[:, :], u_cols(i, 0, T), ACT.Tanh, bias=gc[:, R_GB + i:R_GB + i + 1],
                                   scale=0.5).then_inc(s_g, 1)
                    act.wait_ge(s_g, 2 * g + i + 2)
                    act.sem_inc(s_ufree, 1)
                    act.dma_start(keep["gates"][i, g], gbuf[:, :]).then_inc(s_gst, 16)

                def h0_copy(r):
                    act.wait_ge(s_h0t, 4 * g + r + 1)
                    act.wait_ge(s_pe2, 6 * g + 1)
                    act.activation(h0T[:, r // 2, 4 * (r % 2):4 * (r % 2) + 4, :].rearrange("p b m -> p (b m)"),
                                   (pS, pT)[r % 2][:, :], ACT.Copy).then_inc(s_h0tev, 1)

                chunk(0)
                z(0)
                chunk(1)
                chunk(2)
                z(1)
                chunk(3)
                chunk(4)
                gate(0)
                chunk(5)
                for r in range(4):
                    h0_copy(r)
                gate(1)
                act.wait_ge(s_yz, g + 1)
                act.activation(th[:, :, :], ybuf[:, :, :], ACT.Square).then_inc(s_sq2, 1)
                act.wait_ge(s_out, 2 * g + 2)
                act.wait_ge(s_st_pk, 96 * g + 1)
                act.wait_ge(s_st_pa, 80 * g + 1)
                act.wait_ge(s_st_hp, 16 * g + 1)
                act.activation(pk_rows[:, :, :].rearrange("r q c -> r (q c)"), pC[0:27, :], ACT.Copy).then_inc(s_outev, 1)
                act.wait_ge(s_out, 2 * g + 2 + 1)
                act.activation(hout[:, :, :].rearrange("p i n -> p (i n)"), pY[:, 0:2 * P], ACT.Copy).then_inc(s_outev, 1)
                act.activation(pa_rows[:, :], pY[0:62, 2 * P:3 * P], ACT.Copy).then_inc(s_outev, 1)
                for r in range(2):
                    evac(12 + r)
                    act.activation(zc[:, 0, 280 * r:280 * r + 280], pu[r][:, 0:280], ACT.Sqrt,
                                   scale=1.0 / (2 * P), bias=eps[:, :]).then_inc(s_ufree, 1)

            with act.Fori(0, G - 1) as g:
                group(g)
            group(G - 1, is_last=True)
            act.wait_ge(s_gst, 32 * G + 1)

        @block.tensor
        def _(pe):
            fill_no = [0]

            def fill(parts):
                n = fill_no[0]
                bank = (pS, pT)[n % 2]
                if n >= 2:
                    pe.wait_ge(s_fillfree, n - 1)
                for col, src in parts:
                    R, C = src.shape
                    last = pe.transpose(bank[0:C, col:col + R], src, ident[0:R, 0:R])
                last.then_inc(s_fill, 1)
                fill_no[0] += 1

            pe.wait_ge(s_ident, 1)
            pe.wait_ge(s_crow, 16 * N_CROW)
            pe.wait_ge(s_dsr, 1)
            fill([(64 * j, crow[:, P * j:P * j + P]) for j in range(KD)]
                 + [(64 * g + R_DS + i, dsrow[:, P * (2 * g + i):P * (2 * g + i) + P])
                    for g in range(G) for i in range(2)])
            for t, (c, S) in enumerate(TILES):
                pe.wait_ge(s_xs, t + 1)
                for h in range(2):
                    fill([(P * q, xin[0:S, t, P * (4 * h + q):P * (4 * h + q) + P]) for q in range(4)])
            pe.wait_ge(s_conf, 32)
            for t in range(2):
                for h in range(2):
                    fill([(P * q, confrow[:, t, P * (4 * h + q):P * (4 * h + q) + P]) for q in range(4)])
            pe.wait_ge(s_ssm, 16)
            for f in range(2):
                fill([(32 * q, ssmrow[:, P * (16 * f + q):P * (16 * f + q) + P]) for q in range(16)])
            pe.wait_ge(s_wdl, 1)
            pe.wait_ge(s_xl, 2 * len(TILES))
            for ci, (c, S) in enumerate(CHUNKS):
                for j in range(KD):
                    for n, (x, w) in enumerate(((xh, wdh), (xl, wdh), (xh, wdl))):
                        last = pe.matmul(pC[0:S, NH * ci:NH * ci + NH], x[:, j, c:c + S], w[:, j, :],
                                         start=(j == 0 and n == 0), stop=(j == KD - 1 and n == 2))
            last.then_inc(s_dtp, 1)
            pe.wait_ge(s_a, 1)
            for ci, (c, S) in enumerate(CHUNKS):
                pe.matmul(pY[0:S, NH * ci:NH * ci + NH], (SLb if ci == 0 else SL)[0:S, 0:S], aa[0:S, ci, :],
                          start=True, stop=True)
            for ci, (c, S) in enumerate(CHUNKS[1:], 1):
                last = pe.matmul(pY[:, NH * (6 + ci):NH * (7 + ci)], ones[0:S, :], aa[0:S, ci, :],
                                 start=True, stop=True)
            last.then_inc(s_tp, 1)
            pe.wait_ge(s_te, 7)
            pe.wait_ge(s_slr, 2)
            pe.wait_ge(s_fillfree, 17)

            with pe.Fori(0, G) as g:
                U0 = U_TILES * g

                def free(r):
                    pe.wait_ge(s_ufree, U0 + max(r, 1))

                def block(k, halves=(0, 1)):
                    r = U_OF[k]
                    for h in halves:
                        if h == 0:
                            free(r)
                            low_done(pe, g, k)
                        for j in range(4 * h, 4 * h + 4):
                            for n, (w, x) in enumerate(((wh, xh), (wh, xl), (wl, xh))):
                                for a, b in ((0, USPLIT), (USPLIT, T)):
                                    last = pe.matmul(u_cols(r, a, b), w[:, k % RING, j, :], x[:, j, a:b],
                                                     start=(j == 0 and n == 0), stop=(j == KD - 1 and n == 2))
                        if h == 1:
                            last.then_inc(s_u, 1)

                def stage1(j):
                    ci = ORDER[j]
                    c, S = CHUNKS[ci]
                    pe.wait_ge(s_pre, 12 * g + 2 * j + 2)
                    if j == 0:
                        pe.wait_ge(s_hnew, 4 * g + 1)
                    else:
                        pe.wait_ge(s_L, 6 * g + j)
                    if S < P:
                        settled(pe)
                    for n, rows in enumerate((aUh, aUl)):
                        pe.matmul(pS[0:S, :].rearrange("s (h t) -> s h t", h=HG)[:, :, 0:S],
                                  (SLbr if ci == 0 else SLr)[0:S, 0:S], rows[0:S, :, 0:S],
                                  start=(n == 0), stop=(n == 1))
                    if j == 0:
                        pe.wait_ge(s_cv, 4 * g + 4)
                    else:
                        pe.wait_ge(s_T, 6 * g + j)
                    for q in range(3):
                        pe.transpose(pT[0:S, P * q:P * q + P], cv[:, q, c:c + S], ident[:, :])
                    pe.matmul(pT[0:S, 3 * P:3 * P + S], cv[:, 2, c:c + S], cv[:, 3, c:c + S],
                              start=True, stop=True).then_inc(s_pe1, 1)

                def stage2(j):
                    ci = ORDER[j]
                    c, S = CHUNKS[ci]
                    pe.wait_ge(s_W, 6 * g + j + 2)
                    pe.wait_ge(s_xtl, 6 * g + j + 2)
                    pe.wait_ge(s_y, 6 * g + j + 1)
                    pe.wait_ge(s_outev, 3 * g + 1)
                    yv = pY[:, 0:2 * P].rearrange("p (i t) -> p i t", i=2)
                    for h in range(HG):
                        half = HD * (h % 2)
                        last = pe.matmul(yv[half:half + HD, h // 2, 0:S], xdt[0:S, h, :], Lx[0:S, h, 0:S],
                                         start=True, stop=True)
                    if ci >= 2:
                        for i in range(2):
                            pe.matmul(pC[:, P * i:P * i + S], hT[:, 2 * i:2 * i + 2, :], cv[:, 3, c:c + S],
                                      start=True, stop=True)
                    if ci == 0:
                        pe.wait_ge(s_h0tev, 4 * g + 4)
                        for i in range(2):
                            for b in range(NSAMP):
                                last = pe.matmul(pC[:, P * i + TSAMP * b:P * i + TSAMP * b + TSAMP],
                                                 h0T[:, i, b, :], cv[:, 3, TSAMP * b:TSAMP * b + TSAMP],
                                                 start=True, stop=True)
                    else:
                        last = pe.matmul(pC[:, 2 * P:4 * P], Tt[0:S, 2, :], xtl[0:S, :, :], start=True, stop=True)
                    last.then_inc(s_pe2, 1)

                def states_turned(r):
                    if r == 0:
                        pe.wait_ge(s_h0, 32 * g + 32)
                    if r < 2:
                        pe.wait_ge((s_L, s_T)[r], 6 * g + 6)
                    else:
                        pe.wait_ge(s_h0tev, 4 * g + r - 1)
                    for b in range(4):
                        last = pe.transpose((pS, pT)[r % 2][:, P * b:P * b + P], h0[:, r // 2, 4 * (r % 2) + b, :],
                                            ident[:, :])
                    last.then_inc(s_h0t, 1)

                def states_added(r):
                    pe.wait_ge(s_Bblk, g + 1)
                    if r < 2:
                        pe.wait_ge(s_h0tev, 4 * g + r + 3)
                    else:
                        pe.wait_ge(s_hnew, 4 * g + r)
                    i, q = r // 2, r % 2
                    pe.matmul((pS, pT)[r % 2][:, :], xtl[0:SAMP, 2 * i:2 * i + 2, :],
                              Bblk[:, 4 * q:4 * q + 4, :], start=True, stop=True).then_inc(s_hs, 1)

                for k in range(6):
                    block(k)
                pe.wait_ge(s_ab, 6 * g + 6)
                for i in range(2):
                    free(6 + i)
                    for ci, (c, S) in enumerate(CHUNKS):
                        last = pe.matmul(u_cols(i, c, c + S), ab[0:S, ci, P * i:P * i + P],
                                         (Ub if ci == 0 else U)[0:S, 0:S], start=True, stop=True)
                    last.then_inc(s_u, 1)
                block(6, (0,))
                stage1(0)
                block(6, (1,))
                stage2(0)
                stage1(1)
                block(7, (0,))
                stage2(1)
                stage1(2)
                block(7, (1,))
                stage2(2)
                stage1(3)
                block(8, (0,))
                stage2(3)
                stage1(4)
                block(8, (1,))
                stage2(4)
                stage1(5)
                states_turned(0)
                states_turned(1)
                block(9, (0,))
                states_turned(2)
                states_turned(3)
                stage2(5)
                block(9, (1,))
                for r in range(4):
                    states_added(r)
                pe.wait_ge(s_y, 6 * g + 6 + 1)
                pe.wait_ge(s_pk, 7 * g + 7 + 1)
                for q in range(4):
                    last = pe.transpose(pC[0:27, P * q:P * q + P], pk[:, q, :], ident[:, :])
                last.then_inc(s_out, 1)
                for i in range(2):
                    pe.transpose(pY[:, P * i:P * i + P], hT[:, 2 * i:2 * i + 2, :].rearrange("n h p -> n (h p)"), ident[:, :])
                pe.transpose(pY[0:62, 2 * P:3 * P], pa[:, :], ident[:, :]).then_inc(s_out, 1)
                pe.wait_ge(s_sq2, g + 1)
                for r in range(2):
                    free(12 + r)
                    for i in range(2):
                        last = pe.matmul(pu[r][:, 0:280], ones[:, :], th[:, i, 280 * r:280 * r + 280],
                                         start=(i == 0), stop=(i == 1))
                    last.then_inc(s_u, 1)

        @block.vector
        def _(dve):
            k = Steps(dve, c_dve)

            def stt(out, in0, scalar, in1, op0=ALU.mult, op1=ALU.add):
                return dve.scalar_tensor_tensor(out=out, in0=in0, scalar=scalar, in1=in1, op0=op0, op1=op1)

            dve.memset(ss[:, :], 1.0).then_inc(s_ss, 1)
            k.link(dve.memset(eps[:, :], EPS))
            dve.wait_ge(s_ds0, 16)
            dve.tensor_copy(dsrow.rearrange("p (h c) -> p h c", h=NH),
                            ds0[:, :].unsqueeze(2).broadcast_to([1, NH, HD])).then_inc(s_dsr, 1)
            dve.wait_ge(s_fill, 1)
            k.link(dve.tensor_copy(cs[:, :, :], pS[:, :].rearrange("p (g r) -> p g r", g=G)[:, :, 0:NR]))
            dve.sem_inc(s_fillfree, 1)
            k.link(dve.tensor_scalar(cs[:, :, R_X:R_X + 20], cs[:, :, R_X:R_X + 20], 0.5, None, ALU.mult))
            k.link(dve.tensor_scalar(cs[:, :, R_GB:R_GB + 2], cs[:, :, R_GB:R_GB + 2], 0.5, None, ALU.mult))
            dve.wait_ge(s_sq, 1)
            dve.tensor_scalar(ss[:, 0:5], ss[:, 0:5], 1.0 / D, EPS, ALU.mult, ALU.add).then_inc(s_var, 1)
            dve.wait_ge(s_sqrt, 1)
            k.link(dve.reciprocal(ss[:, 0:5], ss[:, 0:5]))
            for t, (c, S) in enumerate(TILES):
                dve.tensor_scalar(xin[0:S, t, :], xin[0:S, t, :], ss[0:S, t:t + 1], None, ALU.mult).then_inc(s_xs, 1)
            n = 1

            def x_low(m):
                (c, S), h = TILES[m // 2], m % 2
                dve.wait_ge(s_xh, m + 1)
                dve.tensor_tensor(xl[:, 4 * h:4 * h + 4, c:c + S], xt[m % 2][:, :, 0:S],
                                  xh[:, 4 * h:4 * h + 4, c:c + S].bitcast(F32), ALU.subtract).then_inc(s_xl, 1)

            for t, (c, S) in enumerate(TILES):
                for h in range(2):
                    dve.wait_ge(s_fill, n + 1)
                    if n > 2:
                        dve.wait_ge(s_xl, n - 2)
                    w = cs[:, 4 * h:4 * h + 4, R_NMIX].unsqueeze(2).broadcast_to([P, 4, S])
                    dve.tensor_tensor(xt[(n - 1) % 2][:, :, 0:S],
                                      (pS, pT)[n % 2][:, :].rearrange("p (q s) -> p q s", q=4)[:, :, 0:S], w,
                                      ALU.mult).then_inc(s_xt, 1)
                    dve.wait_ge(s_xt, n)
                    dve.sem_inc(s_fillfree, 1)
                    if n > 1:
                        x_low(n - 2)
                    n += 1
            x_low(n - 2)
            dve.wait_ge(s_wdh, 1)
            dve.tensor_tensor(wdl[:, :, :], wdt, wdh[:, :, :].bitcast(F32), ALU.subtract).then_inc(s_wdl, 1)
            for t in range(2):
                for h in range(2):
                    dve.wait_ge(s_fill, n + 1)
                    dve.tensor_copy(stC[:, 4 * h:4 * h + 4, 120 * t:120 * t + 120],
                                    (pS, pT)[n % 2][:, :].rearrange("p (q s) -> p q s", q=4)[:, :, 0:120])\
                       .then_inc(s_fillfree, 1)
                    n += 1
            for f in range(2):
                dve.wait_ge(s_fill, n + 1)
                dve.tensor_copy(stS[:, 16 * f:16 * f + 16, :],
                                (pS, pT)[n % 2][:, :].rearrange("p (q s) -> p q s", q=16)[:, :, 0:24])\
                   .then_inc(s_fillfree, 1)
                n += 1
            dve.wait_ge(s_const, 4)
            dve.wait_ge(s_dtb, 32)
            dve.wait_ge(s_dtp, 1)
            for ci, (c, S) in enumerate(CHUNKS):
                last = dve.tensor_tensor(dtt[0:S, ci, :], pC[0:S, NH * ci:NH * ci + NH], dtb[0:S, :], ALU.add)
            k.link(last)
            k.link(dve.tensor_scalar(tmp1[:, :, :], dtt[:, :, :], 0.0, None, ALU.max))
            stt(tmp2[:, :, :], tmp1[:, :, :], -2.0, dtt[:, :, :]).then_inc(s_dte, 1)
            dve.wait_ge(s_dtl, 1)
            dve.wait_ge(s_expA, 1)
            k.link(dve.tensor_tensor(dtt[:, :, :], tmp1[:, :, :], tmp2[:, :, :], ALU.add))
            stt(aa[:, :, :], dtt[:, :, :], -1.0, expA[:, :].unsqueeze(1).broadcast_to([P, 6, NH]),
                ALU.mult, ALU.mult).then_inc(s_a, 1)
            dve.wait_ge(s_aah, 1)
            k.link(dve.tensor_tensor(aal[:, :, :], aa[:, :, :], aah[:, :, :].bitcast(F32), ALU.subtract))
            dve.wait_ge(s_te, 7)
            dve.tensor_tensor(tail[:, :, :], tail[:, :, :], dtt[:, :, :], ALU.mult).then_inc(s_pro, 1)
            dve.wait_ge(s_pro, 1)

            with dve.Fori(0, G) as g:
                k.enter(g, DVE_STEPS)

                def split(kk):
                    dve.wait_ge(s_wh, BLOCKS * g + kk + 1)
                    low(dve, kk).then_inc(s_wld, 1)

                def conf_tap(j):
                    wj = gc[:, R_CW + j:R_CW + j + 1]
                    outs = (aout if j == CK - 1 else cacc)
                    o_s = outs[:, 0:SAMP].rearrange("p (b r) -> p b r", b=NSAMP)
                    o_p = outs[:, SAMP:T]
                    i_s, i_p = a_s[:, :, j:j + TSAMP], a_p[:, j:j + PROMPT]
                    if j == CK - 1:
                        dve.wait_ge(s_ast, 16 * g + 1)
                    if j == 0:
                        bias = gc[:, R_CB:R_CB + 1]
                        dve.tensor_scalar(o_s, i_s, wj, bias, ALU.mult, ALU.add)
                        k.link(dve.tensor_scalar(o_p, i_p, wj, bias, ALU.mult, ALU.add))
                    else:
                        stt(o_s, i_s, wj, cacc[:, 0:SAMP].rearrange("p (b r) -> p b r", b=NSAMP))
                        ins = stt(o_p, i_p, wj, cacc[:, SAMP:T])
                        if j == CK - 1:
                            ins.then_inc(s_cconv, 1)
                        else:
                            k.link(ins)

                def ssm_conv(q):
                    r = R_X + 5 * q
                    dve.wait_ge(s_ufree, U_TILES * g + 1 + q + 1)
                    dve.wait_ge(s_raw, 4 * g + q + 1)
                    dve.wait_ge(s_sts, 4 * g + q + 1)
                    o_s = cv[:, q, 0:SAMP].rearrange("p (b r) -> p b r", b=NSAMP)
                    o_p = cv[:, q, SAMP:T]
                    for j in range(SK):
                        wj = gc[:, r + j:r + j + 1]
                        i_s, i_p = raw_s[:, q, :, j:j + TSAMP], raw_p[:, q, j:j + PROMPT]
                        if j == 0:
                            bias = gc[:, r + SK:r + SK + 1]
                            dve.tensor_scalar(o_s, i_s, wj, bias, ALU.mult, ALU.add)
                            k.link(dve.tensor_scalar(o_p, i_p, wj, bias, ALU.mult, ALU.add))
                        else:
                            stt(o_s, i_s, wj, o_s)
                            ins = stt(o_p, i_p, wj, o_p)
                            if j == SK - 1:
                                ins.then_inc(s_conv, 1)
                            else:
                                k.link(ins)

                def silu(q):
                    dve.wait_ge(s_thx, 4 * g + q + 1)
                    stt(cv[:, q, :], th[:, q % 2, :], 1.0, cv[:, q, :], ALU.add, ALU.mult).then_inc(s_cv, 1)

                def stage1(j):
                    ci = ORDER[j]
                    S = CHUNKS[ci][1]
                    um = (Ub if ci == 0 else U)[0:S, 0:S]
                    dve.wait_ge(s_T, 6 * g + j + 1)
                    k.link(dve.tensor_tensor(cbm[0:S, 0:S], Tt[0:S, 3, 0:S], um, ALU.mult))
                    dt4 = dtt[0:S, ci, bass.ds(HG * g, HG)].unsqueeze(2).broadcast_to([S, HG, HD])
                    dve.tensor_tensor(xdt[0:S, :, :], Tt[0:S, 0:2, :].rearrange("s i (h p) -> s (i h) p", h=2),
                                      dt4, ALU.mult)
                    dve.tensor_tensor(Lx[0:S, :, 0:S], Lx[0:S, :, 0:S],
                                      cbm[0:S, 0:S].unsqueeze(1).broadcast_to([S, HG, S]),
                                      ALU.mult).then_inc(s_W, 1)

                def stage2(j):
                    ci = ORDER[j]
                    c, S = CHUNKS[ci]
                    dve.wait_ge(s_pe2, 6 * g + j + 2)
                    yv = pY[:, 0:2 * P].rearrange("p (i t) -> p i t", i=2)[:, :, 0:S]
                    if ci == 1:
                        for i in range(2):
                            stt(ybuf[:, i, c:c + S], cv[:, i, c:c + S], gc[:, R_DS + i:R_DS + i + 1], yv[:, i, :])
                    else:
                        v = yi[:, :, 0:S]
                        k.link(dve.tensor_tensor(v, pC[:, 0:2 * P].rearrange("p (i t) -> p i t", i=2)[:, :, 0:S],
                                                 Ed[:, :, c:c + S], ALU.mult))
                        k.link(dve.tensor_tensor(v, v, yv, ALU.add))
                        for i in range(2):
                            last = stt(ybuf[:, i, c:c + S], cv[:, i, c:c + S], gc[:, R_DS + i:R_DS + i + 1],
                                       yi[:, i, 0:S])
                    st = pC[:, 2 * P:4 * P].rearrange("p (h q) -> p h q", h=HG)
                    if ci == 1:
                        last = dve.tensor_copy(hT[:, :, :], st)
                    elif ci > 1:
                        dve.wait_ge(s_hTd, 4 * g + j)
                        last = dve.tensor_tensor(hT[:, :, :], hTd[:, :, :], st, ALU.add)
                    last.then_inc(s_y, 1)

                dve.wait_ge(s_gc, g + 1)
                dve.wait_ge(s_y, 6 * g + 1)
                for q in range(4):
                    ssm_conv(q)
                    if q:
                        silu(q - 1)
                silu(3)
                split(6)
                dve.wait_ge(s_ufree, U_TILES * g + 6 + 1)
                dve.wait_ge(s_stc, g + 1)
                dve.wait_ge(s_pk, 7 * g + 1)
                dve.wait_ge(s_cconv, g + 1)
                stt(a_s[:, :, CK - 1:], zc[:, 1, 0:SAMP].rearrange("p (b r) -> p b r", b=NSAMP), 1.0,
                    zc[:, 0, 0:SAMP].rearrange("p (b r) -> p b r", b=NSAMP), ALU.add, ALU.mult).then_inc(s_ga, 1)
                stt(a_p[:, CK - 1:], zc[:, 1, SAMP:T], 1.0, zc[:, 0, SAMP:T], ALU.add, ALU.mult).then_inc(s_ga, 1)
                dve.wait_ge(s_ga, 2 * g + 2)
                split(7)
                tap = iter(range(CK))

                def taps(n):
                    for _ in range(n):
                        conf_tap(next(tap))

                taps(2)
                stage1(0)
                taps(2)
                stage2(0)
                for j in range(1, 6):
                    stage1(j)
                    if j in (1, 3):
                        split(8 + j // 2)
                    if j < 5:
                        taps(2)
                        stage2(j)
                dve.wait_ge(s_z, 2 * g + 2)
                dve.wait_ge(s_ufree, U_TILES * g + 10 + 1)
                k.link(stt(zc[:, :, :], th[:, :, :], 1.0, zc[:, :, :], ALU.add, ALU.mult))
                taps(8)
                stage2(5)
                dve.wait_ge(s_y, 6 * g + 6 + 1)
                stt(ybuf[:, :, :], ybuf[:, :, :], 0.5, zc[:, :, :], ALU.mult, ALU.mult).then_inc(s_yz, 1)
                for r in range(4):
                    dve.wait_ge(s_hs, 4 * g + r + 2)
                    dve.wait_ge(s_h0t, 4 * g + 4)
                    for b in range(4):
                        bb, i = 4 * (r % 2) + b, r // 2
                        last = stt(h0[:, i, bb, :], h0[:, i, bb, :],
                                   Ed[:, i, TSAMP * bb + TSAMP - 1:TSAMP * bb + TSAMP],
                                   (pS, pT)[r % 2][:, P * b:P * b + P])
                    last.then_inc(s_hnew, 1)
                taps(4)
                dve.wait_ge(s_ufree, U_TILES * g + 14 + 1)
                dve.reciprocal(zc[:, 1, :], zc[:, 0, :]).then_inc(s_rec, 1)
                dve.wait_ge(s_rec, g + 1)
                dve.wait_ge(s_yst, 16 * g + 1)
                for i in range(2):
                    stt(yout[:, i, :], ybuf[:, i, :], gc[:, R_NW + i:R_NW + i + 1], zc[:, 1, :],
                        ALU.mult, ALU.mult).then_inc(s_yn, 1)
                taps(7)
                assert next(tap, None) is None
                k.leave(G)


OT = [(0, SAMP)] + CHUNKS[2:]
NT = len(OT)
ROW = [0] + [SAMP + P * t for t in range(NT - 1)]
NE, NGR, EPG, DE = 32, 4, 8, 256
SLOT = 128
PAIRS = 2 * (SAMP + SEQ)
NTILE = NE + (PAIRS - NE) // SLOT
NSORT = -(-PAIRS // P)
MAXT = -(-(SAMP + SEQ) // SLOT)
BIG = 3.0e38


def mixer(nc, A, O, keep):
    cs, x1, ones = keep["cs"], keep["x1"], keep["ones"]
    with ExitStack() as ctx:
        def sb(name, shape, dt=F32):
            return ctx.enter_context(nc.sbuf_tensor(name, shape, dt))

        sem = ctx.enter_context(semaphores(nc))

        SSM, CONF, WO = KD, KD // 2, 4
        wraw = keep["wraw"]
        vh, vl = sb("vh", [P, 2, 2 * D], F32R), sb("vl", [P, 2, 2 * D], F32R)
        yh, yl = sb("yh", [P, 2 * KD, T], F32R), sb("yl", [P, 2 * KD, T], F32R)
        ah, al, mh, ml = yh[:, 0:KD, :], yl[:, 0:KD, :], yh[:, KD:, :], yl[:, KD:, :]
        YR = 3
        yraw = sb("yraw", [P, YR, 2, T])
        aconv = sb("aconv", [P, KD, T])
        mg = sb("mg", [P, KD, T])
        gt = sb("gt", [P, 4, T])
        sq = sb("sq", [P, 2, T])
        rs = sb("rs", [P, T])
        rr = sb("rr", [P, T])
        mean, ya = rr, sq
        ss2 = sb("ss2", [P, 8])
        pm = [ctx.enter_context(nc.psum_tensor(f"pm{i}", [P, 1024], F32)) for i in range(2)]
        pst = ctx.enter_context(nc.psum_tensor("pst", [P, 1024], F32))
        po = ctx.enter_context(nc.psum_tensor("po", [P, 1024], F32))
        s_w = [sem(f"m_w{i}") for i in range(2)]
        s_yr = [sem(f"m_yr{i}") for i in range(YR)]
        s_g = [sem(f"m_g{i}") for i in range(4)]
        s_xr, s_p, s_stat, s_mean, s_cen, s_sq, s_inv, s_root, s_tan, s_act, s_ya, s_gfree, s_mg, s_o, \
            s_x1, s_ssq, s_var, s_sd = map(sem, (
                "m_xr", "m_p", "m_stat", "m_mean", "m_cen", "m_sq", "m_inv", "m_root",
                "m_tan", "m_act", "m_ya", "m_gfree", "m_mg", "m_o", "m_x1", "m_ssq", "m_var", "m_sd"))
        s_lin, s_rinv, s_sqf, s_ss, s_ac, s_wo = map(sem, ("m_lin", "m_rinv", "m_sqf", "m_ss", "m_ac", "m_wo"))
        s_vh, s_vl, s_yh, s_yl, s_ah, s_al, s_mh, s_ml = map(
            sem, ("m_vh", "m_vl", "m_yh", "m_yl", "m_ah", "m_al", "m_mh", "m_ml"))
        c_dve = sem("m_dve")
        block = ctx.enter_context(nc.Block())

        def cols(ps, a, b):
            return ps[:, UO + a:UO + b]

        def bank(h, t):
            n = (NT * h + t) % 8
            return (pm[0], pm[1], po, pst)[n // 2][:, 512 * (n % 2):512 * (n % 2) + 512]

        def unread(S):
            return gt[0:S, :, :].rearrange("p a b -> p (a b)")[:, 0:D]

        def slot_done(eng, m):
            if m < SSM:
                eng.wait_ge(s_p, m + 1)
            elif m < SSM + CONF:
                eng.wait_ge(s_p, SSM + 2 * (m - SSM) + 2)
            elif m == SSM + CONF:
                eng.wait_ge(s_wo, 1)
            else:
                eng.wait_ge(s_o, NT)

        @block.sync
        def _(sp):
            def weights(m):
                if m >= 2:
                    sp.wait_ge(s_vl, m - 1)
                if m < SSM:
                    src = A["ssm_out_w"][0].rearrange("(k p) n -> p k n", p=P)[:, :, P * m:P * m + P]
                elif m < SSM + CONF:
                    n = m - SSM
                    src = A["conf_out_w"][0].rearrange("(k p) n -> p k n", p=P)[:, :, 2 * P * n:2 * P * n + 2 * P]
                else:
                    h, k = (m - SSM - CONF) // 2, (m - SSM - CONF) % 2
                    src = A["w_o"][0].rearrange("(k p) n -> p k n", p=P)[:, 4 * k:4 * k + 4, 512 * h:512 * h + 512]
                dst = wraw[:, m % 2, :].rearrange("p (k n) -> p k n", k=src.shape[1])
                sp.dma_start(dst, src).then_inc(s_w[m % 2], 16)

            for n in range(KD):
                if n >= YR:
                    sp.wait_ge(s_yl, n - YR + 1)
                sp.dma_start(yraw[:, n % YR], keep["yrows"][n].rearrange("i p t -> p i t")).then_inc(s_yr[n % YR], 16)
            sp.dma_start(aconv[:, :, :], keep["aconv"].rearrange("k p t -> p k t")).then_inc(s_ac, 16)
            for m in range(2, SSM + CONF + WO):
                weights(m)
                if m == SSM:
                    sp.dma_start(x1[0:SAMP, 0, :], A["x_sample"].rearrange("b t d -> (b t) d")).then_inc(s_xr, 16)
                    sp.dma_start(x1[:, 1:NT, :],
                                 A["x_prompt"][0].rearrange("(t p) d -> p t d", p=P)).then_inc(s_xr, 16)

        @block.gpsimd
        def _(pool):
            for n in range(2 * KD):
                if n >= 4:
                    pool.wait_ge(s_gfree, n - 3)
                pool.dma_start(gt[:, n % 4, :], keep["gates"][1 - n // KD, n % KD]).then_inc(s_g[n % 4], 16)

        @block.tensor
        def _(pe):
            def sum_block(ps, j, rhs):
                for a, b in ((0, USPLIT), (USPLIT, T)):
                    last = pe.matmul(cols(ps, a, b), ones[:, :], rhs[:, a:b], start=(j == 0), stop=(j == KD - 1))
                return last

            def product(r, m, w_cols, hi, lo, K, split_sem, per):
                if 2 <= r < KD + 2:
                    pe.wait_ge(s_gfree, r - 1)
                elif r >= KD + 2:
                    pe.wait_ge(s_ya, r - KD - 1)
                pe.wait_ge(s_vl, m + 1)
                for j in range(K):
                    if r in (0, KD):
                        pe.wait_ge(split_sem, j // per + 1)
                    for n, (w, x) in enumerate(((vh, hi), (vh, lo), (vl, hi))):
                        for a, b in ((0, USPLIT), (USPLIT, T)):
                            last = pe.matmul(cols(pm[r % 2], a, b), w[:, m % 2, w_cols(j)], x[:, j, a:b],
                                             start=(j == 0 and n == 0), stop=(j == K - 1 and n == 2))
                last.then_inc(s_p, 1)

            for n in range(SSM):
                product(n, n, lambda j: slice(P * j, P * j + P), yh, yl, 2 * KD, s_yl, 2)
                if n == 1:
                    pe.wait_ge(s_ac, 16)
                    for j in range(KD):
                        last = sum_block(pst, j, aconv[:, j, :])
                    last.then_inc(s_stat, 1)
                if n == 2:
                    for j in range(KD):
                        pe.wait_ge(s_sq, j + 1)
                        sum_block(po, j, sq[:, j % 2, :]).then_inc(s_sqf, 1)
            for n in range(KD):
                product(KD + n, SSM + n // 2,
                        lambda j, n=n: slice(2 * P * j + P * (n % 2), 2 * P * j + P * (n % 2) + P), ah, al, KD, s_al, 1)
            for m in range(SSM + CONF, SSM + CONF + WO):
                h, kk = (m - SSM - CONF) // 2, (m - SSM - CONF) % 2
                pe.wait_ge(s_vl, m + 1)
                pe.wait_ge(s_ml, 4 * kk + 4)
                for t, (c, S) in enumerate(OT):
                    if h == 0 and kk == 0:
                        pe.wait_ge(s_ya, KD - 1 if t < 2 else KD)
                    if NT * h + t >= 8 and kk == 0:
                        pe.wait_ge(s_x1, NT * h + t - 7)
                    for k in range(4):
                        for n, (x, w) in enumerate(((mh, vh), (ml, vh), (mh, vl))):
                            last = pe.matmul(bank(h, t)[0:S, :], x[:, 4 * kk + k, c:c + S],
                                             w[:, m % 2, 512 * k:512 * k + 512],
                                             start=(kk == 0 and k == 0 and n == 0), stop=(kk == 1 and k == 3 and n == 2))
                    if kk == 1:
                        last.then_inc(s_o, 1)
                if m == SSM + CONF:
                    last.then_inc(s_wo, 1)

        @block.scalar
        def _(act):
            def high(m):
                if m >= 2:
                    act.wait_ge(s_w[m % 2], 16 * (m // 2))
                    slot_done(act, m - 2)
                act.activation(vh[:, m % 2, :], wraw[:, m % 2, :], ACT.Copy).then_inc(s_vh, 1)

            high(0)
            for n in range(KD):
                act.wait_ge(s_yr[n % YR], 16 * (n // YR + 1))
                act.activation(yh[:, 2 * n:2 * n + 2, :], yraw[:, n % YR], ACT.Copy).then_inc(s_yh, 1)
            high(1)
            high(2)
            high(3)
            act.wait_ge(s_stat, 1)
            act.activation(mean[:, :], cols(pst, 0, T), ACT.Copy, scale=1.0 / D).then_inc(s_mean, 1)
            for j in range(KD):
                act.wait_ge(s_cen, j + 1)
                if j >= 2:
                    act.wait_ge(s_sqf, j - 1)
                act.activation(sq[:, j % 2, :], aconv[:, j, :], ACT.Square).then_inc(s_sq, 1)
            high(4)
            act.wait_ge(s_inv, 1)
            act.activation(rs[:, :], rr[:, :], ACT.Sqrt).then_inc(s_root, 1)
            for j in range(KD):
                act.wait_ge(s_lin, j + 1)
                if j >= 2:
                    act.wait_ge(s_act, j - 1)
                act.activation(sq[:, j % 2, :], aconv[:, j, :], ACT.Tanh, scale=0.5).then_inc(s_tan, 1)
                if j % 2 == 1:
                    high(5 + j // 2)
            for j in range(KD):
                act.wait_ge(s_act, j + 1)
                act.wait_ge(s_p, SSM)
                act.activation(ah[:, j, :], aconv[:, j, :], ACT.Copy).then_inc(s_ah, 1)
            high(9)

            def merged_high(n):
                act.wait_ge(s_mg, n + 1)
                act.activation(mh[:, n, :], mg[:, n, :], ACT.Copy).then_inc(s_mh, 1)

            for n in range(KD):
                act.wait_ge(s_p, KD + n + 1)
                if n >= 2:
                    act.wait_ge(s_mg, n - 1)
                act.activation(ya[:, n % 2, :], cols(pm[n % 2], 0, T), ACT.Identity, scale=0.5,
                               bias=cs[:, n, R_OB:R_OB + 1]).then_inc(s_ya, 1)
                if n % 2 == 1:
                    high(10 + n // 2)
                if n:
                    merged_high(n - 1)
            merged_high(KD - 1)
            high(14)
            high(15)
            act.wait_ge(s_ss, 1)
            for t, (c, S) in enumerate(OT):
                act.wait_ge(s_x1, NT + t + 1)
                if t:
                    act.wait_ge(s_ssq, t)
                act.activation(unread(S), x1[0:S, t, :], ACT.Square, accum_out=ss2[0:S, t:t + 1]).then_inc(s_ssq, 1)
            act.wait_ge(s_var, 1)
            act.activation(ss2[:, 0:NT], ss2[:, 0:NT], ACT.Sqrt).then_inc(s_sd, 1)

        @block.vector
        def _(dve):
            k = Steps(dve, c_dve)

            def stt(out, in0, scalar, in1, op0=ALU.mult, op1=ALU.add):
                return dve.scalar_tensor_tensor(out=out, in0=in0, scalar=scalar, in1=in1, op0=op0, op1=op1)

            def rest(out, whole, high):
                return dve.tensor_tensor(out, whole, high.bitcast(F32), ALU.subtract)

            def low(m):
                dve.wait_ge(s_vh, m + 1)
                rest(vl[:, m % 2, :], wraw[:, m % 2, :], vh[:, m % 2, :]).then_inc(s_vl, 1)

            def ssm_block(n):
                dve.wait_ge(s_p, n + 1)
                dve.wait_ge(s_g[n % 4], 16 * (n // 4 + 1))
                stt(mg[:, n, :], gt[:, n % 4, :], 1.0, cols(pm[n % 2], 0, T), ALU.add, ALU.mult).then_inc(s_gfree, 1)

            dve.memset(ss2[:, :], 1.0).then_inc(s_ss, 1)
            low(0)
            for n in range(KD):
                dve.wait_ge(s_yh, n + 1)
                rest(yl[:, 2 * n:2 * n + 2, :], yraw[:, n % YR], yh[:, 2 * n:2 * n + 2, :]).then_inc(s_yl, 1)
            low(1)
            for n in range(2):
                ssm_block(n)
                low(n + 2)
            dve.wait_ge(s_mean, 1)
            for j in range(KD):
                dve.tensor_tensor(aconv[:, j, :], aconv[:, j, :], mean[:, :], ALU.subtract).then_inc(s_cen, 1)
            ssm_block(2)
            low(4)
            dve.wait_ge(s_sqf, KD)
            k.link(dve.tensor_scalar(rs[:, :], cols(po, 0, T), 1.0 / D, EPS, ALU.mult, ALU.add))
            dve.reciprocal(rr[:, :], rs[:, :]).then_inc(s_inv, 1)
            dve.wait_ge(s_root, 1)

            for j in range(KD):
                k.link(stt(aconv[:, j, :], aconv[:, j, :], cs[:, j, R_LG:R_LG + 1], rs[:, :], ALU.mult, ALU.mult))
                dve.tensor_scalar(aconv[:, j, :], aconv[:, j, :], cs[:, j, R_LB:R_LB + 1], None,
                                  ALU.add).then_inc(s_lin, 1)
                if j:
                    dve.wait_ge(s_tan, j)
                    stt(aconv[:, j - 1, :], sq[:, (j - 1) % 2, :], 1.0, aconv[:, j - 1, :],
                        ALU.add, ALU.mult).then_inc(s_act, 1)
                if j % 2 == 1:
                    ssm_block(3 + j // 2)
                    low(5 + j // 2)
            dve.wait_ge(s_tan, KD)
            stt(aconv[:, KD - 1, :], sq[:, (KD - 1) % 2, :], 1.0, aconv[:, KD - 1, :],
                ALU.add, ALU.mult).then_inc(s_act, 1)
            for j in range(KD):
                dve.wait_ge(s_ah, j + 1)
                rest(al[:, j, :], aconv[:, j, :], ah[:, j, :]).then_inc(s_al, 1)
            ssm_block(KD - 1)
            low(9)

            def merged_low(n):
                dve.wait_ge(s_mh, n + 1)
                rest(ml[:, n, :], mg[:, n, :], mh[:, n, :]).then_inc(s_ml, 1)

            for n in range(KD):
                dve.wait_ge(s_ya, n + 1)
                m = KD + n
                dve.wait_ge(s_g[m % 4], 16 * (m // 4 + 1))
                k.link(stt(ya[:, n % 2, :], gt[:, m % 4, :], 1.0, ya[:, n % 2, :], ALU.add, ALU.mult))
                dve.sem_inc(s_gfree, 1)
                dve.wait_ge(s_gfree, KD)
                dve.tensor_tensor(mg[:, n, :], mg[:, n, :], ya[:, n % 2, :], ALU.add).then_inc(s_mg, 1)
                if n % 2 == 1:
                    low(10 + n // 2)
                if n:
                    merged_low(n - 1)
            merged_low(KD - 1)
            dve.wait_ge(s_xr, 32)
            for h in range(2):
                low(14 + h)
                for t, (c, S) in enumerate(OT):
                    dve.wait_ge(s_o, NT * h + t + 1)
                    v = x1[0:S, t, 512 * h:512 * h + 512]
                    stt(v, bank(h, t)[0:S, :], 0.5, v).then_inc(s_x1, 1)
            dve.wait_ge(s_ssq, NT)
            dve.tensor_scalar(ss2[:, 0:NT], ss2[:, 0:NT], 1.0 / D, EPS, ALU.mult, ALU.add).then_inc(s_var, 1)
            dve.wait_ge(s_sd, 1)
            dve.reciprocal(keep["rstd"][:, 0:NT], ss2[:, 0:NT]).then_inc(s_rinv, 1)


def route(nc, A, O, keep):
    x1, ident, ones, pos, wgt = (keep[n] for n in ("x1", "ident", "ones", "pos", "wgt"))
    with ExitStack() as ctx:
        def sb(name, shape, dt=F32):
            return ctx.enter_context(nc.sbuf_tensor(name, shape, dt))

        sem = ctx.enter_context(semaphores(nc))

        NL = NGR + NE
        xs = sb("xs", [P, 2, D])
        nw = sb("nw", [P, D])
        xT = sb("xT", [P, 2, KD, P])
        wr = sb("wr", [P, KD, NL])
        rb = sb("rb", [P, NL])
        lg = sb("lg", [P, NT, NL])
        gm = sb("gm", [P, NT])
        sg = sb("sg", [P, NT, NGR])
        eqg = sb("eqg", [P, NT, NGR])
        og = sb("og", [P, NT, NGR])
        gp = sb("gp", [P, NT])
        ei = sb("ei", [P, NT, EPG])
        et = sb("et", [P, NT, EPG])
        m12 = sb("m12", [P, 2, NT])
        sc = sb("sc", [P, NT, EPG])
        ok = sb("ok", [P, 2, NT, EPG])
        rank = sb("rank", [P, EPG])
        valid = sb("valid", [P, NT])
        OH = sb("OH", [P, 2, NT, NE])
        pre = sb("pre", [P, 2 * NT, NE])
        run = sb("run", [P, 2 * NT + 1, NE])
        ntl = sb("ntl", [P, NE])
        tend = sb("tend", [P, NE])
        base = sb("base", [P, NE])
        zer = sb("zer", [P, NE])
        posf = sb("posf", [P, 2 * NT])
        ti = sb("ti", [1, NTILE])
        cmp = sb("cmp", [1, NTILE, NE])
        exf = sb("exf", [1, NTILE])
        SU = sb("SU", [P, P])
        tokid = sb("tokid", [P, NT], U32)
        zu = sb("zu", [NSORT, P], U32)
        srow = sb("srow", [NSORT, P], U32)
        srowf = sb("srowf", [NSORT, P])
        start = sb("start", [P, NE])
        place = sb("place", [P, 2 * NT], U32)
        part = sb("part", [P, 2 * NT, NE])
        px = [ctx.enter_context(nc.psum_tensor(f"rx{i}", [P, 512], F32)) for i in range(2)]
        pl, pc, pt = (ctx.enter_context(nc.psum_tensor(n, [P, 512], F32)) for n in ("rl", "rc", "rt"))
        pc2 = ctx.enter_context(nc.psum_tensor("rc2", [P, 512], F32))
        s_wr, s_rb, s_cst, s_xs, s_t, s_tf, s_l, s_e, s_x, s_oh, s_cnt, s_pos, s_z, s_sct, s_row, s_rowf, \
            s_rt, s_done, s_tok = map(sem, (
                "r_wr", "r_rb", "r_cst", "r_xs", "r_t", "r_tf", "r_l", "r_e", "r_x", "r_oh",
                "r_cnt", "r_pos", "r_z", "r_sct", "r_row", "r_rowf", "r_rt", "r_done", "r_tok"))
        s_nw, s_x1 = sem("r_nw"), sem("r_x1")
        s_xst = [sem(f"r_xst{b}") for b in range(2)]
        c_dve, c_pool = sem("r_dve"), sem("r_pool")
        block = ctx.enter_context(nc.Block())

        @block.sync
        def _(sp):
            sp.dma_start(nw[:, :], A["norm_ffn_w"][0].partition_broadcast(P)).then_inc(s_nw, 16)
            for a, b, w, bias in ((0, NGR, A["router_group_w"], A["router_group_b"]),
                                  (NGR, NL, A["router_expert_w"], A["router_expert_b"])):
                sp.dma_start(wr[:, :, a:b], w[0].rearrange("(k p) n -> p k n", p=P)).then_inc(s_wr, 16)
                sp.dma_start(rb[:, a:b], bias[0].partition_broadcast(P)).then_inc(s_rb, 16)
            for t, (c, S) in enumerate(OT):
                sp.wait_ge(s_xs, t + 1)
                sp.dma_start(keep["xs"][ROW[t]:ROW[t] + S, :], xs[0:S, t % 2, :]).then_inc(s_xst[t % 2], 16)
            sp.dma_start(keep["x1_rows"][ROW[0]:ROW[0] + SAMP, :], x1[0:SAMP, 0, :]).then_inc(s_x1, 16)
            sp.dma_start(keep["x1_rows"][SAMP:, :].rearrange("(t p) d -> p t d", p=P), x1[:, 1:, :]).then_inc(s_x1, 16)
            for b in range(2):
                sp.wait_ge(s_xst[b], 16 * ((NT + 1 - b) // 2))
            sp.wait_ge(s_x1, 32)

        @block.gpsimd
        def _(pool):
            k = Steps(pool, c_pool)
            pool.iota(rank[:, :], [[-1, EPG]], base=EPG, channel_multiplier=0, allow_small_or_imprecise_dtypes=True).then_inc(s_cst, 1)
            pool.iota(ti[:, :], [[1, NTILE]], base=0, channel_multiplier=0, allow_small_or_imprecise_dtypes=True).then_inc(s_cst, 1)
            pool.iota(tokid[:, 0:1], [[0, 1]], base=0, channel_multiplier=1).then_inc(s_cst, 1)
            pool.iota(tokid[:, 1:NT], [[P, NT - 1]], base=ROW[1], channel_multiplier=1).then_inc(s_cst, 1)
            k.link(pool.memset(valid[:, :], 1.0))
            pool.affine_select(out=valid[:, 0:1], in_=valid[:, 0:1], compare_op=ALU.is_ge, fill=0.0,
                               base=SAMP - 1, pattern=[[0, 1]], channel_multiplier=-1).then_inc(s_cst, 1)
            k.link(pool.memset(SU[:, :], 1.0))
            pool.affine_select(out=SU[:, :], in_=SU[:, :], compare_op=ALU.is_gt, fill=0.0, base=0,
                               pattern=[[1, P]], channel_multiplier=-1).then_inc(s_cst, 1)
            pool.memset(lg[:, 0, :], 0.0).then_inc(s_cst, 1)
            pool.memset(zer[:, :], 0.0).then_inc(s_cst, 1)
            k.link(pool.memset(zu[:, :], 0))
            pool.dma_start(keep["sorted"].rearrange("(i p) o -> i (p o)", p=P), zu[:, :]).then_inc(s_z, 16)
            pool.wait_ge(s_z, 16)
            pool.wait_ge(s_cst, 8)
            pool.wait_ge(s_pos, 1)
            for q in range(2):
                for t, (c, S) in enumerate(OT):
                    pool.indirect_dma_start(
                        out=keep["sorted"], out_offset=bass.IndirectOffsetOnAxis(ap=place[0:S, NT * q + t:NT * q + t + 1], axis=0),
                        in_=tokid[0:S, t:t + 1], in_offset=None).then_inc(s_sct, 16)
            pool.wait_ge(s_sct, 16 * 2 * NT)
            pool.dma_start(srow[:, :], keep["sorted"].rearrange("(i p) o -> i (p o)", p=P)).then_inc(s_row, 16)

        @block.tensor
        def _(pe):
            def turn(t):
                S = OT[t][1]
                pe.wait_ge(s_xs, t + 1)
                for h in range(2):
                    n = 2 * t + h
                    if n >= 2:
                        pe.wait_ge(s_tf, n - 1)
                    for q in range(4):
                        last = pe.transpose(px[n % 2][:, P * q:P * q + S], xs[0:S, t % 2, P * (4 * h + q):P * (4 * h + q) + P],
                                            ident[0:S, 0:S])
                    last.then_inc(s_t, 1)

            turn(0)
            for t, (c, S) in enumerate(OT):
                if t + 1 < NT:
                    turn(t + 1)
                pe.wait_ge(s_tf, 2 * t + 2)
                pe.wait_ge(s_wr, 32)
                for j in range(KD):
                    last = pe.matmul(pl[0:S, NL * t:NL * t + NL], xT[:, t % 2, j, 0:S], wr[:, j, :],
                                     start=(j == 0), stop=(j == KD - 1))
                last.then_inc(s_l, 1)
            pe.wait_ge(s_oh, 1)
            pe.wait_ge(s_cst, 8)
            ohv = OH[:, :, :, :].rearrange("p a t e -> p (a t e)")
            pe.matmul(pc[:, 0:2 * NT * NE], SU[:, :], ohv, start=True, stop=True)
            pe.matmul(pc2[:, 0:2 * NT * NE], ones[:, :], ohv, start=True, stop=True).then_inc(s_cnt, 1)
            pe.wait_ge(s_rowf, 1)
            pe.transpose(pt[:, 0:NSORT], srowf[:, :], ident[0:NSORT, 0:NSORT]).then_inc(s_rt, 1)

        @block.scalar
        def _(act):
            act.wait_ge(s_e, 1)
            act.activation(sg[:, :, :], sg[:, :, :], ACT.Exp).then_inc(s_x, 1)
            act.activation(gp[:, :], gp[:, :], ACT.Exp).then_inc(s_x, 1)

        @block.vector
        def _(dve):
            k = Steps(dve, c_dve)

            def tt(out, a, b, op):
                k.link(dve.tensor_tensor(out, a, b, op))

            def stt(out, in0, scalar, in1, op0=ALU.mult, op1=ALU.add):
                k.link(dve.scalar_tensor_tensor(out=out, in0=in0, scalar=scalar, in1=in1, op0=op0, op1=op1))

            def red(out, in_, op):
                k.link(dve.tensor_reduce(out, in_, AX_X, op))

            def normed(t):
                S = OT[t][1]
                if t >= 2:
                    dve.wait_ge(s_xst[t % 2], 16 * (t // 2))
                    dve.wait_ge(s_t, 2 * t - 2)
                dve.scalar_tensor_tensor(out=xs[0:S, t % 2, :], in0=x1[0:S, t, :], scalar=keep["rstd"][0:S, t:t + 1],
                                         in1=nw[0:S, :], op0=ALU.mult, op1=ALU.mult).then_inc(s_xs, 1)

            dve.wait_ge(s_nw, 16)
            normed(0)
            for t, (c, S) in enumerate(OT):
                if t + 1 < NT:
                    normed(t + 1)
                for h in range(2):
                    n = 2 * t + h
                    dve.wait_ge(s_t, n + 1)
                    if t >= 2:
                        dve.wait_ge(s_l, t - 1)
                    dve.tensor_copy(xT[:, t % 2, 4 * h:4 * h + 4, 0:S],
                                    px[n % 2][:, :].rearrange("p (q s) -> p q s", q=4)[:, :, 0:S]).then_inc(s_tf, 1)
            dve.wait_ge(s_rb, 32)
            dve.wait_ge(s_l, NT)
            dve.wait_ge(s_cst, 8)
            for t, (c, S) in enumerate(OT):
                tt(lg[0:S, t, :], pl[0:S, NL * t:NL * t + NL], rb[0:S, :], ALU.add)

            def bc(ap, n):
                return ap.unsqueeze(2).broadcast_to([P, NT, n])

            def first_of(onehot, equal, n):
                r = rank[:, EPG - n:EPG].unsqueeze(1).broadcast_to([P, NT, n])
                tt(equal, equal, r, ALU.mult)
                red(gm[:, :], equal, ALU.max)
                tt(onehot, equal, bc(gm[:, :], n), ALU.is_equal)

            g = lg[:, :, 0:NGR]
            red(gm[:, :], g, ALU.max)
            tt(sg[:, :, :], g, bc(gm[:, :], NGR), ALU.subtract)
            tt(eqg[:, :, :], g, bc(gm[:, :], NGR), ALU.is_equal)
            first_of(og[:, :, :], eqg[:, :, :], NGR)
            for q in range(NGR):
                e = lg[:, :, NGR + EPG * q:NGR + EPG * q + EPG]
                if q == 0:
                    tt(ei[:, :, :], e, bc(og[:, :, q], EPG), ALU.mult)
                else:
                    tt(et[:, :, :], e, bc(og[:, :, q], EPG), ALU.mult)
                    tt(ei[:, :, :], ei[:, :, :], et[:, :, :], ALU.add)
            red(m12[:, 0, :], ei[:, :, :], ALU.max)
            tt(sc[:, :, :], ei[:, :, :], bc(m12[:, 0, :], EPG), ALU.is_equal)
            first_of(ok[:, 0], sc[:, :, :], EPG)
            stt(ei[:, :, :], ok[:, 0], -BIG, ei[:, :, :])
            red(m12[:, 1, :], ei[:, :, :], ALU.max)
            tt(sc[:, :, :], ei[:, :, :], bc(m12[:, 1, :], EPG), ALU.is_equal)
            first_of(ok[:, 1], sc[:, :, :], EPG)
            dve.tensor_tensor(gp[:, :], m12[:, 1, :], m12[:, 0, :], ALU.subtract).then_inc(s_e, 1)
            for q in range(2):
                for b in range(NGR):
                    tt(OH[:, q, :, EPG * b:EPG * b + EPG], ok[:, q], bc(og[:, :, b], EPG), ALU.mult)
                tt(OH[:, q], OH[:, q], bc(valid[:, :], NE), ALU.mult)
            dve.sem_inc(s_oh, 1)
            dve.wait_ge(s_x, 2)
            red(gm[:, :], sg[:, :, :], ALU.add)
            stt(gm[:, :], gp[:, :], 1.0, gm[:, :], ALU.add, ALU.mult)
            k.link(dve.reciprocal(wgt[:, 0, :], gm[:, :]))
            k.link(dve.tensor_scalar(wgt[:, 0, :], wgt[:, 0, :], 0.5, None, ALU.mult))
            tt(wgt[:, 1, :], wgt[:, 0, :], gp[:, :], ALU.mult)
            dve.wait_ge(s_cnt, 1)
            k.link(dve.memset(run[:, 0, :], 0.0))
            for n in range(2 * NT):
                tt(run[:, n + 1, :], run[:, n, :], pc2[:, NE * n:NE * n + NE], ALU.add)
            cnt = run[:, 2 * NT, :]
            ohp = OH[:, :, :, :].rearrange("p a t e -> p (a t) e")
            k.link(dve.tensor_tensor_scan(start[:, :], cnt, zer[:, :], 0.0, ALU.add, ALU.add))
            tt(start[:, :], start[:, :], cnt, ALU.subtract)
            tt(pre[:, :, :], run[:, 0:2 * NT, :], pc[:, 0:2 * NT * NE].rearrange("p (n e) -> p n e", e=NE), ALU.add)
            tt(part[:, :, :], pre[:, :, :], start[:, :].unsqueeze(1).broadcast_to([P, 2 * NT, NE]), ALU.add)
            tt(part[:, :, :], part[:, :, :], ohp, ALU.mult)
            red(posf[:, :], part[:, :, :], ALU.add)
            dve.tensor_copy(place[:, :], posf[:, :]).then_inc(s_pos, 1)
            dve.wait_ge(s_pos, 1)
            k.link(dve.tensor_scalar(ntl[:, :], cnt, 0.0, None, ALU.is_gt))
            for n in range(1, MAXT):
                stt(ntl[:, :], cnt, float(SLOT * n), ntl[:, :], ALU.is_gt, ALU.add)
            k.link(dve.tensor_tensor_scan(tend[:, :], ntl[:, :], zer[:, :], 0.0, ALU.add, ALU.add))
            tt(base[:, :], tend[:, :], ntl[:, :], ALU.subtract)
            k.link(dve.tensor_scalar(base[:, :], base[:, :], float(SLOT), None, ALU.mult))
            tt(pre[:, :, :], pre[:, :, :], base[:, :].unsqueeze(1).broadcast_to([P, 2 * NT, NE]), ALU.add)
            tt(pre[:, :, :], pre[:, :, :], ohp, ALU.mult)
            red(posf[:, :], pre[:, :, :], ALU.add)
            k.link(dve.tensor_copy(pos[:, :], posf[:, :]))
            tt(cmp[:, :, :], ti[:, :].unsqueeze(2).broadcast_to([1, NTILE, NE]),
               tend[0:1, :].unsqueeze(1).broadcast_to([1, NTILE, NE]), ALU.is_ge)
            red(exf[:, :], cmp[:, :, :], ALU.add)
            k.link(dve.tensor_scalar(exf[:, :], exf[:, :], float(NE - 1), None, ALU.min))
            k.link(dve.tensor_copy(keep["expert"][:, :], exf[:, :]))
            stt(ntl[0:1, :], ntl[0:1, :], -float(SLOT), cnt[0:1, :])
            tt(cmp[:, :, :], cmp[:, :, :], ntl[0:1, :].unsqueeze(1).broadcast_to([1, NTILE, NE]), ALU.mult)
            red(exf[:, :], cmp[:, :, :], ALU.add)
            stt(exf[:, :], ti[:, :], float(SLOT), exf[:, :])
            k.link(dve.tensor_scalar(exf[:, :], exf[:, :], float(PAIRS), None, ALU.min))
            dve.tensor_copy(keep["first"][:, :], exf[:, :]).then_inc(s_done, 1)
            dve.wait_ge(s_row, 16)
            dve.tensor_copy(srowf[:, :], srow[:, :]).then_inc(s_rowf, 1)
            dve.wait_ge(s_rt, 1)
            dve.tensor_copy(keep["tok"][:, :], pt[:, 0:NSORT]).then_inc(s_tok, 1)


def experts(nc, A, O, keep):
    ident = keep["ident"]
    with ExitStack() as ctx:
        def sb(name, shape, dt=F32):
            return ctx.enter_context(nc.sbuf_tensor(name, shape, dt))

        sem = ctx.enter_context(semaphores(nc))

        W13 = sb("W13", [P, 2, 2, KD * DE])
        W2 = sb("W2", [P, 2, 2 * D])
        W13h, W13l = sb("W13h", [P, 2, KD, 2 * DE], F32R), sb("W13l", [P, 2, KD, 2 * DE], F32R)
        W2h, W2l = sb("W2h", [P, 2, DE // P, D], F32R), sb("W2l", [P, 1, DE // P, D], F32R)
        xc = sb("xc", [P, KD, PAIRS + P])
        xh, xl = sb("xch", [P, 2, KD, P], F32R), sb("xcl", [P, 2, KD, P], F32R)
        thh = sb("thh", [P, DE])
        ac = sb("ac", [P, 2, DE])
        ah, al = sb("ah", [P, 2, DE], F32R), sb("al", [P, 2, DE], F32R)
        yo = sb("yo", [P, 2, D])
        ph = [ctx.enter_context(nc.psum_tensor(f"eh{i}", [P, 512], F32)) for i in range(2)]
        pa = ctx.enter_context(nc.psum_tensor("ea", [P, 512], F32))
        py = ctx.enter_context(nc.psum_tensor("ey", [P, 1024], F32))
        s_w13 = [sem(f"e_w13{b}") for b in range(2)]
        s_w2 = [sem(f"e_w2{b}") for b in range(2)]
        s_xg = [sem(f"e_xg{b}") for b in range(6)]
        s_turn, s_even, s_odd = sem("e_turn"), sem("e_even"), sem("e_odd")
        s_yst = [sem(f"e_yst{b}") for b in range(2)]
        s_zero, s_xh, s_xl, s_h, s_th, s_s, s_act, s_at, s_ah, s_al, s_y, s_yev = map(sem, (
            "e_zero", "e_xh", "e_xl", "e_h", "e_th", "e_s", "e_act", "e_at", "e_ah", "e_al", "e_y", "e_yev"))
        s_wh, s_wl, s_w2h, s_w2l = map(sem, ("e_wh", "e_wl", "e_w2h", "e_w2l"))
        s_settled = sem("e_settled")
        block = ctx.enter_context(nc.Block())
        xg = [yo[:, n, :] for n in range(2)]
        xg += [W13[:, 1].rearrange("p a c -> p (a c)")[:, D * n:D * n + D] for n in range(2 * KD * DE // D)]
        NXG = len(xg)
        px = (ph[0][:, :], ph[1][:, :], py[:, 0:512], py[:, 512:1024])
        ROUNDS = 2 * NSORT

        def xc_part(n):
            t, h = n // 2, n % 2
            w = min(P, PAIRS + P - P * t)
            return xc[:, 4 * h:4 * h + 4, P * t:P * t + w], w

        def turned(n):
            return px[n % 4].rearrange("p (q s) -> p q s", q=4)

        def xc_done(eng):
            eng.wait_ge(s_zero, 1)
            eng.wait_ge(s_even, NSORT)
            eng.wait_ge(s_odd, NSORT)

        CH, CH2 = 4, 2
        KC = KD // CH
        started = [(s, 2) for s in (s_xh, s_xl, s_h, s_th, s_act, s_at, s_ah, s_al, s_y, s_yev)]
        started += [(s_wh, 2 * CH), (s_wl, 2 * CH), (s_w2h, 2 * CH2), (s_w2l, 2 * CH2)]

        def finished(i, each=1):
            return each * (i + 3)

        def loads(i, b):
            return 16 * ((i - b) // 2 + 1) if isinstance(i, int) else 8 * (i - b) + 16

        def tiles(eng, step):
            for i in range(3):
                step(i, i % 2)
            with eng.Fori(0, NTILE // 2 - 2) as ii:
                step(2 * ii + 3, 1)
                step(2 * ii + 4, 0)
            step(NTILE - 1, 1)

        def w13_part(b, c):
            return W13[:, b].rearrange("p a (k f) -> p a k f", k=KD)[:, :, KC * c:KC * c + KC, :]

        def is_last(i):
            return isinstance(i, int) and i == NTILE - 1

        def is_first(i):
            return isinstance(i, int) and i == 0

        @block.sync
        def _(sp):
            def expert(i):
                return sp.value_load(keep["expert"][0:1, bass.ds(i, 1)], min_val=0, max_val=NE - 1)

            def up(i, b):
                e = expert(i)
                if not isinstance(i, int):
                    sp.wait_ge(s_wl, finished(i - 2, CH))
                for a, w in ((0, A["exp_w1"]), (1, A["exp_w3"])):
                    sp.dma_start(W13[:, b, a], w[0][e].rearrange("(p k) f -> p (k f)", p=P)).then_inc(s_w13[b], 16)

            def down(i, b):
                e = expert(i)
                sp.wait_ge(s_w2l, finished(i - 2, CH2))
                sp.dma_start(W2[:, b], A["exp_w2"][0][e].rearrange("(p k) d -> p (k d)", p=P)).then_inc(s_w2[b], 16)

            up(0, 0)
            sp.wait_ge(s_turn, ROUNDS)
            up(1, 1)
            with sp.Fori(0, NTILE // 2 - 1) as ii:
                for b in range(2):
                    down(2 * ii + b, b)
                    up(2 * ii + 2 + b, b)
            down(NTILE - 2, 0)
            down(NTILE - 1, 1)

        @block.gpsimd
        def _(pool):
            for s, n in started:
                pool.sem_inc(s, n)
            pool.memset(xc[:, :, P * NSORT:], 0.0).then_inc(s_zero, 1)
            for t in range(NSORT):
                if t >= NXG:
                    pool.wait_ge(s_turn, 2 * (t - NXG) + 2)
                pool.indirect_dma_start(out=xg[t % NXG], out_offset=None, in_=keep["xs"],
                                        in_offset=bass.IndirectOffsetOnAxis(ap=keep["tok"][:, t:t + 1], axis=0))\
                    .then_inc(s_xg[t % NXG], 16)

        @block.tensor
        def _(pe):
            for n in range(ROUNDS):
                t, h = n // 2, n % 2
                if h == 0:
                    pe.wait_ge(s_xg[t % NXG], 16 * (t // NXG + 1))
                if n >= 4:
                    pe.wait_ge((s_even, s_odd)[n % 2], n // 2 - 1)
                for q in range(4):
                    last = pe.transpose(turned(n)[:, q, :],
                                        xg[t % NXG].rearrange("s (p k) -> s k p", k=KD)[:, 4 * h + q, :], ident[:, :])
                last.then_inc(s_turn, 1)

            def up(i, b):
                pe.wait_ge(s_xl, finished(i))
                pe.wait_ge(s_act, finished(i - 2))
                for c in range(CH):
                    pe.wait_ge(s_wl, finished(i - 1, CH) + c + 1)
                    for j in range(KC * c, KC * c + KC):
                        for n, (x, w) in enumerate(((xh, W13h), (xl, W13h), (xh, W13l))):
                            last = pe.matmul(ph[b][:, :], x[:, b, j, :], w[:, b, j, :],
                                             start=(j == 0 and n == 0), stop=(j == KD - 1 and n == 2))
                last.then_inc(s_h, 1)

            def turn_act(i, b):
                pe.wait_ge(s_act, finished(i))
                pe.wait_ge(s_al, finished(i - 1))
                for q in range(2):
                    last = pe.transpose(pa[:, P * q:P * q + P], ac[:, b, :].rearrange("s (p k) -> s k p", k=2)[:, q, :], ident[:, :])
                last.then_inc(s_at, 1)

            def down(i, b):
                pe.wait_ge(s_al, finished(i))
                pe.wait_ge(s_yev, finished(i - 1))
                pe.wait_ge(s_w2l, finished(i, CH2))
                for h in range(2):
                    for q in range(2):
                        for n, (x, w) in enumerate(((ah, W2h), (al, W2h), (ah, W2l))):
                            last = pe.matmul(py[:, 512 * h:512 * h + 512], x[:, b, P * q:P * q + P],
                                             w[:, 0 if w is W2l else b, q, 512 * h:512 * h + 512],
                                             start=(q == 0 and n == 0), stop=(q == 1 and n == 2))
                last.then_inc(s_y, 1)

            def step(i, b):
                up(i, b)
                if not is_first(i):
                    down(i - 1, 1 - b)
                turn_act(i, b)

            pe.wait_ge(s_even, NSORT)
            pe.wait_ge(s_odd, NSORT)
            tiles(pe, step)
            down(NTILE - 1, 1)

        @block.scalar
        def _(act):
            def split_up(i, b):
                act.wait_ge(s_w13[b], 2 * loads(i, b))
                act.wait_ge(s_h, finished(i - 2))
                for c in range(CH):
                    act.activation(W13h[:, b, KC * c:KC * c + KC, :].rearrange("p k (a f) -> p a k f", a=2),
                                   w13_part(b, c), ACT.Copy).then_inc(s_wh, 1)

            def split_down(i, b):
                act.wait_ge(s_w2[b], loads(i, b))
                act.wait_ge(s_y, finished(i - 2))
                for c in range(CH2):
                    act.activation(W2h[:, b, c, :], W2[:, b, D * c:D * c + D], ACT.Copy).then_inc(s_w2h, 1)

            def rows(i, b):
                c = act.value_load(keep["first"][0:1, bass.ds(i, 1)], min_val=0, max_val=PAIRS)
                act.wait_ge(s_h, finished(i - 2))
                act.activation(xh[:, b], xc[:, :, bass.ds(c, P)], ACT.Copy).then_inc(s_xh, 1)

            def store(i, b):
                act.wait_ge(s_y, finished(i))
                if not isinstance(i, int) or i >= 2:
                    act.wait_ge(s_yst[b], loads(i, b) - 16)
                act.activation(yo[:, b, :], py[:, :], ACT.Copy).then_inc(s_yev, 1)
                act.wait_ge(s_yev, finished(i))
                act.dma_start(keep["ysc"].rearrange("(i p) d -> i p d", p=P)[i], yo[:, b, :]).then_inc(s_yst[b], 16)

            def step(i, b):
                if not is_last(i):
                    split_up(i + 1, 1 - b)
                act.wait_ge(s_h, finished(i))
                act.wait_ge(s_act, finished(i - 1))
                act.activation(thh[:, :], ph[b][:, 0:DE], ACT.Tanh, scale=0.5).then_inc(s_th, 1)
                if not is_last(i):
                    rows(i + 1, 1 - b)
                split_down(i, b)
                if not is_first(i):
                    store(i - 1, 1 - b)
                act.wait_ge(s_at, finished(i))
                act.wait_ge(s_y, finished(i - 2))
                act.activation(ah[:, b, :], pa[:, 0:DE], ACT.Copy).then_inc(s_ah, 1)

            for n in range(0, ROUNDS, 2):
                act.wait_ge(s_turn, n + 1)
                act.activation(xc_part(n)[0], turned(n), ACT.Copy).then_inc(s_even, 1)
                if n == 6:
                    split_up(0, 0)
            xc_done(act)
            rows(0, 0)
            tiles(act, step)
            store(NTILE - 1, 1)
            for b in range(2):
                act.wait_ge(s_yst[b], 16 * (NTILE // 2))

        @block.vector
        def _(dve):
            def low(out, whole, high):
                return dve.tensor_tensor(out, whole, high.bitcast(F32), ALU.subtract)

            def split_up(i, b):
                dve.wait_ge(s_h, finished(i - 2))
                for c in range(CH):
                    dve.wait_ge(s_wh, finished(i - 1, CH) + c + 1)
                    l, h = (w[:, b, KC * c:KC * c + KC, :].rearrange("p k (a f) -> p a k f", a=2) for w in (W13l, W13h))
                    low(l, w13_part(b, c), h).then_inc(s_wl, 1)

            def split_down(i, b):
                dve.wait_ge(s_y, finished(i - 1))
                for c in range(CH2):
                    dve.wait_ge(s_w2h, finished(i - 1, CH2) + c + 1)
                    low(W2l[:, 0, c, :], W2[:, b, D * c:D * c + D], W2h[:, b, c, :]).then_inc(s_w2l, 1)

            def rows(i, b):
                c = dve.value_load(keep["first"][0:1, bass.ds(i, 1)], min_val=0, max_val=PAIRS)
                dve.wait_ge(s_xh, finished(i))
                dve.wait_ge(s_h, finished(i - 2))
                low(xl[:, b], xc[:, :, bass.ds(c, P)], xh[:, b]).then_inc(s_xl, 1)

            def step(i, b):
                if not is_last(i):
                    split_up(i + 1, 1 - b)
                dve.wait_ge(s_th, finished(i))
                dve.wait_ge(s_at, finished(i - 2))
                dve.scalar_tensor_tensor(out=ac[:, b, :], in0=thh[:, :], scalar=1.0, in1=ph[b][:, 0:DE],
                                         op0=ALU.add, op1=ALU.mult).then_inc(s_s, 1)
                dve.wait_ge(s_s, i + 1)
                dve.tensor_tensor(ac[:, b, :], ac[:, b, :], ph[b][:, DE:2 * DE], ALU.mult).then_inc(s_act, 1)
                if not is_last(i):
                    rows(i + 1, 1 - b)
                split_down(i, b)
                dve.wait_ge(s_ah, finished(i))
                dve.wait_ge(s_y, finished(i - 2))
                low(al[:, b, :], pa[:, 0:DE], ah[:, b, :]).then_inc(s_al, 1)

            for n in range(1, ROUNDS, 2):
                dve.wait_ge(s_turn, n + 1)
                dve.tensor_copy(xc_part(n)[0], turned(n)).then_inc(s_odd, 1)
                if n == 7:
                    split_up(0, 0)
            xc_done(dve)
            rows(0, 0)
            tiles(dve, step)


def finish(nc, A, O, keep):
    pos, wgt = keep["pos"], keep["wgt"]
    with ExitStack() as ctx:
        def sb(name, shape, dt=F32):
            return ctx.enter_context(nc.sbuf_tensor(name, shape, dt))

        sem = ctx.enter_context(semaphores(nc))

        x1 = sb("x2", [P, NT, D])
        ye = sb("ye", [P, 2 * NT, D])
        nf = sb("nf", [P, D])
        junk = sb("junk", [P, D])
        ssf = sb("ssf", [P, NT])
        rsf = sb("rsf", [P, NT])
        s_nf, s_x2, s_sum, s_var, s_sd, s_out, s_st = map(sem, ("f_nf", "f_x2", "f_sum", "f_var", "f_sd", "f_out", "f_st"))
        s_ye = [sem(f"f_ye{n}") for n in range(2 * NT)]
        s_x1, c_dve = [sem(f"f_x1{n}") for n in range(2)], sem("f_dve")
        block = ctx.enter_context(nc.Block())

        @block.sync
        def _(sp):
            sp.dma_start(x1[0:SAMP, 0, :], keep["x1_rows"][0:SAMP, :]).then_inc(s_x1[0], 16)
            sp.dma_start(x1[:, 1:, :], keep["x1_rows"][SAMP:, :].rearrange("(t p) d -> p t d", p=P)).then_inc(s_x1[1], 16)
            sp.dma_start(nf[:, :], A["norm_final_w"].partition_broadcast(P)).then_inc(s_nf, 16)
            for t, (c, S) in enumerate(OT):
                sp.wait_ge(s_out, t + 1)
                dst = (O["y_sample"].rearrange("b t d -> (b t) d") if t == 0
                       else O["y_prompt"][0][P * (t - 1):P * t, :])
                sp.dma_start(dst, x1[0:S, t, :]).then_inc(s_st, 16)
            sp.wait_ge(s_st, 16 * NT)

        @block.gpsimd
        def _(pool):
            for t, (c, S) in enumerate(OT):
                for q in range(2):
                    n = NT * q + t
                    pool.indirect_dma_start(out=ye[0:S, n, :], out_offset=None, in_=keep["ysc"],
                                            in_offset=bass.IndirectOffsetOnAxis(ap=pos[0:S, n:n + 1], axis=0))\
                        .then_inc(s_ye[n], 16)

        @block.scalar
        def _(act):
            for t, (c, S) in enumerate(OT):
                act.wait_ge(s_x2, t + 1)
                if t:
                    act.wait_ge(s_sum, t)
                act.activation(junk[0:S, :], x1[0:S, t, :], ACT.Square, accum_out=ssf[0:S, t:t + 1]).then_inc(s_sum, 1)
                act.wait_ge(s_var, t + 1)
                act.activation(ssf[0:S, t:t + 1], ssf[0:S, t:t + 1], ACT.Sqrt).then_inc(s_sd, 1)

        @block.vector
        def _(dve):
            k = Steps(dve, c_dve)

            def combine(t):
                S = OT[t][1]
                if t < 2:
                    dve.wait_ge(s_x1[t], 16)
                for q in range(2):
                    dve.wait_ge(s_ye[NT * q + t], 16)
                    ins = dve.scalar_tensor_tensor(out=x1[0:S, t, :], in0=ye[0:S, NT * q + t, :],
                                                   scalar=wgt[0:S, q, t:t + 1], in1=x1[0:S, t, :],
                                                   op0=ALU.mult, op1=ALU.add)
                    if q:
                        ins.then_inc(s_x2, 1)
                    else:
                        k.link(ins)

            def variance(t):
                S = OT[t][1]
                dve.wait_ge(s_sum, t + 1)
                dve.tensor_scalar(ssf[0:S, t:t + 1], ssf[0:S, t:t + 1], 1.0 / D, EPS, ALU.mult, ALU.add).then_inc(s_var, 1)

            def normalise(t):
                S = OT[t][1]
                dve.wait_ge(s_sd, t + 1)
                k.link(dve.reciprocal(rsf[0:S, t:t + 1], ssf[0:S, t:t + 1]))
                dve.scalar_tensor_tensor(out=x1[0:S, t, :], in0=x1[0:S, t, :], scalar=rsf[0:S, t:t + 1],
                                         in1=nf[0:S, :], op0=ALU.mult, op1=ALU.mult).then_inc(s_out, 1)

            combine(0)
            dve.wait_ge(s_nf, 16)
            for t in range(1, NT):
                combine(t)
                variance(t - 1)
                if t >= 2:
                    normalise(t - 2)
            normalise(NT - 2)
            variance(NT - 1)
            normalise(NT - 1)


_OUTS = [("y_prompt", (1, SEQ, D)), ("y_sample", (NSAMP, TSAMP, D)), ("new_conf_prompt", (1, 1, CK - 1, D)),
         ("new_sconv_prompt", (1, 1, SK - 1, 4 * D)), ("new_ssm_prompt", (1, 1, NH, HD, N)),
         ("new_conf_sample", (1, NSAMP, CK - 1, D)), ("new_sconv_sample", (1, NSAMP, SK - 1, 4 * D)),
         ("new_ssm_sample", (1, NSAMP, NH, HD, N))]


def program(nc, A, O):
    with ExitStack() as ctx:
        def sb(name, shape, dt=F32):
            return ctx.enter_context(nc.sbuf_tensor(name, shape, dt))

        keep = {"gates": nc.dram_tensor("gates", (2, KD, P, T), F32, kind="Internal").ap(),
                "aconv": nc.dram_tensor("conv_rows", (KD, P, T), F32, kind="Internal").ap(),
                "yrows": nc.dram_tensor("ssd_rows", (G, 2, P, T), F32, kind="Internal").ap(),
                "xs": nc.dram_tensor("xs_rows", (SAMP + SEQ, D), F32, kind="Internal").ap(),
                "x1_rows": nc.dram_tensor("x1_rows", (SAMP + SEQ, D), F32, kind="Internal").ap(),
                "sorted": nc.dram_tensor("sorted", (NSORT * P, 1), U32, kind="Internal").ap(),
                "ysc": nc.dram_tensor("slot_rows", (NTILE * SLOT, D), F32, kind="Internal").ap()}
        keep["ident"], keep["ones"], keep["rstd"] = sb("ident", [P, P]), sb("ones", [P, P]), sb("rstd", [P, 8])
        keep["pos"], keep["wgt"] = sb("pos", [P, 2 * NT], U32), sb("wgt", [P, 2, NT])
        keep["expert"], keep["first"] = sb("expert", [1, NTILE], U32), sb("first", [1, NTILE], U32)
        keep["tok"] = sb("tok", [P, NSORT], U32)
        with ExitStack() as outer:
            keep["x1"] = outer.enter_context(nc.sbuf_tensor("x1", [P, NT, D], F32))
            with nc.sbuf_tensor("cs", [P, KD, NR], F32) as keep["cs"], \
                    nc.sbuf_tensor("wraw", [P, 2, 2 * D], F32) as keep["wraw"]:
                trunk(nc, A, O, keep)
                mixer(nc, A, O, keep)
            route(nc, A, O, keep)
        experts(nc, A, O, keep)
        finish(nc, A, O, keep)


def kernel(**inputs):
    import numpy as _np
    import concourse.bacc as _bacc
    from concourse import mybir as _mybir
    from concourse.bass_utils import run_bass_kernel_spmd as _run

    nc = _bacc.Bacc("TRN2", target_bir_lowering=False, num_devices=1)
    arrays, A, O = {}, {}, {}
    for name, value in inputs.items():
        a = _np.ascontiguousarray(value)
        arrays[f"in_{name}"] = a
        A[name] = nc.dram_tensor(f"in_{name}", a.shape, _mybir.dt.float32, kind="ExternalInput").ap()
    for name, shape in _OUTS:
        O[name] = nc.dram_tensor(f"out_{name}", shape, _mybir.dt.float32, kind="ExternalOutput").ap()
    program(nc, A, O)
    r = _run(nc, [arrays], core_ids=[0])
    return tuple(r.results[0][f"out_{name}"] for name, _ in _OUTS)
```
